# Optimizing a Trainium2 kernel written in Bass

```python
import math
import jax, jax.numpy as jnp
from jax import lax
import numpy as np

D_MODEL = 1024
BATCH = 1
SEQ = 512
DEPTH = 1
DEC_BATCH = 8
DEC_SEQ = 4
PAST_LEN = 2048
PAGE_SIZE = 128

HEAD_DIM = 64
ATTN_WIDTH = D_MODEL // 2
ATTN_HEADS = ATTN_WIDTH // HEAD_DIM
SSM_WIDTH = D_MODEL - ATTN_WIDTH
SSM_GROUP_CH = 16
SSM_GROUPS = SSM_WIDTH // SSM_GROUP_CH
SSM_STATE = 64
WINDOWS = (128, 512, 2048)
DILATIONS = (1, 4, 16)
MAX_WINDOW = 2048
N_BUCKETS = 32
MAX_EXACT = 16
BUCKET_MAX_DIST = 2048
N_EXPERT_GROUPS = 4
EXPERTS_PER_GROUP = 4
EXPERT_TOP_K = 2
D_EXPERT = 512
NORM_EPS = 1e-6
DT_MIN = 1e-3
DT_MAX = 1e-1
F32 = jnp.float32

kernel_name = "hymba_dilated_s5_hmoe_step"

def rmsnorm(x, g):
    xf = x.astype(F32)
    y = xf * lax.rsqrt(jnp.mean(xf * xf, axis=-1, keepdims=True) + NORM_EPS)
    return (y * g.astype(F32)).astype(x.dtype)

def t5_bucket(dist):
    d = jnp.maximum(dist, MAX_EXACT).astype(F32)
    log_part = MAX_EXACT + (jnp.log(d / MAX_EXACT) / math.log(BUCKET_MAX_DIST / MAX_EXACT)
                            * (N_BUCKETS - MAX_EXACT)).astype(jnp.int32)
    return jnp.where(dist < MAX_EXACT, dist, jnp.minimum(log_part, N_BUCKETS - 1))

def merge_branches(ms, dens, nums):
    m_all = jnp.max(jnp.stack(ms), axis=0)
    num = jnp.zeros_like(nums[0])
    den = jnp.zeros_like(dens[0])
    for m, d, nm in zip(ms, dens, nums):
        w = jnp.exp(m - m_all)
        num = num + w[..., None] * nm
        den = den + w * d
    return num / den[..., None]

def dilated_attn_prompt(q, k, v, rel_bias):
    n_seq, s_len, n_h, d_h = q.shape
    qf = q.astype(F32) * HEAD_DIM ** -0.5
    kf, vf = k.astype(F32), v.astype(F32)
    bias_tab = rel_bias.astype(F32)
    ms, dens, nums = [], [], []
    for w, r in zip(WINDOWS, DILATIONS):
        steps = w // r
        L = s_len // r
        nb = -(-L // steps)
        Lp = nb * steps

        def to_res(a):
            a = a.reshape(n_seq, L, r, n_h, d_h)
            a = jnp.pad(a, ((0, 0), (0, Lp - L), (0, 0), (0, 0), (0, 0)))
            return a.reshape(n_seq, nb, steps, r, n_h, d_h)

        def band(a):
            prev = jnp.pad(a, ((0, 0), (1, 0), (0, 0), (0, 0), (0, 0), (0, 0)))[:, :-1]
            return jnp.concatenate([prev, a], axis=2)

        qr = to_res(qf)
        kb, vb = band(to_res(kf)), band(to_res(vf))
        ql = jnp.arange(steps)
        kl = jnp.arange(2 * steps)
        j = ql[:, None] + steps - kl[None, :]
        blk = jnp.arange(nb)
        key_ok = (blk[:, None] * steps + kl[None, :] - steps) >= 0
        mask = ((j >= 0) & (j <= steps))[None] & key_ok[:, None, :]
        bias = bias_tab[t5_bucket(jnp.clip(j, 0, steps) * r)]
        bias = jnp.transpose(bias, (2, 0, 1))
        s = jnp.einsum('bnqrhd,bnkrhd->bnrhqk', qr, kb) + bias[None, None, None]
        s = jnp.where(mask[None, :, None, None], s, -jnp.inf)
        m = jnp.max(s, axis=-1)
        p = jnp.exp(s - m[..., None])
        den = jnp.sum(p, axis=-1)
        num = jnp.einsum('bnrhqk,bnkrhd->bnqrhd', p, vb)

        def back(a):
            a = a.reshape((n_seq, Lp, r) + a.shape[4:])[:, :L]
            return a.reshape((n_seq, s_len) + a.shape[3:])

        ms.append(back(jnp.transpose(m, (0, 1, 4, 2, 3))))
        dens.append(back(jnp.transpose(den, (0, 1, 4, 2, 3))))
        nums.append(back(num))
    return merge_branches(ms, dens, nums)

def dilated_attn_decode(q, k_all, v_all, rel_bias):
    n_seq, t_len = q.shape[:2]
    w_rows = k_all.shape[1] - t_len
    qf = q.astype(F32) * HEAD_DIM ** -0.5
    kf, vf = k_all.astype(F32), v_all.astype(F32)
    bias_tab = rel_bias.astype(F32)
    ms, dens, nums = [], [], []
    for w, r in zip(WINDOWS, DILATIONS):
        steps = w // r
        j = jnp.arange(steps + 1)
        idx = w_rows + jnp.arange(t_len)[:, None] - r * j[None, :]
        valid = idx >= 0
        idx = jnp.maximum(idx, 0)
        kg, vg = kf[:, idx], vf[:, idx]
        bias = bias_tab[t5_bucket(r * j)].T
        s = jnp.einsum('nthd,ntjhd->nhtj', qf, kg) + bias[None, :, None, :]
        s = jnp.where(valid[None, None], s, -jnp.inf)
        m = jnp.max(s, axis=-1)
        p = jnp.exp(s - m[..., None])
        dens.append(jnp.transpose(jnp.sum(p, axis=-1), (0, 2, 1)))
        ms.append(jnp.transpose(m, (0, 2, 1)))
        nums.append(jnp.einsum('nhtj,ntjhd->nthd', p, vg))
    return merge_branches(ms, dens, nums)

def _complex_affine_combine(e1, e2):
    a1r, a1i, b1r, b1i = e1
    a2r, a2i, b2r, b2i = e2
    return (a2r * a1r - a2i * a1i, a2r * a1i + a2i * a1r,
            a2r * b1r - a2i * b1i + b2r, a2r * b1i + a2i * b1r + b2i)

def s5_branch(u, h0, a_re, a_im, log_dt, b_re, b_im, c_re, c_im, d_skip, glu_a, glu_b):
    n_seq, t_len, _ = u.shape
    uf = u.astype(F32).reshape(n_seq, t_len, SSM_GROUPS, SSM_GROUP_CH)
    lam_re = jnp.minimum(a_re.astype(F32), -1e-4)
    lam_im = a_im.astype(F32)
    dt = jnp.exp(log_dt.astype(F32))[:, None]
    mag = jnp.exp(lam_re * dt)
    ph = lam_im * dt
    abar_re, abar_im = mag * jnp.cos(ph), mag * jnp.sin(ph)
    nr, ni = abar_re - 1.0, abar_im
    den = lam_re * lam_re + lam_im * lam_im
    coef_re = (nr * lam_re + ni * lam_im) / den
    coef_im = (ni * lam_re - nr * lam_im) / den
    br, bi = b_re.astype(F32), b_im.astype(F32)
    bbar_re = coef_re[..., None] * br - coef_im[..., None] * bi
    bbar_im = coef_re[..., None] * bi + coef_im[..., None] * br
    bu_re = jnp.einsum('ntgc,gpc->ntgp', uf, bbar_re)
    bu_im = jnp.einsum('ntgc,gpc->ntgp', uf, bbar_im)
    if h0 is not None:
        h0_re, h0_im = h0[0].astype(F32), h0[1].astype(F32)
        bu_re = bu_re.at[:, 0].add(abar_re * h0_re - abar_im * h0_im)
        bu_im = bu_im.at[:, 0].add(abar_re * h0_im + abar_im * h0_re)
    a_r = jnp.broadcast_to(abar_re, bu_re.shape)
    a_i = jnp.broadcast_to(abar_im, bu_im.shape)
    _, _, h_re, h_im = lax.associative_scan(_complex_affine_combine, (a_r, a_i, bu_re, bu_im), axis=1)
    y = (jnp.einsum('ntgp,gcp->ntgc', h_re, c_re.astype(F32))
         - jnp.einsum('ntgp,gcp->ntgc', h_im, c_im.astype(F32))
         + d_skip.astype(F32) * uf)
    y = jax.nn.gelu(y)
    y = (jnp.einsum('ntgc,gce->ntge', y, glu_a.astype(F32))
         * jax.nn.sigmoid(jnp.einsum('ntgc,gce->ntge', y, glu_b.astype(F32))))
    return y.reshape(n_seq, t_len, SSM_WIDTH).astype(u.dtype), h_re[:, -1], h_im[:, -1]

def hier_moe(h, rg_w, rg_b, re_w, re_b, w_gate, w_up, w_down):
    n_seq, t_len, d = h.shape
    t = h.reshape(n_seq * t_len, d)
    g_prob = jax.nn.softmax((t @ rg_w + rg_b).astype(F32), axis=-1)
    g_star = jnp.argmax(g_prob, axis=-1)
    p_star = jnp.max(g_prob, axis=-1)
    g_hot = jax.nn.one_hot(g_star, N_EXPERT_GROUPS, dtype=F32)
    e_logits = (jnp.einsum('td,gde->tge', t, re_w) + re_b).astype(F32)
    e_sel = jnp.sum(e_logits * g_hot[:, :, None], axis=1)
    top_v, top_i = lax.top_k(e_sel, EXPERT_TOP_K)
    top_w = jax.nn.softmax(top_v, axis=-1) * p_star[:, None]
    e_w = jnp.sum(jax.nn.one_hot(top_i, EXPERTS_PER_GROUP, dtype=F32) * top_w[..., None], axis=1)
    gw = (g_hot[:, :, None] * e_w[:, None, :]).astype(h.dtype)
    out = jnp.zeros_like(t)
    for g in range(N_EXPERT_GROUPS):
        a = (jax.nn.silu(jnp.einsum('td,edf->tef', t, w_gate[g]))
             * jnp.einsum('td,edf->tef', t, w_up[g]))
        out = out + jnp.einsum('tef,efd->td', a * gw[:, g, :, None], w_down[g])
    return out.reshape(n_seq, t_len, d)

def hybrid_layer(x, c, past, rel_bias, ada_w, ada_b, norm1_g, w_in, ssm_a_re, ssm_a_im, ssm_log_dt,
                 ssm_b_re, ssm_b_im, ssm_c_re, ssm_c_im, ssm_d, glu_a, glu_b, attn_out_g, ssm_out_g,
                 w_out, norm2_g, router_g_w, router_g_b, router_e_w, router_e_b, w_gate, w_up, w_down):
    n_seq, t_len, _ = x.shape
    mod = jnp.einsum('nd,de->ne', jax.nn.silu(c), ada_w) + ada_b
    sh1, sc1, g1, sh2, sc2, g2 = [m[:, None, :] for m in jnp.split(mod, 6, axis=-1)]
    h = rmsnorm(x, norm1_g) * (1 + sc1) + sh1
    z = jnp.einsum('ntd,de->nte', h, w_in)
    aw = ATTN_WIDTH
    q = z[..., :aw].reshape(n_seq, t_len, ATTN_HEADS, HEAD_DIM)
    k = z[..., aw:2 * aw].reshape(n_seq, t_len, ATTN_HEADS, HEAD_DIM)
    v = z[..., 2 * aw:3 * aw].reshape(n_seq, t_len, ATTN_HEADS, HEAD_DIM)
    u = z[..., 3 * aw:]
    if past is None:
        att = dilated_attn_prompt(q, k, v, rel_bias)
        keep = min(MAX_WINDOW, t_len)
        k_new, v_new = k[:, t_len - keep:], v[:, t_len - keep:]
        h0 = None
    else:
        past_k, past_v, h0_re, h0_im = past
        k_all = jnp.concatenate([past_k.astype(k.dtype), k], axis=1)
        v_all = jnp.concatenate([past_v.astype(v.dtype), v], axis=1)
        att = dilated_attn_decode(q, k_all, v_all, rel_bias)
        k_new, v_new = k, v
        h0 = (h0_re, h0_im)
    ssm_y, hT_re, hT_im = s5_branch(u, h0, ssm_a_re, ssm_a_im, ssm_log_dt, ssm_b_re, ssm_b_im,
                                    ssm_c_re, ssm_c_im, ssm_d, glu_a, glu_b)
    att = att.reshape(n_seq, t_len, ATTN_WIDTH).astype(x.dtype)
    mixed = jnp.concatenate([rmsnorm(att, attn_out_g), rmsnorm(ssm_y, ssm_out_g)], axis=-1)
    x = x + g1 * jnp.einsum('nte,ed->ntd', mixed, w_out)
    h2 = rmsnorm(x, norm2_g) * (1 + sc2) + sh2
    x = x + g2 * hier_moe(h2, router_g_w, router_g_b, router_e_w, router_e_b, w_gate, w_up, w_down)
    return x, (k_new, v_new, hT_re, hT_im)

def setup_inputs(seed: int = 0) -> dict:
    key = jax.random.key(seed)
    ks = jax.random.split(key, 40)
    nrm = lambda i, shape, s: jax.random.normal(ks[i], shape, F32) * s
    D, G, P, Cg = D_MODEL, SSM_GROUPS, SSM_STATE, SSM_GROUP_CH
    NG, EPG, FE = N_EXPERT_GROUPS, EXPERTS_PER_GROUP, D_EXPERT
    win = min(MAX_WINDOW, PAST_LEN)
    proj_w = 3 * ATTN_WIDTH + SSM_WIDTH
    a_im0 = jnp.pi * jnp.arange(P, dtype=F32)
    return {
        "x_prompt": nrm(0, (BATCH, SEQ, D), 1.0),
        "x_sample": nrm(1, (DEC_BATCH, DEC_SEQ, D), 1.0),
        "c_prompt": nrm(2, (BATCH, D), 1.0),
        "c_sample": nrm(3, (DEC_BATCH, D), 1.0),
        "cache_k": nrm(4, (DEPTH, DEC_BATCH, win, ATTN_HEADS, HEAD_DIM), 1.0),
        "cache_v": nrm(5, (DEPTH, DEC_BATCH, win, ATTN_HEADS, HEAD_DIM), 1.0),
        "state_ssm_re": nrm(6, (DEPTH, DEC_BATCH, G, P), 1.0),
        "state_ssm_im": nrm(7, (DEPTH, DEC_BATCH, G, P), 1.0),
        "rel_bias": nrm(8, (N_BUCKETS, ATTN_HEADS), 0.5),
        "ada_w": nrm(9, (DEPTH, D, 6 * D), 0.5 * D ** -0.5),
        "ada_b": nrm(10, (DEPTH, 6 * D), 0.02),
        "norm1_g": 1.0 + nrm(11, (DEPTH, D), 0.05),
        "w_in": nrm(12, (DEPTH, D, proj_w), D ** -0.5),
        "ssm_a_re": -0.5 + nrm(13, (DEPTH, G, P), 0.01),
        "ssm_a_im": a_im0 + nrm(14, (DEPTH, G, P), 0.01),
        "ssm_log_dt": jax.random.uniform(ks[15], (DEPTH, G), F32, math.log(DT_MIN), math.log(DT_MAX)),
        "ssm_b_re": nrm(16, (DEPTH, G, P, Cg), (2 * Cg) ** -0.5),
        "ssm_b_im": nrm(17, (DEPTH, G, P, Cg), (2 * Cg) ** -0.5),
        "ssm_c_re": nrm(18, (DEPTH, G, Cg, P), (2 * P) ** -0.5),
        "ssm_c_im": nrm(19, (DEPTH, G, Cg, P), (2 * P) ** -0.5),
        "ssm_d": nrm(20, (DEPTH, G, Cg), 1.0),
        "glu_a": nrm(21, (DEPTH, G, Cg, Cg), Cg ** -0.5),
        "glu_b": nrm(22, (DEPTH, G, Cg, Cg), Cg ** -0.5),
        "attn_out_g": 1.0 + nrm(23, (DEPTH, ATTN_WIDTH), 0.05),
        "ssm_out_g": 1.0 + nrm(24, (DEPTH, SSM_WIDTH), 0.05),
        "w_out": nrm(25, (DEPTH, D, D), D ** -0.5),
        "norm2_g": 1.0 + nrm(26, (DEPTH, D), 0.05),
        "router_g_w": nrm(27, (DEPTH, D, NG), D ** -0.5),
        "router_g_b": nrm(28, (DEPTH, NG), 0.01),
        "router_e_w": nrm(29, (DEPTH, NG, D, EPG), D ** -0.5),
        "router_e_b": nrm(30, (DEPTH, NG, EPG), 0.01),
        "w_gate": nrm(31, (DEPTH, NG, EPG, D, FE), D ** -0.5),
        "w_up": nrm(32, (DEPTH, NG, EPG, D, FE), D ** -0.5),
        "w_down": nrm(33, (DEPTH, NG, EPG, FE, D), FE ** -0.5),
        "final_norm_g": 1.0 + nrm(34, (D,), 0.05),
    }

def reference(x_prompt, x_sample, c_prompt, c_sample, cache_k, cache_v, state_ssm_re, state_ssm_im,
              rel_bias, ada_w, ada_b, norm1_g, w_in, ssm_a_re, ssm_a_im, ssm_log_dt, ssm_b_re, ssm_b_im,
              ssm_c_re, ssm_c_im, ssm_d, glu_a, glu_b, attn_out_g, ssm_out_g, w_out, norm2_g,
              router_g_w, router_g_b, router_e_w, router_e_b, w_gate, w_up, w_down, final_norm_g):
    layer_params = (ada_w, ada_b, norm1_g, w_in, ssm_a_re, ssm_a_im, ssm_log_dt, ssm_b_re, ssm_b_im,
                    ssm_c_re, ssm_c_im, ssm_d, glu_a, glu_b, attn_out_g, ssm_out_g, w_out, norm2_g,
                    router_g_w, router_g_b, router_e_w, router_e_b, w_gate, w_up, w_down)
    xp, xs = x_prompt, x_sample
    kp, vp, ks_, vs_, rp, ip, rs, is_ = [], [], [], [], [], [], [], []
    for l in range(DEPTH):
        lw = tuple(w[l] for w in layer_params)
        xp, (k1, v1, r1, i1) = hybrid_layer(xp, c_prompt, None, rel_bias, *lw)
        xs, (k2, v2, r2, i2) = hybrid_layer(
            xs, c_sample, (cache_k[l], cache_v[l], state_ssm_re[l], state_ssm_im[l]), rel_bias, *lw)
        kp.append(k1); vp.append(v1); rp.append(r1); ip.append(i1)
        ks_.append(k2); vs_.append(v2); rs.append(r2); is_.append(i2)
    y_prompt = rmsnorm(xp, final_norm_g)
    y_sample = rmsnorm(xs, final_norm_g)
    return (y_prompt, y_sample, jnp.stack(kp), jnp.stack(vp), jnp.stack(ks_), jnp.stack(vs_),
            jnp.stack(rp), jnp.stack(ip), jnp.stack(rs), jnp.stack(is_))


_drawn_inputs = setup_inputs


def setup_inputs(seed=0):
    import zlib

    import numpy as np

    out = dict(_drawn_inputs(seed))
    spreads = {}
    factors = {'ssm_a_re': 3.914,
     'attn_out_g': 4.625,
     'ssm_out_g': 4.691,
     'norm2_g': 3.364,
     'router_g_b': 8.0,
     'router_e_b': 8.0}
    for name, (base, spread) in spreads.items():
        noise = np.random.default_rng([zlib.crc32(name.encode()), seed]).standard_normal(out[name].shape)
        drawn = base * np.exp(spread * noise) if base else spread * noise
        out[name] = __import__('jax').numpy.asarray(drawn.astype(out[name].dtype))
    for name, factor in factors.items():
        out[name] = (out[name] * factor).astype(out[name].dtype)
    return out
```

```python
from contextlib import ExitStack

import numpy as np

import concourse.bass as bass
from concourse import mybir

F32 = mybir.dt.float32
U32 = mybir.dt.uint32
I32 = mybir.dt.int32
ALU = mybir.AluOpType
ACT = mybir.ActivationFunctionType
AX = mybir.AxisListType

P = 128
D = 1024
KD = D // P
SEQ = 512
NSEQ, TDEC = 8, 4
NS = NSEQ * TDEC
NTOK = SEQ + NS
TW = [P] * (SEQ // P) + [NS]
NT = len(TW)
QT = SEQ // P
HEADS, DH = 8, 64
AW = HEADS * DH
NC = NSEQ + 1
PAST = 2048
WINDOWS, DILATIONS = (128, 512, 2048), (1, 4, 16)
BUCKETS, MAX_EXACT = 32, 16
GRP, GC, ST = 32, 16, 64
STT = GRP * ST // P
CH = 128
NG, EPG = 4, 4
NE = NG * EPG
FE = 512
EPS = 1e-6
EXTRA = 8
NTILE = NE + EXTRA
NEG = -1.0e30

CROWS = [r for r in range(PAST) if r >= PAST - WINDOWS[1] or r % DILATIONS[2] < TDEC]
CK = len(CROWS)
CB = CK // P
DK = CK + NS
SLOT = 4096
R1 = 4
R2 = 6
N_ADA, N_WIN = 12, 4
IT_ADA, IT_WIN = 0, N_ADA
IT_OH = IT_WIN + N_WIN
IT_KV = IT_OH + 1
IT_WO = IT_KV + 2 * NSEQ
N_ITEMS = IT_WO + 2


def _bucket(dist):
    d = np.maximum(dist, MAX_EXACT).astype(np.float32)
    log_part = MAX_EXACT + (np.log(d / np.float32(MAX_EXACT)) / np.float32(np.log(PAST / MAX_EXACT))
                            * np.float32(BUCKETS - MAX_EXACT)).astype(np.int32)
    return np.where(dist < MAX_EXACT, dist, np.minimum(log_part, BUCKETS - 1))


def _distance_rows(dist):
    n = np.zeros(dist.shape, np.int64)
    for w, r in zip(WINDOWS, DILATIONS):
        n += (dist >= 0) & (dist <= w) & (dist % r == 0)
    out = np.zeros((BUCKETS + 1,) + dist.shape, np.float32)
    b = _bucket(np.maximum(dist, 0))
    for i in range(BUCKETS):
        out[i] = (b == i) & (n > 0)
    out[BUCKETS] = np.where(n > 0, np.log(np.maximum(n, 1)), NEG)
    return out


def _constants():
    p = np.arange(P)
    blocks = {}
    blocks["ident"] = np.eye(P)
    blocks["flip"] = np.eye(P)[::-1]
    blocks["tri"] = (p[:, None] < p[None, :])
    blocks["ones"] = np.ones((P, P))
    blocks["iota"] = np.broadcast_to(np.arange(P), (P, P))
    head = (p % 32) // TDEC
    blocks["headsel"] = head[:, None] == (np.arange(AW) // DH)[None, :]
    nm = np.zeros((P, 2, NS))
    ts = np.zeros((P, 2, NS))
    for g in range(2):
        seq = 4 * g + p // 32
        tok = np.arange(NS)
        nm[:, g] = np.where(seq[:, None] == tok[None, :] // TDEC, 0.0, NEG)
        ts[:, g] = (seq * TDEC + p % TDEC)[:, None] == tok[None, :]
    blocks["newmask"] = nm.reshape(P, -1)
    blocks["toksel"] = ts.reshape(P, -1)
    blocks["tokid"] = p[:, None] + P * np.arange(NT)[None, :]
    blocks["valid"] = (p[:, None] < np.array(TW)[None, :])
    row = lambda a: np.broadcast_to(np.asarray(a).reshape(1, -1), (P, np.asarray(a).size))
    blocks["first"] = row([4, 3, 2, 1])
    blocks["ebase"] = row(np.arange(NE) * P)
    blocks["exbase"] = row((NE - 1 - np.arange(NE)) * P)
    blocks["eidx"] = row(np.arange(NE))
    blocks["jidx"] = row(np.arange(EXTRA))
    blocks["tbase"] = row(np.arange(NTILE) * P)
    cols, at = {}, 0
    for k, v in blocks.items():
        blocks[k] = np.asarray(v, np.float32)
        cols[k] = (at, at + blocks[k].shape[1])
        at += blocks[k].shape[1]
    return np.concatenate(list(blocks.values()), axis=1), cols


CONST, CCOL = _constants()
_dist0 = SEQ - 1 - np.arange(640)
OH_PROMPT = _distance_rows(_dist0)
_t = np.arange(TDEC)[:, None]
_cached = PAST + _t - np.array(CROWS)[None, :]
_new = np.broadcast_to(_t - (np.arange(NS) % TDEC)[None, :], (TDEC, NS))
OH_DECODE = _distance_rows(np.concatenate([_cached, _new], axis=1)).reshape(BUCKETS + 1, TDEC * DK)

PC = {}
_at = 0
for _k, _n in (("a_re", 16), ("a_im", 16), ("log_dt", 16), ("dskip", 4), ("attg", 4), ("ssmg", 4),
               ("b_re", 256), ("b_im", 256)):
    PC[_k] = (_at, _at + _n)
    _at += _n
NPAR = _at


class Order:

    def __init__(self, eng, sem, base=0):
        self.eng, self.sem, self.n = eng, sem, base

    def __call__(self, ins):
        ins.then_inc(self.sem, 1)
        self.n += 1
        self.eng.wait_ge(self.sem, self.n)


def build(nc, I, O):
    ctx = ExitStack()
    with ctx:
        _build(nc, I, O, ctx)


def _build(nc, I, O, ctx):
    B0 = 16512

    def at(name, shape, off, dt=F32):
        assert off % 32 == 0 and B0 + off + 4 * int(np.prod(shape[1:])) <= 229368, name
        return nc.alloc_sbuf_tensor_at(name, shape, dt, offset=B0 + off)

    def sem(name):
        return ctx.enter_context(nc.semaphore(name))

    RING, E, C, SM = 0, 65536, 98304, 98304 + 6656
    HT, QK, V, U = 106496, 123904, 141312, 151552
    TAB, W = 160256, 176640

    ring = [at(f"ring{i}", [P, SLOT], RING + 16384 * i) for i in range(R1)]
    bt = [at("bt_re", [P, STT, P], E), at("bt_im", [P, STT, P], E + 8192)]
    ct = [at("ct_re", [P, STT, 32], E + 16384), at("ct_im", [P, STT, 32], E + 18432)]
    xr, xi, gr, gi, hr, hi = [at(n, [P, 4, CH], E + 20480 + 2048 * i)
                              for i, n in enumerate(("s5_xr", "s5_xi", "s5_gr", "s5_gi", "s5_hr", "s5_hi"))]
    ering = [at(f"ering{i}", [P, SLOT], RING + 16384 * i) for i in range(R2)]

    NCC = CONST.shape[1]
    assert NCC * 4 <= 6656, NCC
    const = at("const", [P, NCC], C)

    def cst(name, rows=P):
        a, b = CCOL[name]
        return const[0:rows, a:b]

    sm_at = [SM]

    def small(name, cols, rows=P, dt=F32):
        t = at(name, [rows, cols], sm_at[0], dt)
        sm_at[0] += (4 * cols + 31) // 32 * 32
        assert sm_at[0] <= HT, name
        return t

    mag, cth, sth = small("mag", 16), small("cth", 16), small("sth", 16)
    ctab33 = small("tab33", 8, BUCKETS + 1)
    car, cai = small("carry_re", 16), small("carry_im", 16)
    las, lai = small("last_re", 16), small("last_im", 16)
    gains = small("gains", 12)
    ctmp = small("ctmp", 16)
    stat = small("stat", 64)
    dstat = small("dstat", 64)
    rssm = small("rssm", 8)
    nbias = small("nbias", 2 * NS)

    hT = at("hT", [P, KD, NTOK], HT)
    mixT = at("mixT", [P, KD, NTOK], HT)
    h2T = at("h2T", [P, KD, NTOK], HT)
    modsb = at("modsb", [NC, 2, 512], HT)
    ohp = at("oh_prompt", [BUCKETS + 1, 640], HT + 4096)
    gsb = at("gsb", [HEADS, 640], HT + 8192)
    toep = at("toeplitz", [P, 2, SEQ], HT)
    qkT = at("qkT", [P, 8, NTOK], QK)
    adab = at("adab", [1, 6 * D], QK)
    vrow = at("vrow", [P, NT, AW], V)
    uT = at("uT", [P, 4, NTOK], U)
    ngain = at("ngain", [NC, 2, D], U)
    cosT, sinT = at("cosT", [P, STT, CH], TAB), at("sinT", [P, STT, CH], TAB + 8192)

    xt = at("xt", [P, 2, D], W)
    hb = at("hb", [P, 2, D], W + 8192)
    par = at("par", [P, NPAR], W + 8192)
    bbr, bbi = at("bbr", [P, STT, GC], W + 8192 + 2304), at("bbi", [P, STT, GC], W + 8192 + 3328)
    bt1, bt2 = at("bt1", [P, STT, GC], W + 8192 + 4352), at("bt2", [P, STT, GC], W + 8192 + 5376)
    pr = at("pr", [P, 20, 16], W + 8192 + 6400)
    assert NPAR * 4 <= 2304 and 6400 + 1280 <= 8192
    modP, modS = at("modP", [P, 2, D], W + 16384), at("modS", [NS, 2, D], W + 24576)
    bpad = [at("bpad_re", [P, STT, P], W + 16384), at("bpad_im", [P, STT, P], W + 24576)]
    cT, cE, cS = [at(n, [P, KD, NC], W + 32768 + 288 * i) for i, n in enumerate(("cT", "cE", "cS"))]
    dt1, dt2 = at("dt1", [P, STT, CH // 2], W), at("dt2", [P, STT, CH // 2], W + 4096)

    att = at("att", [P, NT, AW], W)
    dPT = at("dPT", [P, 8, P], W)
    dO = at("dO", [P, 2, AW], W + 4096)
    Sb = at("Sb", [P, 2, SEQ], W + 10240)
    qbd = at("qbd", [P, NSEQ, 4, 32], W + 10240)
    PTs = at("PTs", [P, 2, SEQ], W + 14336)
    glu = at("glu", [P, 2, 4, P], W + 14336)
    dbias = at("dbias", [P, DK], W + 18432)
    dP = at("dP", [P, DK], W + 22144)
    th = at("gelu_th", [P, 4, CH], W + 25856)
    ta, tb = at("s5_ta", [P, 4, CH], W + 27904), at("s5_tb", [P, 4, CH], W + 29952)
    yd, y2 = at("gelu_yd", [P, 4, CH], W + 32000), at("gelu_y2", [P, 4, CH], W + 34048)
    padT = at("padT", [BUCKETS + 1, 4, P], W + 27904)
    x2 = at("x2", [P, NT, D], QK)
    mod3P = at("mod3P", [P, 3, D], QK + 20480)
    mod3S = at("mod3S", [NS, 3, D], TAB)
    xt3 = at("xt3", [P, 2, D], W)
    h2 = at("h2", [P, 2, D], W + 8192)
    pt1, pt2 = at("pt1", [P, 2, D], W + 16384), at("pt2", [P, D], W + 24576)
    rw = at("rw", [P, KD, 20], W + 28672)
    rb = at("rb", [1, 20], W + 29312)
    rt_at = [TAB + 12288]

    def rt(name, shape, dt=F32):
        n = int(np.prod(shape[1:])) * 4
        if rt_at[0] <= W < rt_at[0] + n:
            rt_at[0] = W + 29440
        t = at(name, shape, rt_at[0], dt)
        rt_at[0] += (n + 31) // 32 * 32
        return t

    lg = rt("logits", [P, NT, 20])
    g4a, g4b, g4c = [rt(n, [P, NT, 4]) for n in ("g4a", "g4b", "g4c")]
    ghot = rt("ghot", [P, NT, 4])
    gmax, gsum = rt("gmax", [P, NT]), rt("gsum", [P, NT])
    e16 = rt("e16", [P, NT, NE])
    esel, o1, o2 = [rt(n, [P, NT, 4]) for n in ("esel", "o1", "o2")]
    v1, v2, w1, w2 = [rt(n, [P, NT]) for n in ("v1", "v2", "w1", "w2")]
    E1, E2, M = [rt(n, [P, NT, NE]) for n in ("E1", "E2", "M")]
    pos = rt("pos", [P, NT, NE])
    cnt, nx, xb, nx2 = [rt(n, [P, NE]) for n in ("cnt", "nx", "xb", "nx2")]
    slot = rt("slotrow", [P, NT, NE])
    sl = [rt("slot0", [P, NT]), rt("slot1", [P, NT])]
    ms = [rt("inslot0", [P, NT]), rt("inslot1", [P, NT])]
    td = rt("tile_dist", [P, NT, NTILE])
    tt = [rt("tile_tok0", [P, NT, NTILE]), rt("tile_tok1", [P, NT, NTILE])]
    tm = rt("tile_tmp", [P, NT, NTILE])
    slot1h = at("slot1h", [P, 2, NT, P], HT + 8192)
    gidx = rt("gidx", [P, NTILE], U32)
    sidx = rt("sidx", [P, 2, NT], U32)
    eid8, eid9 = rt("eid8", [P, EXTRA, NE]), rt("eid9", [P, EXTRA, NE])
    eid = rt("eid", [P, EXTRA])
    eidi = rt("eidi", [P, EXTRA], I32)
    xtot, npair = rt("extra_tiles", [P, 1]), rt("extra_pairs", [P, 1], I32)
    wk = [w1, w2]
    xg = at("xg", [P, 2, D], W)
    xgT = at("xgT", [P, 2, KD, P], W + 8192)
    a_s = at("a_s", [P, 2, FE], W + 16384)
    a_t = at("a_t", [P, 2, FE], W + 20480)
    aT = at("aT", [P, 2, 4, P], W + 24576)
    ysb = at("ysb", [P, 2, D], HT)
    fgain = at("fgain", [P, D], QK + 20480)
    yg = at("yg", [P, NT, 2, D], RING)
    fo = at("fo", [P, 2, D], W + 16384)

    ps = nc.alloc_psum_tensor("ps", [P, 8, 512], F32)

    mod_d = nc.dram_tensor("mod_d", [NC, 6 * D], F32).ap()
    g_d = nc.dram_tensor("g_d", [HEADS, 640], F32).ap()
    h2_d = nc.dram_tensor("h2_d", [NTOK, D], F32).ap()
    y_d = nc.dram_tensor("y_d", [NTILE * P, D], F32).ap()

    made = {}

    def s(name):
        if name not in made:
            made[name] = sem("s_" + name)
        return made[name]

    rfull = [sem(f"ring_full{i}") for i in range(R1)]
    efull = [sem(f"ering_full{i}") for i in range(R2)]
    s_x = [sem(f"x_full{i}") for i in range(2)]
    s_modst = [sem(f"mod_stored{i}") for i in range(2)]
    s_toep = [sem(f"toep_full{i}") for i in range(2)]
    s_x3 = [sem(f"x3_full{i}") for i in range(2)]
    s_xg = [sem(f"xg_full{i}") for i in range(2)]
    s_yst = [sem(f"y_stored{i}") for i in range(2)]
    s_yg = [sem(f"yg_full{j}") for j in range(NT)]
    s_fst = [sem(f"out_stored{i}") for i in range(2)]
    s_h2st = [sem(f"h2_stored{i}") for i in range(2)]

    def wait_item(eng, i):
        eng.wait_ge(rfull[i % R1], 16 * (i // R1 + 1))

    def used(eng, i):
        if i < IT_WIN:
            eng.wait_ge(s("ada"), i + 1)
        elif i < IT_OH:
            it = i - IT_WIN
            if it == 2:
                eng.wait_ge(s("v"), NT)
            else:
                eng.wait_ge(s("z"), 8 * (it + 1 - (it > 2)))
        elif i == IT_OH:
            eng.wait_ge(s("dbp"), 1)
        elif i < IT_WO:
            g, c = divmod(i - IT_KV, 8)
            eng.wait_ge(s("dS") if c < 4 else s("dOp"), 4 * g + c % 4 + 1)
        else:
            eng.wait_ge(s("woS"), NT)

    def tok(j):
        return slice(j * P, j * P + TW[j])

    block = ctx.enter_context(nc.Block())

    @block.sync
    def _(sp):
        for dst, srcd in ((const[:, :], I["const"]), (par[:, :], I["par"]), (cT[:, :, :], I["cT"]),
                          (ctab33[:, :], I["tab33"]), (ohp[:, :], I["oh_prompt"]),
                          (ct[0][:, :, :], I["ct_re"]), (ct[1][:, :, :], I["ct_im"]),
                          (adab[:, :], I["ada_b"]),
                          (ngain[:, 0, :], I["norm1_g"].partition_broadcast(NC)),
                          (ngain[:, 1, :], I["norm2_g"].partition_broadcast(NC))):
            sp.dma_start(dst, srcd).then_inc(s("init"), 16)

        ada_v = I["ada_w"].rearrange("(k p) n -> p k n", p=P)
        win_v = I["w_in"].rearrange("(k p) n -> p k n", p=P)
        wo_v = I["w_out"].rearrange("(k p) n -> p k n", p=P)

        def item(i):
            if i >= R1:
                used(sp, i - R1)
            r = ring[i % R1]
            if i < IT_WIN:
                c = i - IT_ADA
                dst, src = r[:, :].rearrange("p (k n) -> p k n", k=KD), ada_v[:, :, 512 * c:512 * (c + 1)]
            elif i < IT_OH:
                c = i - IT_WIN
                dst, src = r[:, :].rearrange("p (k n) -> p k n", k=KD), win_v[:, :, 512 * c:512 * (c + 1)]
            elif i == IT_OH:
                dst, src = r[0:BUCKETS + 1, 0:TDEC * DK], I["oh_decode"]
            elif i < IT_WO:
                g, m = divmod(i - IT_KV, 8)
                n = 4 * g + m % 4
                dst, src = r[:, 0:4 * CK], I["cache_v" if m >= 4 else "cache_k"][n]
            else:
                c = i - IT_WO
                dst, src = r[:, :].rearrange("p (k n) -> p k n", k=KD), wo_v[:, :, 512 * c:512 * (c + 1)]
            sp.dma_start(dst, src).then_inc(rfull[i % R1], 16)

        def x_tile(j):
            if j >= 2:
                sp.wait_ge(s("h"), j - 1)
            sp.dma_start(xt[0:TW[j], j % 2, :], I["x"][tok(j), :]).then_inc(s_x[j % 2], 16)

        for i in range(8):
            item(i)
        sp.wait_ge(s("tables"), 1)
        for j in range(2):
            x_tile(j)
        for i in range(8, IT_OH):
            item(i)
        for b in range(2):
            sp.wait_ge(s_modst[b], 16 * N_ADA // 2)
        sp.wait_ge(s("btT"), 8)
        sp.dma_start(modP[:, :, :], mod_d[0:1, 0:2 * D].rearrange("a (v n) -> (a v) n", v=2)
                     .partition_broadcast(P)).then_inc(s("modld"), 16)
        for t in range(TDEC):
            sp.dma_start(modS[t:NS:TDEC, :, :], mod_d[1:NC, 0:2 * D].rearrange("a (v n) -> a v n", v=2))\
              .then_inc(s("modld"), 16)
        for j in range(2, NT):
            x_tile(j)
        for i in range(IT_OH, N_ITEMS):
            item(i)
        sp.wait_ge(s("gluo"), QT + 1)
        sp.wait_ge(s("dOp"), NSEQ)
        sp.wait_ge(s("attS"), 1)
        sp.wait_ge(s("kvst"), 48)
        sp.dma_start(mod3P[:, :, :], mod_d[0:1, 2 * D:5 * D].rearrange("a (v n) -> (a v) n", v=3)
                     .partition_broadcast(P)).then_inc(s("mod3"), 16)
        for t in range(TDEC):
            sp.dma_start(mod3S[t:NS:TDEC, :, :], mod_d[1:NC, 2 * D:5 * D].rearrange("a (v n) -> a v n", v=3))\
              .then_inc(s("mod3"), 16)
        sp.wait_ge(s("attT"), NT)
        sp.wait_ge(s("ssmst"), 48)
        sp.dma_start(rw[:, :, :], I["router_w"]).then_inc(s("mod3"), 16)
        sp.dma_start(rb[:, :], I["router_b"]).then_inc(s("mod3"), 16)
        for j in range(NT):
            if j >= 2:
                sp.wait_ge(s("x2"), j - 1)
            sp.dma_start(xt3[0:TW[j], j % 2, :], I["x"][tok(j), :]).then_inc(s_x3[j % 2], 16)

        done = (s("egate"), s("eup"), s("ey"))

        def expert(e, u):
            for w, (name, k) in enumerate((("w_gate", KD), ("w_up", KD), ("w_down", FE // P))):
                yield (w, ering[3 * u + w][:, :].rearrange("p (k n) -> p k n", k=k),
                       I[name][bass.ds(e, 1)].rearrange("a (k p) n -> p (a k) n", p=P))

        for u in range(2):
            for w, dst, src in expert(u, u):
                m = 3 * u + w
                if m < R1:
                    used(sp, N_ITEMS - R1 + (m - N_ITEMS) % R1)
                if m >= 4:
                    sp.wait_ge(s("yp"), 4 * QT + 1)
                sp.dma_start(dst, src).then_inc(efull[m], 16)
        with sp.Fori(1, NE // 2) as i:
            for u in range(2):
                for w, dst, src in expert(2 * i + u, u):
                    sp.wait_ge(done[w], 2 * i + (u - 1))
                    sp.dma_start(dst, src).then_inc(efull[3 * u + w], 16)
        sp.wait_ge(s("eid"), 1)
        pairs = sp.value_load(npair[0:1, 0:1], min_val=0, max_val=EXTRA // 2)
        with sp.Fori(0, EXTRA // 2) as i:
            with sp.If(pairs > i):
                for u in range(2):
                    e = sp.value_load(eidi[0:1, bass.ds(2 * i + u, 1)], min_val=0, max_val=NE - 1)
                    for w, dst, src in expert(e, u):
                        sp.wait_ge(done[w], 2 * i + (NE + u - 1))
                        sp.dma_start(dst, src).then_inc(efull[3 * u + w], 16)
        sp.wait_ge(s("kvst"), 48)
        sp.wait_ge(s("ssmst"), 48)
        for b in range(2):
            sp.wait_ge(s_fst[b], 16 * ((NT - b + 1) // 2))

    @block.gpsimd
    def _(pool):
        o = Order(pool, s("pool_order"))
        pool.wait_ge(s("init"), 160)
        for b in range(2):
            o(pool.memset(bpad[b][:, :, :], 0.0))
        for half in range(2):
            for r in range(4):
                for b, src in enumerate((bbr, bbi)):
                    if half == 0 and r == 0 and b == 0:
                        pool.wait_ge(s("bbar"), 1)
                    rows = slice(64 * half, 64 * half + 64)
                    c0 = 32 * r + GC * half
                    ins = pool.tensor_copy(bpad[b][rows, r::4, c0:c0 + GC], src[rows, r::4, :])
                    o(ins)
        pool.sem_inc(s("bpad"), 1)
        for n, c in enumerate((2, 3, 8, 9)):
            pool.wait_ge(s("adae"), c + 1)
            m = modsb[:, c % 2, :]
            gn = ngain[:, c // 6, 512 * (c % 2):512 * (c % 2) + 512]
            pool.tensor_tensor(m, m, gn, ALU.mult).then_inc(s("modg"), 1)
        pool.wait_ge(s("modld"), 80)
        for j in range(NT):
            w = TW[j]
            pool.wait_ge(s("hA"), j + 1)
            sh = modP[:, 0, :] if j < QT else modS[:, 0, :]
            pool.tensor_tensor(hb[0:w, j % 2, :], hb[0:w, j % 2, :], sh, ALU.add).then_inc(s("h"), 1)
        pool.wait_ge(s("hTp"), 2 * NT)
        pool.wait_ge(s("h"), NT)
        o(pool.memset(padT[:, :, :], 0.0))
        for t in range(TDEC):
            for n in range(4):
                ins = pool.tensor_copy(padT[:, t, 32 * n + t:32 * n + 32:TDEC], ctab33[:, :])
                o(ins)
        pool.sem_inc(s("padt"), 1)
        pool.wait_ge(s("gst"), 16)
        pool.wait_ge(s("z"), 24)
        for h in range(HEADS):
            if h >= 2:
                pool.wait_ge(s("S"), QT * (h - 1))
            pool.dma_start(toep[:, h % 2, :], bass.AP(g_d.tensor, 640 * h, [[1, P], [1, SEQ]]))\
                .then_inc(s_toep[h % 2], 16)
        pool.wait_ge(s("pt"), HEADS * QT)
        pool.wait_ge(s("pv"), HEADS * QT)
        pool.dma_start(glu[:, 0, :, :], I["glu_a"]).then_inc(s("glul"), 16)
        pool.dma_start(glu[:, 1, :, :], I["glu_b"]).then_inc(s("glul"), 16)
        pool.dma_start(y_d[NE * P:NTILE * P, :], I["zero"].partition_broadcast(EXTRA * P)).then_inc(s("yzero"), 16)
        o(pool.memset(qbd[:, :, :, :], 0.0))
        for h in range(HEADS):
            r = slice(64 * (h % 2), 64 * (h % 2) + 64)
            o(pool.tensor_copy(qbd[r, :, h // 2, TDEC * h:TDEC * (h + 1)],
                               qkT[r, h // 2, SEQ:NTOK].rearrange("p (n t) -> p n t", t=TDEC)))
        pool.sem_inc(s("qbd"), 1)

        def turn_back(i, cs, sn, w=None):
            pool.wait_ge(s("scan"), i + 1)
            if i >= 1:
                pool.wait_ge(s("yp"), i)
            o(pool.tensor_tensor(hr[:, :, :], gr[:, :, :], cs, ALU.mult))
            o(pool.tensor_tensor(xr[:, :, :], gi[:, :, :], sn, ALU.mult))
            o(pool.tensor_tensor(hi[:, :, :], gr[:, :, :], sn, ALU.mult))
            o(pool.tensor_tensor(xi[:, :, :], gi[:, :, :], cs, ALU.mult))
            o(pool.tensor_tensor(hr[:, :, :], hr[:, :, :], xr[:, :, :], ALU.subtract))
            o(pool.tensor_tensor(hi[:, :, :], hi[:, :, :], xi[:, :, :], ALU.add))

        for i in range(16):
            k, q = divmod(i, 4)
            tq = slice(4 * q, 4 * q + 4)
            pool.wait_ge(s("buread"), i + 1)
            o(pool.tensor_tensor(xr[:, :, :], xr[:, :, :], ta[:, :, :], ALU.add))
            pool.tensor_tensor(xi[:, :, :], xi[:, :, :], tb[:, :, :], ALU.subtract).then_inc(s("xadd"), 1)
            pool.wait_ge(s("xadd"), i + 1)
            turn_back(i, cosT[:, tq, :], sinT[:, tq, :])
            lr, li = hr[:, :, CH - 1], hi[:, :, CH - 1]
            if k == QT - 1:
                o(pool.tensor_copy(las[:, tq], lr))
                o(pool.tensor_copy(lai[:, tq], li))
            else:
                o(pool.tensor_tensor(car[:, tq], lr, cth[:, tq], ALU.mult))
                o(pool.tensor_tensor(ctmp[:, 0:4], li, sth[:, tq], ALU.mult))
                o(pool.tensor_tensor(car[:, tq], car[:, tq], ctmp[:, 0:4], ALU.subtract))
                o(pool.tensor_tensor(cai[:, tq], lr, sth[:, tq], ALU.mult))
                o(pool.tensor_tensor(ctmp[:, 4:8], li, cth[:, tq], ALU.mult))
                o(pool.tensor_tensor(cai[:, tq], cai[:, tq], ctmp[:, 4:8], ALU.add))
            pool.sem_inc(s("hout"), 1)

        sv = lambda a: a[:, :, :].rearrange("p a b -> p (a b)").rearrange("p (s n t) -> p s n t", s=STT, n=NSEQ)
        h0v = lambda a: a[:, :, :].rearrange("p a b -> p (a b)")[:, 0:STT * NSEQ].rearrange("p (s n) -> p s n", s=STT)
        tmpv = lambda a, i: a[:, :, :].rearrange("p a b -> p (a b)")[:, 128 * i:128 * i + 128]\
            .rearrange("p (s n) -> p s n", s=STT)
        pool.dma_start(h0v(gr), I["h0_re"]).then_inc(s("h0"), 16)
        pool.dma_start(h0v(gi), I["h0_im"]).then_inc(s("h0"), 16)
        o(pool.tensor_tensor(car[:, :], mag[:, :], cth[:, :], ALU.mult))
        o(pool.tensor_tensor(cai[:, :], mag[:, :], sth[:, :], ALU.mult))
        pool.wait_ge(s("yp"), 16)
        pool.wait_ge(s("buS"), 1)
        pool.wait_ge(s("h0"), 32)
        acr, aci = car[:, :].unsqueeze(2).broadcast_to([P, STT, NSEQ]), cai[:, :].unsqueeze(2).broadcast_to([P, STT, NSEQ])
        for t in range(TDEC):
            pr_, pi_ = (h0v(gr), h0v(gi)) if t == 0 else (sv(hr)[:, :, :, t - 1], sv(hi)[:, :, :, t - 1])
            t1, t2, t3, t4 = tmpv(ta, 0), tmpv(ta, 1), tmpv(ta, 2), tmpv(ta, 3)
            o(pool.tensor_tensor(t1, pr_, acr, ALU.mult))
            o(pool.tensor_tensor(t2, pi_, aci, ALU.mult))
            o(pool.tensor_tensor(t3, pr_, aci, ALU.mult))
            o(pool.tensor_tensor(t4, pi_, acr, ALU.mult))
            o(pool.tensor_tensor(t1, t1, t2, ALU.subtract))
            o(pool.tensor_tensor(t3, t3, t4, ALU.add))
            o(pool.tensor_tensor(sv(hr)[:, :, :, t], t1, sv(xr)[:, :, :, t], ALU.add))
            o(pool.tensor_tensor(sv(hi)[:, :, :, t], t3, sv(xi)[:, :, :, t], ALU.add))
        o(pool.tensor_copy(tmpv(tb, 0), sv(hr)[:, :, :, TDEC - 1]))
        o(pool.tensor_copy(tmpv(tb, 1), sv(hi)[:, :, :, TDEC - 1]))
        pool.sem_inc(s("hout"), 1)
        flat = tb[:, :, :].rearrange("p a b -> p (a b)")
        pool.dma_start(O["ssm_s"], flat[:, 0:256]).then_inc(s("ssmst"), 16)
        pool.dma_start(O["ssm_p"][:, 0, :], las[:, :]).then_inc(s("ssmst"), 16)
        pool.dma_start(O["ssm_p"][:, 1, :], lai[:, :]).then_inc(s("ssmst"), 16)

        pool.wait_ge(s("mod3"), 112)
        for j in range(NT):
            w = TW[j]
            m3 = mod3P if j < QT else mod3S
            pool.wait_ge(s("wog"), j + 1)
            pool.wait_ge(s_x3[j % 2], 16 * (j // 2 + 1))
            o(pool.tensor_tensor(pt2[0:w, :], pt1[0:w, j % 2, :], m3[0:w, 0, :], ALU.mult))
            pool.tensor_tensor(x2[0:w, j, :], pt2[0:w, :], xt3[0:w, j % 2, :], ALU.add).then_inc(s("x2"), 1)
            pool.wait_ge(s("hA"), NT + j + 1)
            pool.tensor_tensor(h2[0:w, j % 2, :], h2[0:w, j % 2, :], m3[0:w, 1, :], ALU.add).then_inc(s("h"), 1)
            pool.wait_ge(s("h"), NT + j + 1)
            pool.dma_start(h2_d[tok(j), :], h2[0:w, j % 2, :]).then_inc(s_h2st[j % 2], 16)
        pool.wait_ge(s_h2st[0], 48)
        pool.wait_ge(s_h2st[1], 32)
        pool.wait_ge(s("gidx"), 1)

        def gather(t):
            u = t % 2
            if t >= 2:
                pool.wait_ge(s("xgp"), t - 1)
                pool.wait_ge(s_xg[u], 16 * (t // 2))
            pool.indirect_dma_start(xg[:, u, :], None, h2_d, bass.IndirectOffsetOnAxis(ap=gidx[:, t:t + 1], axis=0))\
                .then_inc(s_xg[u], 16)

        for t in range(NE):
            gather(t)
        pool.wait_ge(s("eid"), 1)
        pairs = pool.value_load(npair[0:1, 0:1], min_val=0, max_val=EXTRA // 2)
        for i in range(EXTRA // 2):
            with pool.If(pairs > i):
                gather(NE + 2 * i)
                gather(NE + 2 * i + 1)
        pool.wait_ge(s("y_all"), 1)
        for j in range(NT):
            w = TW[j]
            for k in range(2):
                pool.indirect_dma_start(yg[0:w, j, k, :], None, y_d,
                                        bass.IndirectOffsetOnAxis(ap=sidx[0:w, k, j:j + 1], axis=0))\
                    .then_inc(s_yg[j], 16)
        for j in range(NT):
            w = TW[j]
            g2 = mod3P[0:w, 1, :] if j < QT else mod3S[0:w, 0, :]
            pool.wait_ge(s("endld"), 96)
            pool.wait_ge(s("ysum"), j + 1)
            a = yg[0:w, j, 0, :]
            pool.tensor_tensor(a, a, g2, ALU.mult).then_inc(s("ygate"), 1)

    @block.scalar
    def _(act):
        o = Order(act, s("act_order"))

        def f(out, in_, func, **kw):
            return nc.scalar.activation(out, in_, func, **kw)

        act.wait_ge(s("init"), 160)
        f(cE[:, :, :], cT[:, :, :], ACT.Exp, scale=-1.0).then_inc(s("cexp"), 1)
        f(pr[:, 1, :], par[:, PC["log_dt"][0]:PC["log_dt"][1]], ACT.Exp).then_inc(s("dt"), 1)
        act.wait_ge(s("magin"), 1)
        f(mag[:, :], pr[:, 2, :], ACT.Exp).then_inc(s("mag"), 1)
        act.wait_ge(s("phr"), 1)
        f(pr[:, 5, :], pr[:, 4, :], ACT.Sin).then_inc(s("sin"), 1)
        f(pr[:, 6, :], pr[:, 4, :], ACT.Sin, scale=0.5).then_inc(s("sin"), 1)
        for c in range(N_ADA):
            act.wait_ge(s("ada"), c + 1)
            if c >= 2:
                act.wait_ge(s_modst[c % 2], 16 * (c // 2))
            scale_row = c in (2, 3, 8, 9)
            f(modsb[:, c % 2, :], ps[0:NC, c % 2, :], ACT.Copy, bias=1.0 if scale_row else 0.0)\
                .then_inc(s("adae"), 1)
            if scale_row:
                act.wait_ge(s("modg"), {2: 1, 3: 2, 8: 3, 9: 4}[c])
            else:
                act.wait_ge(s("adae"), c + 1)
            act.dma_start(mod_d[:, 512 * c:512 * (c + 1)], modsb[:, c % 2, :]).then_inc(s_modst[c % 2], 16)
            if c == 3:
                for n in range(8):
                    act.wait_ge(s("btT"), n + 1)
                    b, q = n // 4, n % 4
                    f(bt[b][:, 4 * q:4 * q + 4, :], ps[:, 2 + n % 2, :].rearrange("p (a b) -> p a b", a=4), ACT.Copy)\
                        .then_inc(s("btTe"), 1)
        act.wait_ge(s("gsb"), 1)
        act.dma_start(g_d, gsb[:, :]).then_inc(s("gst"), 16)
        for j in range(NT):
            w = TW[j]
            act.wait_ge(s_x[j % 2], 16 * (j // 2 + 1))
            f(ps[0:w, 6:8, :], xt[0:w, j % 2, :].rearrange("p (a b) -> p a b", a=2), ACT.Square,
              accum_out=stat[0:w, j:j + 1]).then_inc(s("sq"), 1)
            act.wait_ge(s("rin"), j + 1)
            f(stat[0:w, 16 + j:17 + j], stat[0:w, 8 + j:9 + j], ACT.Sqrt).then_inc(s("rt"), 1)
            act.wait_ge(s("hTp"), 2 * j + 1)
            act.wait_ge(s("gst"), 16)
            f(hT[:, 0:4, tok(j)], ps[:, 2 + 2 * (j % 2), 0:4 * w].rearrange("p (a b) -> p a b", a=4), ACT.Copy)\
                .then_inc(s("hTa"), 1)
        for z in range(12):
            kind, c = divmod(z, 4)
            act.wait_ge(s("z"), 2 * z + 1)
            dst = qkT[:, 4 * kind + c, 0:SEQ] if kind < 2 else uT[:, c, 0:SEQ]
            f(dst, ps[:, z % 2, :], ACT.Copy, scale=DH ** -0.5 if kind == 0 else 1.0).then_inc(s("za"), 1)
        act.wait_ge(s("za"), 12)
        act.wait_ge(s("zd"), 12)
        act.wait_ge(s("ve"), NT)
        act.dma_start(O["kT"].rearrange("(c p) t -> p c t", p=P), qkT[:, 4:8, :]).then_inc(s("kvst"), 16)
        act.dma_start(O["v"][0:SEQ, :].rearrange("(j p) n -> p j n", p=P), vrow[:, 0:QT, :]).then_inc(s("kvst"), 16)
        act.dma_start(O["v"][SEQ:NTOK, :], vrow[0:NS, QT, :]).then_inc(s("kvst"), 16)
        for st in range(HEADS * QT):
            qt = st % QT
            m = P * (qt + 1)
            act.wait_ge(s("sm"), st + 1)
            if st >= 2:
                act.wait_ge(s("rd"), st - 1)
                act.wait_ge(s("pt"), st - 1)
            f(Sb[:, st % 2, 0:m], ps[:, st % 2, 0:m], ACT.Exp, bias=stat[:, 26 + st % 2:27 + st % 2],
              accum_out=stat[:, 28 + st % 2:29 + st % 2]).then_inc(s("P"), 1)
            act.wait_ge(s("pt"), st + 1)
            if st >= 2:
                act.wait_ge(s("pv"), st - 1)
            f(PTs[:, st % 2, 0:m], ps[:, 2 + st % 2, 0:m], ACT.Copy).then_inc(s("ptr"), 1)

        def att_norm(j):
            w = TW[j]
            f(ps[0:w, 0, :], att[0:w, j, :], ACT.Square, accum_out=stat[0:w, j:j + 1]).then_inc(s("sq"), 1)
            act.wait_ge(s("rin"), NT + j + 1)
            f(stat[0:w, 16 + j:17 + j], stat[0:w, 8 + j:9 + j], ACT.Sqrt).then_inc(s("rt"), 1)

        act.wait_ge(s("att"), HEADS * QT)
        for j in range(QT):
            att_norm(j)

        def gelu(n, w):
            act.wait_ge(s("yread"), n + 1)
            f(y2[:, :, 0:w], yd[:, :, 0:w], ACT.Square).then_inc(s("ysq"), 1)
            act.wait_ge(s("gin"), n + 1)
            f(th[:, :, 0:w], y2[:, :, 0:w], ACT.Tanh, scale=float(np.sqrt(2.0 / np.pi))).then_inc(s("gth"), 1)
            act.wait_ge(s("glut"), n + 1)
            f(th[:, :, 0:w], ps[:, 6, 0:4 * w].rearrange("p (a b) -> p a b", a=4), ACT.Tanh, scale=0.25)\
                .then_inc(s("gate"), 1)

        def dec_exp(g):
            act.wait_ge(s("dSm"), g + 1)
            f(dP[:, :], dP[:, :], ACT.Exp, bias=dstat[:, 4:5], accum_out=dstat[:, 5:6]).then_inc(s("dP"), 1)
            act.wait_ge(s("dPt"), g + 1)
            if g:
                act.wait_ge(s("dOp"), 4 * g)
            f(dPT[:, 4:7, :], ps[:, 3, 0:3 * P].rearrange("p (a b) -> p a b", a=3), ACT.Copy)
            f(dPT[0:NS, 7, :], ps[0:NS, 3, 3 * P:4 * P], ACT.Copy).then_inc(s("dPta"), 1)

        dec_exp(0)
        gelu(0, CH)
        gelu(1, CH)
        dec_exp(1)
        gelu(2, CH)
        gelu(3, CH)
        gelu(4, NS)
        act.wait_ge(s("attS"), 1)
        att_norm(QT)
        act.wait_ge(s("ssin"), 1)
        f(dstat[:, 24:24 + NT], dstat[:, 16:16 + NT], ACT.Sqrt).then_inc(s("ssrt"), 1)
        for j in range(NT):
            w = TW[j]
            act.wait_ge(s("woA"), j + 1)
            if j >= 2:
                act.wait_ge(s("x2"), j - 1)
            f(pt1[0:w, j % 2, :].rearrange("p (a b) -> p a b", a=2), ps[0:w, 0:2, :], ACT.Copy).then_inc(s("woa"), 1)
            act.wait_ge(s("x2"), j + 1)
            if j >= 2:
                act.wait_ge(s("hTp"), 2 * (NT + j - 1))
                act.wait_ge(s_h2st[j % 2], 16 * (j // 2))
            f(h2[0:w, j % 2, :], x2[0:w, j, :], ACT.Square,
              accum_out=stat[0:w, j:j + 1]).then_inc(s("sq"), 1)
            act.wait_ge(s("rin"), 2 * NT + j + 1)
            f(stat[0:w, 16 + j:17 + j], stat[0:w, 8 + j:9 + j], ACT.Sqrt).then_inc(s("rt"), 1)
            act.wait_ge(s("hTp"), 2 * (NT + j) + 1)
            f(h2T[:, 0:4, tok(j)], ps[:, 6, 0:4 * w].rearrange("p (a b) -> p a b", a=4), ACT.Copy)\
                .then_inc(s("hTa"), 1)
        act.wait_ge(s("h"), 2 * NT)
        act.wait_ge(s("x2"), NT)
        act.dma_start(mod3P[:, 1, :], mod_d[0:1, 5 * D:6 * D].partition_broadcast(P)).then_inc(s("endld"), 16)
        for t in range(TDEC):
            act.dma_start(mod3S[t:NS:TDEC, 0, :], mod_d[1:NC, 5 * D:6 * D]).then_inc(s("endld"), 16)
        act.dma_start(fgain[:, :], I["final_g"].partition_broadcast(P)).then_inc(s("endld"), 16)
        act.wait_ge(s("gexpin"), 1)
        f(g4b[:, :, :], g4a[:, :, :], ACT.Exp).then_inc(s("gexp"), 1)
        act.wait_ge(s("gapin"), 1)
        f(w2[:, :], v2[:, :], ACT.Exp).then_inc(s("gapexp"), 1)

        def rows(t, u):
            act.wait_ge(s("xgp"), t + 1)
            f(xgT[:, u, 0:4, :], ps[:, 4, :].rearrange("p (a b) -> p a b", a=4), ACT.Copy).then_inc(s("xga"), 1)

        def gate(t, u):
            act.wait_ge(s("egate"), t + 1)
            f(a_t[:, u, :], ps[:, u, :], ACT.Tanh, scale=0.5).then_inc(s("eth"), 1)

        def hidden(t, u):
            act.wait_ge(s("aTp"), t + 1)
            f(aT[:, u, :, :], ps[:, u, :].rearrange("p (a b) -> p a b", a=4), ACT.Copy).then_inc(s("aTe"), 1)

        def finish(t, u, dst, waity):
            act.wait_ge(s("ey"), t + 1)
            if waity is not None:
                act.wait_ge(s_yst[u], waity)
            f(ysb[:, u, 0:512], ps[:, 6, :], ACT.Copy).then_inc(s("eya"), 1)
            act.wait_ge(s("eya"), t + 1)
            act.wait_ge(s("eyd"), t + 1)
            act.dma_start(dst, ysb[:, u, :]).then_inc(s_yst[u], 16)

        def y_tile(t):
            return y_d.rearrange("(t p) n -> t p n", p=P)[bass.ds(t, 1)].rearrange("t p n -> (t p) n")

        rows(0, 0)
        gate(0, 0)
        rows(1, 1)
        for t in (1, 2):
            u = t % 2
            gate(t, u)
            hidden(t - 1, 1 - u)
            rows(t + 1, 1 - u)
            finish(t - 1, 1 - u, y_d[P * (t - 1):P * t, :], None)
        with act.Fori(1, NE // 2 - 1) as i:
            for u in (1, 0):
                t = 2 * i + (2 - u)
                gate(t, u)
                hidden(2 * i + (1 - u), 1 - u)
                rows(2 * i + (3 - u), 1 - u)
                finish(2 * i + (1 - u), 1 - u, y_tile(2 * i + (1 - u)), 16 * i)
        gate(NE - 1, 1)
        hidden(NE - 2, 0)
        finish(NE - 2, 0, y_tile(NE - 2), 16 * (NE // 2 - 1))
        hidden(NE - 1, 1)
        finish(NE - 1, 1, y_tile(NE - 1), 16 * (NE // 2 - 1))
        act.wait_ge(s("eid"), 1)
        act.wait_ge(s("yzero"), 16)
        pairs = act.value_load(npair[0:1, 0:1], min_val=0, max_val=EXTRA // 2)
        with act.Fori(0, EXTRA // 2) as i:
            with act.If(pairs > i):
                rows(2 * i + NE, 0)
                gate(2 * i + NE, 0)
                rows(2 * i + (NE + 1), 1)
                gate(2 * i + (NE + 1), 1)
                for u in range(2):
                    hidden(2 * i + (NE + u), u)
                    finish(2 * i + (NE + u), u, y_tile(2 * i + (NE + u)), 16 * i + 16 * (NE // 2))
        for u in range(2):
            act.wait_ge(s_yst[u], 16 * pairs + 16 * (NE // 2))
        act.sem_inc(s("y_all"), 1)
        for n in range(NT + 2):
            if n < NT:
                j, w = n, TW[n]
                act.wait_ge(s_yg[j], 32)
                f(yg[0:w, j, 0, :], yg[0:w, j, 0, :], ACT.Copy, scale=w1[0:w, j:j + 1]).then_inc(s("yw"), 1)
            if n < 2:
                continue
            j = n - 2
            w = TW[j]
            act.wait_ge(s("x3"), j + 1)
            f(ps[0:w, 0:2, :], x2[0:w, j, :].rearrange("p (a b) -> p a b", a=2), ACT.Square,
              accum_out=stat[0:w, j:j + 1]).then_inc(s("sq"), 1)
            act.wait_ge(s("rin"), 3 * NT + j + 1)
            f(stat[0:w, 16 + j:17 + j], stat[0:w, 8 + j:9 + j], ACT.Sqrt).then_inc(s("rt"), 1)
            act.wait_ge(s("fo"), j + 1)
            act.dma_start(O["y"][tok(j), :], fo[0:w, j % 2, :]).then_inc(s_fst[j % 2], 16)

    @block.vector
    def _(dve):
        o = Order(dve, s("dve_order"))
        v = nc.vector
        tt_, ts_, stt = v.tensor_tensor, v.tensor_scalar, v.scalar_tensor_tensor
        o(v.memset(stat[:, :], 1.0))
        o(v.memset(dstat[:, :], 1.0))
        dve.wait_ge(s("init"), 160)

        pa = lambda n: par[:, PC[n][0]:PC[n][1]]
        q_ = lambda i: pr[:, i, :]
        lam_re, lam_im, dt = q_(0), pa("a_im"), q_(1)
        o(ts_(lam_re, pa("a_re"), -1e-4, None, ALU.min))
        dve.wait_ge(s("dt"), 1)
        tt_(q_(2), lam_re, dt, ALU.mult).then_inc(s("magin"), 1)
        o(tt_(q_(3), lam_im, dt, ALU.mult))
        big = float(3 << 22)
        c1 = 6.28125
        o(ts_(q_(7), q_(3), 1.0 / (2 * np.pi), big, ALU.mult, ALU.add))
        o(ts_(q_(7), q_(7), -big, None, ALU.add))
        o(stt(out=q_(4), in0=q_(7), scalar=-c1, in1=q_(3), op0=ALU.mult, op1=ALU.add))
        o(stt(out=q_(4), in0=q_(7), scalar=-(2 * np.pi - c1), in1=q_(4), op0=ALU.mult, op1=ALU.add))
        ts_(q_(4), q_(4), 3.1415925, -3.1415925, ALU.min, ALU.max).then_inc(s("phr"), 1)
        dve.wait_ge(s("cexp"), 1)
        o(ts_(cE[:, :, :], cE[:, :, :], 1.0, None, ALU.add))
        o(v.reciprocal(cE[:, :, :], cE[:, :, :]))
        tt_(cS[:, :, :], cT[:, :, :], cE[:, :, :], ALU.mult).then_inc(s("cs"), 1)
        dve.wait_ge(s("sin"), 2)
        o(v.tensor_copy(sth[:, :], q_(5)))
        o(tt_(q_(8), q_(6), q_(6), ALU.mult))
        o(ts_(cth[:, :], q_(8), -2.0, 1.0, ALU.mult, ALU.add))
        dve.wait_ge(s("mag"), 1)
        o(tt_(q_(9), mag[:, :], cth[:, :], ALU.mult))
        o(tt_(q_(10), mag[:, :], sth[:, :], ALU.mult))
        o(ts_(q_(11), q_(9), -1.0, None, ALU.add))
        o(tt_(q_(12), lam_re, lam_re, ALU.mult))
        o(tt_(q_(13), lam_im, lam_im, ALU.mult))
        o(tt_(q_(12), q_(12), q_(13), ALU.add))
        o(v.reciprocal(q_(12), q_(12)))
        o(tt_(q_(13), q_(11), lam_re, ALU.mult))
        o(tt_(q_(14), q_(10), lam_im, ALU.mult))
        o(tt_(q_(13), q_(13), q_(14), ALU.add))
        o(tt_(q_(13), q_(13), q_(12), ALU.mult))
        o(tt_(q_(14), q_(10), lam_re, ALU.mult))
        o(tt_(q_(15), q_(11), lam_im, ALU.mult))
        o(tt_(q_(14), q_(14), q_(15), ALU.subtract))
        o(tt_(q_(14), q_(14), q_(12), ALU.mult))
        crb = q_(13).unsqueeze(2).broadcast_to([P, STT, GC])
        cib = q_(14).unsqueeze(2).broadcast_to([P, STT, GC])
        b_re, b_im = [pa(n).rearrange("p (a b) -> p a b", a=STT) for n in ("b_re", "b_im")]
        o(tt_(bt1[:, :, :], b_re, crb, ALU.mult))
        o(tt_(bt2[:, :, :], b_im, cib, ALU.mult))
        o(tt_(bbr[:, :, :], bt1[:, :, :], bt2[:, :, :], ALU.subtract))
        o(tt_(bt1[:, :, :], b_im, crb, ALU.mult))
        o(tt_(bt2[:, :, :], b_re, cib, ALU.mult))
        tt_(bbi[:, :, :], bt1[:, :, :], bt2[:, :, :], ALU.add).then_inc(s("bbar"), 1)
        o(v.tensor_copy(gains[:, :], par[:, PC["dskip"][0]:PC["ssmg"][1]]))
        o(ts_(ct[1][:, :, :], ct[1][:, :, :], -1.0, None, ALU.mult))
        o(v.memset(cosT[:, :, 0:1], 1.0))
        o(v.memset(sinT[:, :, 0:1], 0.0))
        cm, sm_, c2, s2, c3, s3 = [q_(i) for i in (2, 3, 4, 5, 6, 7)]
        o(v.tensor_copy(cm, cth[:, :]))
        o(v.tensor_copy(sm_, sth[:, :]))
        m = 1
        while m < CH:
            cb, sb_ = [a.unsqueeze(2).broadcast_to([P, STT, m]) for a in (cm, sm_)]
            C_, S_ = cosT[:, :, 0:m], sinT[:, :, 0:m]
            Cn, Sn = cosT[:, :, m:2 * m], sinT[:, :, m:2 * m]
            o(tt_(Cn, C_, cb, ALU.mult))
            o(tt_(dt1[:, :, 0:m], S_, sb_, ALU.mult))
            o(tt_(Cn, Cn, dt1[:, :, 0:m], ALU.subtract))
            o(tt_(Sn, C_, sb_, ALU.mult))
            o(tt_(dt2[:, :, 0:m], S_, cb, ALU.mult))
            o(tt_(Sn, Sn, dt2[:, :, 0:m], ALU.add))
            o(tt_(c2, cm, cm, ALU.mult))
            o(tt_(c3, sm_, sm_, ALU.mult))
            o(tt_(s2, cm, sm_, ALU.mult))
            o(tt_(cm, c2, c3, ALU.subtract))
            o(ts_(sm_, s2, 2.0, None, ALU.mult))
            m *= 2
        dve.sem_inc(s("tables"), 1)
        dve.wait_ge(s("gp"), 1)
        v.tensor_copy(gsb[:, :], ps[0:HEADS, 6:8, :].rearrange("p a b -> p (a b)")[:, 0:640]).then_inc(s("gsb"), 1)

        def rstd(j, w, width, n):
            dve.wait_ge(s("sq"), n)
            ts_(stat[0:w, 8 + j:9 + j], stat[0:w, j:j + 1], 1.0 / width, EPS, ALU.mult, ALU.add).then_inc(s("rin"), 1)
            dve.wait_ge(s("rt"), n)
            o(v.reciprocal(stat[0:w, 56 + j:57 + j], stat[0:w, 16 + j:17 + j]))

        dve.wait_ge(s("bpad"), 1)
        for j in range(NT):
            w = TW[j]
            rstd(j, w, D, j + 1)
            dve.wait_ge(s("modld"), 80)
            if j >= 2:
                dve.wait_ge(s("hTp"), 2 * (j - 1))
            A = modP[:, 1, :] if j < QT else modS[:, 1, :]
            stt(out=hb[0:w, j % 2, :], in0=xt[0:w, j % 2, :], scalar=stat[0:w, 56 + j:57 + j], in1=A,
                op0=ALU.mult, op1=ALU.mult).then_inc(s("hA"), 1)
            dve.wait_ge(s("gst"), 16)
            dve.wait_ge(s("hTp"), 2 * j + 2)
            v.tensor_copy(hT[:, 4:8, tok(j)], ps[:, 3 + 2 * (j % 2), 0:4 * w].rearrange("p (a b) -> p a b", a=4))\
                .then_inc(s("hTd"), 1)

        def z_small(z):
            kind, c = divmod(z, 4)
            dve.wait_ge(s("z"), 2 * z + 2)
            dst = qkT[:, 4 * kind + c, SEQ:NTOK] if kind < 2 else uT[:, c, SEQ:NTOK]
            ts_(dst, ps[:, 6 + z % 2, 0:NS], DH ** -0.5 if kind == 0 else 1.0, None, ALU.mult).then_inc(s("zd"), 1)

        for z in range(8):
            z_small(z)
        for j in range(NT):
            w = TW[j]
            dve.wait_ge(s("v"), j + 1)
            v.tensor_copy(vrow[0:w, j, :], ps[0:w, 2 + j % 2, :]).then_inc(s("ve"), 1)
        for z in range(8, 12):
            z_small(z)
        dve.wait_ge(s("dbp"), 1)
        o(v.tensor_copy(dbias[:, :], ps[:, 2:4, :].rearrange("p a b -> p (a b)")[:, 0:DK]))
        for g in range(2):
            o(tt_(nbias[:, NS * g:NS * g + NS], dbias[:, CK:DK], cst("newmask")[:, NS * g:NS * g + NS], ALU.add))
        dve.sem_inc(s("dbias"), 1)

        NST = HEADS * QT

        def row_max(st):
            h, qt = divmod(st, QT)
            b, m = st % 2, P * (qt + 1)
            dve.wait_ge(s("S"), st + 1)
            o(v.tensor_reduce(stat[:, 24 + b:25 + b], ps[:, b, 0:m], AX.X, ALU.max))
            ts_(stat[:, 26 + b:27 + b], stat[:, 24 + b:25 + b], -1.0, None, ALU.mult).then_inc(s("sm"), 1)

        def head_out(st):
            h, qt = divmod(st, QT)
            b = st % 2
            dve.wait_ge(s("P"), st + 1)
            v.reciprocal(stat[:, 30 + b:31 + b], stat[:, 28 + b:29 + b]).then_inc(s("rd"), 1)
            dve.wait_ge(s("rd"), st + 1)
            dve.wait_ge(s("pv"), st + 1)
            ts_(att[:, qt, DH * h:DH * (h + 1)], ps[:, 4 + qt, DH * h:DH * (h + 1)], stat[:, 30 + b:31 + b], None,
                ALU.mult).then_inc(s("att"), 1)

        for st in range(NST + 2):
            if st < NST:
                row_max(st)
            if st >= 2:
                head_out(st - 2)

        def att_tile(j):
            w = TW[j]
            rstd(j, w, AW, NT + j + 1)
            ts_(att[0:w, j, :], att[0:w, j, :], stat[0:w, 56 + j:57 + j], None, ALU.mult).then_inc(s("attn"), 1)
            dve.wait_ge(s("attT"), j + 1)
            for c in range(4):
                ins = ts_(mixT[:, c, tok(j)], ps[:, 1 + j % 2, w * c:w * (c + 1)], gains[:, 4 + c:5 + c], None, ALU.mult)
            ins.then_inc(s("attTe"), 1)

        dve.wait_ge(s("att"), NST)
        for j in range(QT):
            att_tile(j)

        def turn_in(i):
            q = i % 4
            cs, sn = cosT[:, 4 * q:4 * q + 4, :], sinT[:, 4 * q:4 * q + 4, :]
            bre, bim = [ps[:, 5 + n, :].rearrange("p (a b) -> p a b", a=4) for n in range(2)]
            dve.wait_ge(s("bu"), i + 1)
            if i >= 1:
                dve.wait_ge(s("hout"), i)
            tt_(xr[:, :, :], bre, cs, ALU.mult)
            tt_(ta[:, :, :], bim, sn, ALU.mult)
            tt_(xi[:, :, :], bim, cs, ALU.mult)
            tt_(tb[:, :, :], bre, sn, ALU.mult).then_inc(s("buread"), 1)

        def scans(i):
            k, q = divmod(i, 4)
            dve.wait_ge(s("xadd"), i + 1)
            for r in range(4):
                t = 4 * q + r
                m = mag[:, t:t + 1].broadcast_to([P, CH])
                v.tensor_tensor_scan(gr[:, r, :], m, xr[:, r, :], 0.0 if k == 0 else car[:, t:t + 1], ALU.mult, ALU.add)
                ins = v.tensor_tensor_scan(gi[:, r, :], m, xi[:, r, :], 0.0 if k == 0 else cai[:, t:t + 1],
                                           ALU.mult, ALU.add)
            ins.then_inc(s("scan"), 1)

        def gelu_glu(n, w, t0):
            dve.wait_ge(s("yp"), 4 * n + 4 if n < QT else 4 * QT + 1)
            for q in range(4):
                ins = stt(out=yd[:, q, 0:w], in0=uT[:, q, t0:t0 + w], scalar=gains[:, q:q + 1],
                          in1=ps[:, 7, w * q:w * (q + 1)], op0=ALU.mult, op1=ALU.add)
            ins.then_inc(s("yread"), 1)
            dve.wait_ge(s("ysq"), n + 1)
            o(ts_(y2[:, :, 0:w], y2[:, :, 0:w], 0.044715, 1.0, ALU.mult, ALU.add))
            tt_(y2[:, :, 0:w], y2[:, :, 0:w], yd[:, :, 0:w], ALU.mult).then_inc(s("gin"), 1)
            dve.wait_ge(s("gth"), n + 1)
            stt(out=y2[:, :, 0:w], in0=th[:, :, 0:w], scalar=1.0, in1=yd[:, :, 0:w], op0=ALU.add, op1=ALU.mult)\
                .then_inc(s("gel"), 1)
            dve.wait_ge(s("gate"), n + 1)
            ga = ps[:, 5, 0:4 * w].rearrange("p (a b) -> p a b", a=4)
            o(stt(out=y2[:, :, 0:w], in0=th[:, :, 0:w], scalar=1.0, in1=ga, op0=ALU.add, op1=ALU.mult))
            for q in range(4):
                ts_(mixT[:, 4 + q, t0:t0 + w], y2[:, q, 0:w], gains[:, 8 + q:9 + q], 0.25, ALU.mult, ALU.mult)
            stt(out=yd[:, :, 0:w], in0=y2[:, :, 0:w], scalar=0.0625, in1=y2[:, :, 0:w], op0=ALU.mult, op1=ALU.mult)\
                .then_inc(s("gsq"), 1)
            dve.wait_ge(s("ssp"), n + 1)
            v.tensor_copy(dstat[0:w, 8 + n:9 + n], ps[0:w, 5, 0:1]).then_inc(s("gluo"), 1)

        def dec_softmax(g):
            dve.wait_ge(s("dS"), 4 * (g + 1))
            if g:
                dve.wait_ge(s("dPt"), g)
            flat = ps[:, 0:2, :].rearrange("p a b -> p (a b)")
            o(v.tensor_tensor_reduce(out=dP[:, 0:CK], in0=flat[:, 0:CK], in1=dbias[:, 0:CK], scale=1.0,
                                     scalar=-3.0e38, op0=ALU.add, op1=ALU.max, accum_out=dstat[:, 0:1]))
            o(v.tensor_tensor_reduce(out=dP[:, CK:DK], in0=flat[:, CK:DK], in1=nbias[:, NS * g:NS * g + NS], scale=1.0,
                                     scalar=-3.0e38, op0=ALU.add, op1=ALU.max, accum_out=dstat[:, 1:2]))
            o(tt_(dstat[:, 2:3], dstat[:, 0:1], dstat[:, 1:2], ALU.max))
            ts_(dstat[:, 4:5], dstat[:, 2:3], -1.0, None, ALU.mult).then_inc(s("dSm"), 1)

        def dec_probs(g):
            dve.wait_ge(s("dP"), g + 1)
            o(v.reciprocal(dstat[:, 6:7], dstat[:, 5:6]))
            dve.wait_ge(s("dPt"), g + 1)
            if g:
                dve.wait_ge(s("dOp"), 4 * g)
            v.tensor_copy(dPT[:, 0:4, :], ps[:, 2, :].rearrange("p (a b) -> p a b", a=4)).then_inc(s("dPtd"), 1)

        def dec_out(g):
            dve.wait_ge(s("dOp"), 4 * (g + 1))
            stt(out=dO[:, g, :], in0=ps[:, 4, :], scalar=dstat[:, 6:7], in1=cst("headsel"),
                op0=ALU.mult, op1=ALU.mult).then_inc(s("dOe"), 1)

        for i in range(16):
            if i in (3, 11):
                dec_softmax(i // 8)
            turn_in(i)
            scans(i)
            if i in (3, 11):
                dec_probs(i // 8)
            if i % 4 == 3:
                gelu_glu(i // 4, CH, CH * (i // 4))
            if i == 8:
                dec_out(0)
        dve.wait_ge(s("bu"), 17)
        dve.wait_ge(s("hout"), 16)
        o(v.tensor_copy(xr[:, :, :].rearrange("p a b -> p (a b)"), ps[:, 5, :]))
        v.tensor_copy(xi[:, :, :].rearrange("p a b -> p (a b)"), ps[:, 6, :]).then_inc(s("buS"), 1)
        dec_out(1)
        dve.wait_ge(s("attSp"), 1)
        v.tensor_copy(att[0:NS, QT, :], ps[0:NS, 4, :]).then_inc(s("attS"), 1)
        gelu_glu(QT, NS, SEQ)
        att_tile(QT)
        dve.wait_ge(s("gluo"), NT)
        ts_(dstat[:, 16:16 + NT], dstat[:, 8:8 + NT], 1.0 / (D - AW), EPS, ALU.mult, ALU.add).then_inc(s("ssin"), 1)
        dve.wait_ge(s("ssrt"), 1)
        o(v.reciprocal(rssm[:, 0:NT], dstat[:, 24:24 + NT]))
        o(v.memset(lg[:, :, :], 0.0))

        dve.wait_ge(s("mod3"), 112)

        def join(j):
            w = TW[j]
            dve.wait_ge(s("woa"), j + 1)
            dve.wait_ge(s("woS"), j + 1)
            a = pt1[0:w, j % 2, :].rearrange("p (a b) -> p a b", a=2)
            stt(out=a, in0=ps[0:w, 2:4, :], scalar=rssm[0:w, j:j + 1], in1=a, op0=ALU.mult, op1=ALU.add)\
                .then_inc(s("wog"), 1)

        for j in range(NT):
            w = TW[j]
            m3 = mod3P if j < QT else mod3S
            join(j)
            rstd(j, w, D, 2 * NT + j + 1)
            stt(out=h2[0:w, j % 2, :], in0=x2[0:w, j, :], scalar=stat[0:w, 56 + j:57 + j], in1=m3[0:w, 2, :],
                op0=ALU.mult, op1=ALU.mult).then_inc(s("hA"), 1)
            dve.wait_ge(s("hTp"), 2 * (NT + j) + 2)
            v.tensor_copy(h2T[:, 4:8, tok(j)], ps[:, 7, 0:4 * w].rearrange("p (a b) -> p a b", a=4))\
                .then_inc(s("hTd"), 1)
            dve.wait_ge(s("lg"), j + 1)
            o(v.tensor_copy(lg[0:w, j, :], ps[0:w, 4, 20 * j:20 * j + 20]))

        G = lg[:, :, 0:4]
        Lv = lg[:, :, 4:20].rearrange("p j (g e) -> p j g e", g=NG)
        b4 = lambda a: a[:, :].unsqueeze(2).broadcast_to([P, NT, 4])
        first = cst("first").unsqueeze(1).broadcast_to([P, NT, 4])

        def first_max(hot, vals, top, t1):
            o(v.tensor_reduce(top[:, :], vals, AX.X, ALU.max))
            o(tt_(t1[:, :, :], vals, b4(top), ALU.is_equal))
            o(tt_(t1[:, :, :], t1[:, :, :], first, ALU.mult))
            o(v.tensor_reduce(gmax[:, :], t1[:, :, :], AX.X, ALU.max))
            o(tt_(hot[:, :, :], t1[:, :, :], b4(gmax), ALU.is_equal))

        first_max(ghot, G, gsum, g4c)
        tt_(g4a[:, :, :], G, b4(gsum), ALU.subtract).then_inc(s("gexpin"), 1)
        o(tt_(ghot[:, :, :], ghot[:, :, :], b4(cst("valid")), ALU.mult))
        e44 = lambda a: a[:, :, :].rearrange("p j (g e) -> p j g e", g=NG)
        gh4 = ghot[:, :, :].unsqueeze(3).broadcast_to([P, NT, NG, EPG])
        o(tt_(e44(e16), Lv, gh4, ALU.mult))
        o(v.tensor_reduce(esel[:, :, :], e16[:, :, :].rearrange("p j (g e) -> p j e g", g=NG), AX.X, ALU.add))
        first_max(o1, esel[:, :, :], v1, g4c)
        o(stt(out=esel[:, :, :], in0=o1[:, :, :], scalar=NEG, in1=esel[:, :, :], op0=ALU.mult, op1=ALU.add))
        first_max(o2, esel[:, :, :], v2, g4c)
        tt_(v2[:, :], v2[:, :], v1[:, :], ALU.subtract).then_inc(s("gapin"), 1)
        for E_, o_ in ((E1, o1), (E2, o2)):
            o(tt_(e44(E_), gh4, o_[:, :, :].unsqueeze(2).broadcast_to([P, NT, NG, EPG]), ALU.mult))
        tt_(M[:, :, :], E1[:, :, :], E2[:, :, :], ALU.add).then_inc(s("rM"), 1)
        dve.wait_ge(s("gexp"), 1)
        o(v.tensor_reduce(gsum[:, :], g4b[:, :, :], AX.X, ALU.add))
        dve.wait_ge(s("gapexp"), 1)
        o(ts_(w1[:, :], w2[:, :], 1.0, None, ALU.add))
        o(tt_(w1[:, :], w1[:, :], gsum[:, :], ALU.mult))
        o(v.reciprocal(w1[:, :], w1[:, :]))
        o(tt_(w2[:, :], w2[:, :], w1[:, :], ALU.mult))
        dve.wait_ge(s("posp"), 1)
        o(v.tensor_copy(pos[:, :, :], ps[:, 0, 0:NT * NE].rearrange("p (j e) -> p j e", j=NT)))
        o(v.tensor_copy(cnt[:, :], ps[:, 1, 0:NE]))
        o(ts_(nx[:, :], cnt[:, :], float(P), None, ALU.is_gt))
        for i in range(2, -(-NTOK // P)):
            o(stt(out=nx[:, :], in0=cnt[:, :], scalar=float(P * i), in1=nx[:, :], op0=ALU.is_gt, op1=ALU.add))
        o(v.tensor_tensor_scan(xb[:, :], cst("ones")[:, 0:NE], nx[:, :], 0.0, ALU.mult, ALU.add))
        o(tt_(xb[:, :], xb[:, :], nx[:, :], ALU.subtract))
        be = lambda a: a[:, :].unsqueeze(1).broadcast_to([P, EXTRA, NE])
        jb = cst("jidx").unsqueeze(2).broadcast_to([P, EXTRA, NE])
        o(tt_(eid8[:, :, :], be(xb), jb, ALU.subtract))
        o(tt_(eid9[:, :, :], eid8[:, :, :], be(nx), ALU.add))
        o(ts_(eid9[:, :, :], eid9[:, :, :], 0.0, None, ALU.is_gt))
        o(stt(out=eid9[:, :, :], in0=eid8[:, :, :], scalar=0.0, in1=eid9[:, :, :], op0=ALU.is_le, op1=ALU.mult))
        o(tt_(eid9[:, :, :], eid9[:, :, :], be(cst("eidx")), ALU.mult))
        o(v.tensor_reduce(eid[:, :], eid9[:, :, :], AX.X, ALU.add))
        o(v.tensor_copy(eidi[:, :], eid[:, :]))
        o(v.tensor_reduce(xtot[:, :], nx[:, :], AX.X, ALU.add))
        o(ts_(eid[:, 0:EXTRA // 2], cst("jidx")[:, 0:EXTRA:2], xtot[:, 0:1], None, ALU.is_lt))
        o(v.tensor_reduce(xtot[:, :], eid[:, 0:EXTRA // 2], AX.X, ALU.add))
        v.tensor_copy(npair[:, :], xtot[:, :]).then_inc(s("eid"), 1)
        o(stt(out=nx2[:, :], in0=xb[:, :], scalar=float(P), in1=cst("exbase"), op0=ALU.mult, op1=ALU.add))
        bj = lambda a: a[:, :].unsqueeze(1).broadcast_to([P, NT, NE])
        o(ts_(slot[:, :, :], pos[:, :, :], float(P), None, ALU.is_ge))
        o(tt_(slot[:, :, :], slot[:, :, :], bj(nx2), ALU.mult))
        o(tt_(slot[:, :, :], slot[:, :, :], pos[:, :, :], ALU.add))
        o(tt_(slot[:, :, :], slot[:, :, :], bj(cst("ebase")), ALU.add))
        tbb = cst("tbase").unsqueeze(1).broadcast_to([P, NT, NTILE])
        bt_ = lambda a: a[:, :].unsqueeze(2).broadcast_to([P, NT, NTILE])
        for k, E_ in enumerate((E1, E2)):
            o(tt_(e16[:, :, :], E_[:, :, :], slot[:, :, :], ALU.mult))
            o(v.tensor_reduce(sl[k][:, :], e16[:, :, :], AX.X, ALU.add))
            o(v.tensor_copy(sidx[:, k, :], sl[k][:, :]))
            o(tt_(td[:, :, :], tbb, bt_(sl[k]), ALU.subtract))
            o(ts_(tm[:, :, :], td[:, :, :], -float(P), None, ALU.is_gt))
            o(stt(out=tt[k][:, :, :], in0=td[:, :, :], scalar=0.0, in1=tm[:, :, :], op0=ALU.is_le, op1=ALU.mult))
            o(tt_(tm[:, :, :], tt[k][:, :, :], td[:, :, :], ALU.mult))
            o(v.tensor_reduce(ms[k][:, :], tm[:, :, :], AX.X, ALU.add))
            o(ts_(ms[k][:, :], ms[k][:, :], -1.0, None, ALU.mult))
            o(tt_(slot1h[:, k, :, :], cst("iota").unsqueeze(1).broadcast_to([P, NT, P]),
                  ms[k][:, :].unsqueeze(2).broadcast_to([P, NT, P]), ALU.is_equal))
            o(tt_(tt[k][:, :, :], tt[k][:, :, :], bt_(cst("tokid")), ALU.mult))
            ins = tt_(tt[k][:, :, :], tt[k][:, :, :], bt_(cst("valid")), ALU.mult)
            ins.then_inc(s("oneh"), 1)
        dve.wait_ge(s("idxp"), 1)
        v.tensor_copy(gidx[:, :], ps[:, 2, 0:NTILE]).then_inc(s("gidx"), 1)

        def rows(t, u):
            dve.wait_ge(s("xgp"), t + 1)
            v.tensor_copy(xgT[:, u, 4:8, :], ps[:, 5, :].rearrange("p (a b) -> p a b", a=4)).then_inc(s("xgd"), 1)

        def hidden(t, u):
            dve.wait_ge(s("eth"), t + 1)
            stt(out=a_s[:, u, :], in0=a_t[:, u, :], scalar=1.0, in1=ps[:, u, :], op0=ALU.add, op1=ALU.mult)\
                .then_inc(s("esilu"), 1)
            dve.wait_ge(s("esilu"), t + 1)
            dve.wait_ge(s("eup"), t + 1)
            stt(out=a_t[:, u, :], in0=a_s[:, u, :], scalar=0.5, in1=ps[:, 2 + u, :], op0=ALU.mult, op1=ALU.mult)\
                .then_inc(s("ahid"), 1)

        def finish(t, u, wait_store):
            dve.wait_ge(s("ey"), t + 1)
            if wait_store is not None:
                dve.wait_ge(s_yst[u], wait_store)
            v.tensor_copy(ysb[:, u, 512:1024], ps[:, 7, :]).then_inc(s("eyd"), 1)

        rows(0, 0)
        hidden(0, 0)
        rows(1, 1)
        for t in (1, 2):
            u = t % 2
            hidden(t, u)
            rows(t + 1, 1 - u)
            finish(t - 1, 1 - u, None)
        with dve.Fori(1, NE // 2 - 1) as i:
            for u in (1, 0):
                hidden(2 * i + (2 - u), u)
                rows(2 * i + (3 - u), 1 - u)
                finish(2 * i + (1 - u), 1 - u, 16 * i)
        hidden(NE - 1, 1)
        finish(NE - 2, 0, 16 * (NE // 2 - 1))
        finish(NE - 1, 1, 16 * (NE // 2 - 1))
        dve.wait_ge(s("eid"), 1)
        pairs = dve.value_load(npair[0:1, 0:1], min_val=0, max_val=EXTRA // 2)
        with dve.Fori(0, EXTRA // 2) as i:
            with dve.If(pairs > i):
                for u in range(2):
                    rows(2 * i + (NE + u), u)
                    if u:
                        hidden(2 * i + NE, 0)
                hidden(2 * i + (NE + 1), 1)
                for u in range(2):
                    finish(2 * i + (NE + u), u, 16 * i + 16 * (NE // 2))

        for n in range(NT + 2):
            if n < NT:
                j, w = n, TW[n]
                dve.wait_ge(s("yw"), j + 1)
                a, b = yg[0:w, j, 0, :], yg[0:w, j, 1, :]
                stt(out=a, in0=b, scalar=w2[0:w, j:j + 1], in1=a, op0=ALU.mult, op1=ALU.add).then_inc(s("ysum"), 1)
            if 1 <= n <= NT:
                j, w = n - 1, TW[n - 1]
                dve.wait_ge(s("ygate"), j + 1)
                tt_(x2[0:w, j, :], x2[0:w, j, :], yg[0:w, j, 0, :], ALU.add).then_inc(s("x3"), 1)
            if n >= 2:
                j, w = n - 2, TW[n - 2]
                rstd(j, w, D, 3 * NT + j + 1)
                if j >= 2:
                    dve.wait_ge(s_fst[j % 2], 16 * (j // 2))
                stt(out=fo[0:w, j % 2, :], in0=x2[0:w, j, :], scalar=stat[0:w, 56 + j:57 + j], in1=fgain[0:w, :],
                    op0=ALU.mult, op1=ALU.mult).then_inc(s("fo"), 1)

    @block.tensor
    def _(pe):
        t_ = nc.tensor
        mm = t_.matmul
        ident = cst("ident")

        def tr(out, in_):
            n = in_.shape[0]
            return mm(out, lhsT=in_, rhs=ident[0:n, 0:n], start=True, stop=True, is_transpose=True)

        pe.wait_ge(s("init"), 160)
        mm(ps[0:HEADS, 6, :], ctab33[:, :], ohp[:, 0:512], start=True, stop=True)
        mm(ps[0:HEADS, 7, 0:128], ctab33[:, :], ohp[:, 512:640], start=True, stop=True).then_inc(s("gp"), 1)

        pe.wait_ge(s("cs"), 1)
        for c in range(N_ADA):
            if c >= 2:
                pe.wait_ge(s("adae"), c - 1)
            out = ps[0:NC, c % 2, :]
            mm(out, cst("ones", 1)[:, 0:NC], adab[:, 512 * c:512 * (c + 1)], start=True, stop=False)
            wait_item(pe, IT_ADA + c)
            r = ring[(IT_ADA + c) % R1]
            for k in range(KD):
                ins = mm(out, cS[:, k, :], r[:, 512 * k:512 * (k + 1)], start=False, stop=k == KD - 1)
            ins.then_inc(s("ada"), 1)
            if c == 3:
                pe.wait_ge(s("bpad"), 1)
                for n in range(8):
                    b, q = n // 4, n % 4
                    if n >= 2:
                        pe.wait_ge(s("btTe"), n - 1)
                    for r_ in range(4):
                        ins = tr(ps[:, 2 + n % 2, P * r_:P * (r_ + 1)], bpad[b][:, 4 * q + r_, :])
                    ins.then_inc(s("btT"), 1)
        pe.wait_ge(s("btTe"), 8)

        for j in range(NT):
            w = TW[j]
            pe.wait_ge(s("h"), j + 1)
            if j >= 2:
                pe.wait_ge(s("hTa"), j - 1)
                pe.wait_ge(s("hTd"), j - 1)
            for half in range(2):
                for c in range(4):
                    k = 4 * half + c
                    ins = tr(ps[:, 2 + 2 * (j % 2) + half, w * c:w * (c + 1)], hb[0:w, j % 2, P * k:P * (k + 1)])
                ins.then_inc(s("hTp"), 1)

        pe.wait_ge(s("hTa"), NT)
        pe.wait_ge(s("hTd"), NT)
        pe.wait_ge(s("adae"), N_ADA)
        pe.wait_ge(s("gsb"), 1)
        pe.wait_ge(s("sq"), NT)
        zi = 0
        for it in range(N_WIN):
            i = IT_WIN + it
            wait_item(pe, i)
            r = ring[i % R1]
            if it == 2:
                for j in range(NT):
                    w = TW[j]
                    if j >= 2:
                        pe.wait_ge(s("ve"), j - 1)
                    for k in range(KD):
                        ins = mm(ps[0:w, 2 + j % 2, :], hT[:, k, tok(j)], r[:, 512 * k:512 * (k + 1)],
                                 start=k == 0, stop=k == KD - 1)
                    ins.then_inc(s("v"), 1)
                continue
            for c in range(4):
                if zi >= 2:
                    pe.wait_ge(s("za"), zi - 1)
                    pe.wait_ge(s("zd"), zi - 1)
                for n, (out, cols) in enumerate(((ps[:, zi % 2, :], slice(0, SEQ)),
                                                 (ps[:, 6 + zi % 2, 0:NS], slice(SEQ, NTOK)))):
                    for k in range(KD):
                        ins = mm(out, r[:, 512 * k + P * c:512 * k + P * (c + 1)], hT[:, k, cols],
                                 start=k == 0, stop=k == KD - 1)
                    ins.then_inc(s("z"), 1)
                zi += 1

        wait_item(pe, IT_OH)
        pe.wait_ge(s("padt"), 1)
        pe.wait_ge(s("ve"), NT)
        r = ring[IT_OH % R1]
        for b, (c0, c1) in enumerate(((0, 512), (512, DK))):
            for t in range(TDEC):
                ins = mm(ps[:, 2 + b, 0:c1 - c0], padT[:, t, :], r[0:BUCKETS + 1, DK * t + c0:DK * t + c1],
                         start=t == 0, stop=t == TDEC - 1)
        ins.then_inc(s("dbp"), 1)

        NST = HEADS * QT
        pe.wait_ge(s("za"), 12)
        pe.wait_ge(s("zd"), 12)
        pe.wait_ge(s("dbias"), 1)

        def scores(st):
            h, qt = divmod(st, QT)
            rows = slice(64 * (h % 2), 64 * (h % 2) + 64)
            if st >= 2:
                pe.wait_ge(s("P"), st - 1)
            m = P * (qt + 1)
            mm(ps[:, st % 2, 0:m], qkT[rows, h // 2, P * qt:m], qkT[rows, 4 + h // 2, 0:m], start=True, stop=False)
            pe.wait_ge(s_toep[h % 2], 16 * (h // 2 + 1))
            mm(ps[:, st % 2, 0:m], cst("flip"), toep[:, h % 2, SEQ - m:SEQ], start=False, stop=True)\
                .then_inc(s("S"), 1)

        def probs_t(st):
            qt = st % QT
            pe.wait_ge(s("P"), st + 1)
            if st >= 2:
                pe.wait_ge(s("ptr"), st - 1)
            for kt in range(qt + 1):
                ins = tr(ps[:, 2 + st % 2, P * kt:P * (kt + 1)], Sb[:, st % 2, P * kt:P * (kt + 1)])
            ins.then_inc(s("pt"), 1)

        def pv(st):
            h, qt = divmod(st, QT)
            pe.wait_ge(s("ptr"), st + 1)
            for kt in range(qt + 1):
                ins = mm(ps[:, 4 + qt, DH * h:DH * (h + 1)], PTs[:, st % 2, P * kt:P * (kt + 1)],
                         vrow[:, kt, DH * h:DH * (h + 1)], start=kt == 0, stop=kt == qt)
            ins.then_inc(s("pv"), 1)

        for st in range(NST + 2):
            if st < NST:
                scores(st)
            if 1 <= st <= NST:
                probs_t(st - 1)
            if st >= 2:
                pv(st - 2)

        def att_t(j):
            w = TW[j]
            pe.wait_ge(s("attn"), j + 1)
            if j >= 2:
                pe.wait_ge(s("attTe"), j - 1)
            for c in range(4):
                ins = tr(ps[:, 1 + j % 2, w * c:w * (c + 1)], att[0:w, j, P * c:P * (c + 1)])
            ins.then_inc(s("attT"), 1)

        for j in range(QT):
            att_t(j)
        pe.wait_ge(s("attTe"), QT)

        pe.wait_ge(s("qbd"), 1)
        pe.wait_ge(s("glul"), 32)
        pe.wait_ge(s("att"), NST)

        def dec_item(m):
            g, c = divmod(m, 8)
            n4 = c % 4
            n = 4 * g + n4
            rows = slice(32 * n4, 32 * n4 + 32)
            wait_item(pe, IT_KV + m)
            r = ring[(IT_KV + m) % R1]
            if c < 4:
                if c == 0 and g:
                    pe.wait_ge(s("dSm"), g)
                for out, c0, c1 in ((ps[rows, 0, :], 0, 512), (ps[rows, 1, 0:CK - 512], 512, CK)):
                    for q in range(4):
                        mm(out, qbd[:, n, q, :], r[:, CK * q + c0:CK * q + c1], start=q == 0, stop=q == 3,
                           tile_position=(0, 32 * n4))
                for q in range(4):
                    ins = mm(ps[rows, 1, CK - 512:DK - 512], qbd[:, n, q, :], qkT[:, 4 + q, SEQ:NTOK],
                             start=q == 0, stop=q == 3, tile_position=(0, 32 * n4))
                ins.then_inc(s("dS"), 1)
            else:
                if c == 4:
                    pe.wait_ge(s("dPtd"), g + 1)
                    pe.wait_ge(s("dPta"), g + 1)
                    if g:
                        pe.wait_ge(s("dOe"), g)
                for b in range(CB):
                    mm(ps[rows, 4, :], dPT[:, b, rows], r[:, AW * b:AW * (b + 1)], start=b == 0, stop=False,
                       tile_position=(0, 32 * n4))
                mm(ps[rows, 4, :], dPT[0:NS, CB, rows], vrow[0:NS, QT, :], start=False, stop=True,
                   tile_position=(0, 32 * n4)).then_inc(s("dOp"), 1)

        def dec_probs_t(g):
            pe.wait_ge(s("dP"), g + 1)
            for b in range(CB):
                tr(ps[:, 2 + b // 4, P * (b % 4):P * (b % 4 + 1)], dP[:, P * b:P * (b + 1)])
            tr(ps[0:NS, 3, 3 * P:4 * P], dP[:, CK:DK]).then_inc(s("dPt"), 1)

        def s5_in(i):
            k, q = divmod(i, 4)
            if i >= 1:
                pe.wait_ge(s("buread"), i)
            if i % 4 == 0 and i:
                pe.wait_ge(s("gluo"), i // 4)
            for n in range(2):
                for r_ in range(4):
                    ins = mm(ps[:, 5 + n, CH * r_:CH * (r_ + 1)], bt[n][:, 4 * q + r_, :],
                             uT[:, q, CH * k:CH * (k + 1)], start=True, stop=True)
            ins.then_inc(s("bu"), 1)

        def s5_out(i):
            k, q = divmod(i, 4)
            pe.wait_ge(s("hout"), i + 1)
            if q == 0 and k:
                pe.wait_ge(s("yread"), k)
            for r_ in range(4):
                for n, a in enumerate((hr, hi)):
                    ins = mm(ps[32 * r_:32 * r_ + 32, 7, CH * q:CH * (q + 1)], ct[n][:, 4 * q + r_, :], a[:, r_, :],
                             start=n == 0, stop=n == 1, tile_position=(0, 32 * r_))
            ins.then_inc(s("yp"), 1)

        def s5_glu(n, w):
            pe.wait_ge(s("gel"), n + 1)
            for a in range(2):
                for q in range(4):
                    ins = mm(ps[:, 5 + a, w * q:w * (q + 1)], glu[:, a, q, :], y2[:, q, 0:w], start=True, stop=True)
            ins.then_inc(s("glut"), 1)
            pe.wait_ge(s("gsq"), n + 1)
            for q in range(4):
                ins = mm(ps[0:w, 5, 0:1], yd[:, q, 0:w], cst("ones")[:, 0:1], start=q == 0, stop=q == 3)
            ins.then_inc(s("ssp"), 1)

        for i in range(16):
            dec_item(i)
            if i:
                s5_out(i - 1)
                if i % 4 == 0:
                    s5_glu(i // 4 - 1, CH)
            s5_in(i)
            if i in (3, 11):
                dec_probs_t(i // 8)
        s5_out(15)
        s5_glu(QT - 1, CH)
        pe.wait_ge(s("gluo"), QT)
        for n in range(2):
            for t in range(STT):
                ins = mm(ps[:, 5 + n, NS * t:NS * (t + 1)], bt[n][:, t, :], uT[:, t // 4, SEQ:NTOK],
                         start=True, stop=True)
        ins.then_inc(s("bu"), 1)
        pe.wait_ge(s("dOe"), 2)
        for g in range(2):
            ins = mm(ps[0:NS, 4, :], cst("toksel")[:, NS * g:NS * (g + 1)], dO[:, g, :], start=g == 0, stop=g == 1)
        ins.then_inc(s("attSp"), 1)
        pe.wait_ge(s("hout"), 17)
        pe.wait_ge(s("yread"), QT)
        hs = [a[:, :, :].rearrange("p a b -> p (a b)") for a in (hr, hi)]
        for t in range(STT):
            r_, q = t % 4, t // 4
            for n in range(2):
                ins = mm(ps[32 * r_:32 * r_ + 32, 7, NS * q:NS * (q + 1)], ct[n][:, t, :], hs[n][:, NS * t:NS * (t + 1)],
                         start=n == 0, stop=n == 1, tile_position=(0, 32 * r_))
        ins.then_inc(s("yp"), 1)
        s5_glu(QT, NS)
        att_t(QT)

        pe.wait_ge(s("attTe"), NT)
        pe.wait_ge(s("gluo"), NT)
        wait_item(pe, IT_WO)
        wait_item(pe, IT_WO + 1)

        def h2_t(j):
            w = TW[j]
            pe.wait_ge(s("h"), NT + j + 1)
            if j:
                pe.wait_ge(s("hTa"), NT + j)
                pe.wait_ge(s("hTd"), NT + j)
            for half in range(2):
                for c in range(4):
                    k = 4 * half + c
                    ins = tr(ps[:, 6 + half, w * c:w * (c + 1)], h2[0:w, j % 2, P * k:P * (k + 1)])
                ins.then_inc(s("hTp"), 1)

        def logits(j):
            w = TW[j]
            pe.wait_ge(s("hTa"), NT + j + 1)
            pe.wait_ge(s("hTd"), NT + j + 1)
            out = ps[0:w, 4, 20 * j:20 * j + 20]
            mm(out, cst("ones", 1)[:, 0:w], rb[:, :], start=True, stop=False)
            for k in range(KD):
                ins = mm(out, h2T[:, k, tok(j)], rw[:, k, :], start=False, stop=k == KD - 1)
            ins.then_inc(s("lg"), 1)

        pe.wait_ge(s("mod3"), 112)
        for j in range(NT):
            w = TW[j]
            for half, (left, made_) in enumerate(((s("woa"), s("woA")), (s("wog"), s("woS")))):
                if j:
                    pe.wait_ge(left, j)
                for n in range(2):
                    r = ring[(IT_WO + n) % R1]
                    for k in range(4 * half, 4 * half + 4):
                        ins = mm(ps[0:w, 2 * half + n, :], mixT[:, k, tok(j)], r[:, 512 * k:512 * (k + 1)],
                                 start=k % 4 == 0, stop=k % 4 == 3)
                ins.then_inc(made_, 1)
            if j:
                h2_t(j - 1)
                logits(j - 1)
        h2_t(NT - 1)
        logits(NT - 1)

        pe.wait_ge(s("rM"), 1)
        for j in range(NT):
            for j2 in range(j + 1):
                mm(ps[:, 0, NE * j:NE * (j + 1)], cst("tri") if j2 == j else cst("ones"), M[:, j2, :],
                   start=j2 == 0, stop=j2 == j)
        for j in range(NT):
            ins = mm(ps[:, 1, 0:NE], cst("ones"), M[:, j, :], start=j == 0, stop=j == NT - 1)
        ins.then_inc(s("posp"), 1)
        pe.wait_ge(s("oneh"), 2)
        for k in range(2):
            for j in range(NT):
                ins = mm(ps[:, 2, 0:NTILE], slot1h[:, k, j, :], tt[k][:, j, :], start=k + j == 0,
                         stop=(k, j) == (1, NT - 1))
        ins.then_inc(s("idxp"), 1)

        def rows_t(t, u, wait_gather):
            pe.wait_ge(s_xg[u], wait_gather)
            for c in range(KD):
                ins = tr(ps[:, 4 + c // 4, P * (c % 4):P * (c % 4 + 1)], xg[:, u, P * c:P * (c + 1)])
            ins.then_inc(s("xgp"), 1)

        def weights(w, u, turn):
            pe.wait_ge(efull[3 * u + w], 16 * turn)
            return ering[3 * u + w]

        def half_in(t, u, w, turn, old=True):
            if w == 0:
                pe.wait_ge(s("xga"), t + 1)
                pe.wait_ge(s("xgd"), t + 1)
                if old:
                    pe.wait_ge(s("aTe"), t - 1)
            r = weights(w, u, turn)
            for k in range(KD):
                ins = mm(ps[:, 2 * w + u, :], xgT[:, u, k, :], r[:, 512 * k:512 * (k + 1)],
                         start=k == 0, stop=k == KD - 1)
            ins.then_inc(s("egate") if w == 0 else s("eup"), 1)

        def hidden_t(t, u):
            pe.wait_ge(s("ahid"), t + 1)
            for c in range(4):
                ins = tr(ps[:, u, P * c:P * (c + 1)], a_t[:, u, P * c:P * (c + 1)])
            ins.then_inc(s("aTp"), 1)

        def down(t, u, turn, old=True):
            pe.wait_ge(s("aTe"), t + 1)
            if old:
                pe.wait_ge(s("eya"), t)
                pe.wait_ge(s("eyd"), t)
            r = weights(2, u, turn)
            for n in range(2):
                for c in range(4):
                    ins = mm(ps[:, 6 + n, :], aT[:, u, c, :], r[:, D * c + 512 * n:D * c + 512 * (n + 1)],
                             start=c == 0, stop=c == 3)
            ins.then_inc(s("ey"), 1)

        pe.wait_ge(s("gidx"), 1)
        rows_t(0, 0, 16)
        half_in(0, 0, 0, 1, old=False)
        half_in(0, 0, 1, 1)
        rows_t(1, 1, 16)
        for t in (1, 2):
            u = t % 2
            half_in(t, u, 0, 1 + t // 2, old=t >= 2)
            hidden_t(t - 1, 1 - u)
            half_in(t, u, 1, 1 + t // 2)
            rows_t(t + 1, 1 - u, 32)
            down(t - 1, 1 - u, 1, old=t >= 2)
        with pe.Fori(1, NE // 2 - 1) as i:
            for u in (1, 0):
                t = 2 * i + (2 - u)
                half_in(t, u, 0, i + (2 - u))
                hidden_t(2 * i + (1 - u), 1 - u)
                half_in(t, u, 1, i + (2 - u))
                rows_t(2 * i + (3 - u), 1 - u, 16 * i + 32)
                down(2 * i + (1 - u), 1 - u, i + 1)
        half_in(NE - 1, 1, 0, NE // 2)
        hidden_t(NE - 2, 0)
        half_in(NE - 1, 1, 1, NE // 2)
        down(NE - 2, 0, NE // 2)
        hidden_t(NE - 1, 1)
        down(NE - 1, 1, NE // 2)
        pe.wait_ge(s("eid"), 1)
        pairs = pe.value_load(npair[0:1, 0:1], min_val=0, max_val=EXTRA // 2)
        with pe.Fori(0, EXTRA // 2) as i:
            with pe.If(pairs > i):
                t, turn = 2 * i + NE, i + (NE // 2 + 1)
                rows_t(t, 0, 16 * i + 16 * (NE // 2 + 1))
                half_in(t, 0, 0, turn)
                half_in(t, 0, 1, turn)
                rows_t(t + 1, 1, 16 * i + 16 * (NE // 2 + 1))
                half_in(t + 1, 1, 0, turn)
                hidden_t(t, 0)
                half_in(t + 1, 1, 1, turn)
                down(t, 0, turn)
                hidden_t(t + 1, 1)
                down(t + 1, 1, turn)


def kernel(**inputs):
    import concourse.bacc as bacc
    from concourse.bass_utils import run_bass_kernel_spmd

    x = {k: np.asarray(v) for k, v in inputs.items()}
    nc = bacc.Bacc("TRN2", target_bir_lowering=False, num_devices=1)

    def state(a):
        return np.ascontiguousarray(a.reshape((STT, P) + a.shape[2:]).swapaxes(0, 1))

    def channel(a):
        return np.ascontiguousarray(a.reshape(4, P).T)

    def blocks(a, n):
        g, r, c = a.shape
        out = np.zeros((g // n, n, r, n, c), a.dtype)
        for i in range(n):
            out[:, i, :, i, :] = a.reshape(g // n, n, r, c)[:, i]
        return out.reshape(g // n, n * r, n * c)

    c_all = np.concatenate([x["c_prompt"], x["c_sample"]])
    par = [state(x["ssm_a_re"][0]), state(x["ssm_a_im"][0]),
           state(np.broadcast_to(x["ssm_log_dt"][0][:, None], (GRP, ST))),
           channel(x["ssm_d"][0].reshape(-1)), channel(x["attn_out_g"][0]), channel(x["ssm_out_g"][0]),
           state(x["ssm_b_re"][0]).reshape(P, -1), state(x["ssm_b_im"][0]).reshape(P, -1)]
    ck = x["cache_k"][0][:, CROWS]
    cv = x["cache_v"][0][:, CROWS]
    A = {
        "zero": np.zeros(D, np.float32),
        "const": CONST,
        "par": np.concatenate(par, axis=1),
        "cT": c_all.reshape(NC, KD, P).transpose(2, 1, 0),
        "tab33": np.concatenate([x["rel_bias"], np.ones((1, HEADS), np.float32)]),
        "oh_prompt": OH_PROMPT, "oh_decode": OH_DECODE,
        "ct_re": blocks(x["ssm_c_re"][0].transpose(0, 2, 1), 2).transpose(1, 0, 2),
        "ct_im": blocks(x["ssm_c_im"][0].transpose(0, 2, 1), 2).transpose(1, 0, 2),
        "glu_a": blocks(x["glu_a"][0], 8).transpose(1, 0, 2),
        "glu_b": blocks(x["glu_b"][0], 8).transpose(1, 0, 2),
        "ada_w": x["ada_w"][0], "ada_b": x["ada_b"],
        "norm1_g": x["norm1_g"][0], "norm2_g": x["norm2_g"][0], "final_g": x["final_norm_g"],
        "w_in": x["w_in"][0], "w_out": x["w_out"][0],
        "x": np.concatenate([x["x_prompt"][0], x["x_sample"].reshape(NS, D)]),
        "cache_k": ck.reshape(NSEQ, CK, 4, P).transpose(0, 3, 2, 1).reshape(NSEQ, P, 4 * CK),
        "cache_v": cv.reshape(NSEQ, CB, P, AW).transpose(0, 2, 1, 3).reshape(NSEQ, P, CB * AW),
        "h0_re": state(x["state_ssm_re"][0].transpose(1, 2, 0)), "h0_im": state(x["state_ssm_im"][0].transpose(1, 2, 0)),
        "router_w": np.concatenate([x["router_g_w"][0], x["router_e_w"][0].transpose(1, 0, 2).reshape(D, NE)], axis=1)
        .reshape(KD, P, NG + NE).transpose(1, 0, 2),
        "router_b": np.concatenate([x["router_g_b"][0], x["router_e_b"][0].reshape(-1)])[None, :],
        "w_gate": x["w_gate"][0].reshape(NE, D, FE), "w_up": x["w_up"][0].reshape(NE, D, FE),
        "w_down": x["w_down"][0].reshape(NE, FE, D),
    }
    A = {k: np.ascontiguousarray(a) for k, a in A.items()}
    I = {k: nc.dram_tensor("in_" + k, a.shape, mybir.dt.from_np(a.dtype), kind="ExternalInput").ap()
         for k, a in A.items()}
    shapes = {"y": (NTOK, D), "kT": (AW, NTOK), "v": (NTOK, AW), "ssm_p": (P, 2, STT), "ssm_s": (P, 2 * STT * NSEQ)}
    O = {k: nc.dram_tensor("out_" + k, shp, F32, kind="ExternalOutput").ap() for k, shp in shapes.items()}
    build(nc, I, O)
    r = run_bass_kernel_spmd(nc, [{"in_" + k: a for k, a in A.items()}], core_ids=[0]).results[0]
    y, kT, v, sp, ss = (np.asarray(r["out_" + k]) for k in ("y", "kT", "v", "ssm_p", "ssm_s"))
    k = kT.T
    heads = lambda a, lead: np.ascontiguousarray(a.reshape(lead + (HEADS, DH)))
    sp = sp.transpose(1, 2, 0).reshape(2, 1, 1, GRP, ST)
    ss = ss.reshape(P, 2, STT, NSEQ).transpose(1, 3, 2, 0).reshape(2, 1, NSEQ, GRP, ST)
    c = np.ascontiguousarray
    return (c(y[:SEQ].reshape(1, SEQ, D)), c(y[SEQ:].reshape(NSEQ, TDEC, D)),
            heads(k[:SEQ], (1, 1, SEQ)), heads(v[:SEQ], (1, 1, SEQ)),
            heads(k[SEQ:], (1, NSEQ, TDEC)), heads(v[SEQ:], (1, NSEQ, TDEC)),
            c(sp[0]), c(sp[1]), c(ss[0]), c(ss[1]))
```

```python
from contextlib import ExitStack

import numpy as np

import concourse.bass as bass
from concourse import mybir

F32 = mybir.dt.float32
U32 = mybir.dt.uint32
I32 = mybir.dt.int32
ALU = mybir.AluOpType
ACT = mybir.ActivationFunctionType
AX = mybir.AxisListType

P = 128
D = 1024
KD = D // P
SEQ = 512
NSEQ, TDEC = 8, 4
NS = NSEQ * TDEC
NTOK = SEQ + NS
HALF = NTOK // 2
TW = [P] * (SEQ // P) + [NS]
NT = len(TW)
QT = SEQ // P
HEADS, DH = 8, 64
AW = HEADS * DH
NC = NSEQ + 1
PAST = 2048
WINDOWS, DILATIONS = (128, 512, 2048), (1, 4, 16)
BUCKETS, MAX_EXACT = 32, 16
GRP, GC, ST = 32, 16, 64
STT = GRP * ST // P
CH = 128
NG, EPG = 4, 4
NE = NG * EPG
FE = 512
EPS = 1e-6
EXTRA = 8
NTILE = NE + EXTRA
NEG = -1.0e30

CROWS = [r for r in range(PAST) if r >= PAST - WINDOWS[1] or r % DILATIONS[2] < TDEC]
CK = len(CROWS)
CB = CK // P
DK = CK + NS
SLOT = 4096
R1 = 4
R2 = 6
N_ADA, N_WIN = 12, 4
IT_ADA, IT_WIN = 0, N_ADA
IT_OH = IT_WIN + N_WIN
IT_KV = IT_OH + 1
IT_WO = IT_KV + 2 * NSEQ
N_ITEMS = IT_WO + 2


def _bucket(dist):
    d = np.maximum(dist, MAX_EXACT).astype(np.float32)
    log_part = MAX_EXACT + (np.log(d / np.float32(MAX_EXACT)) / np.float32(np.log(PAST / MAX_EXACT))
                            * np.float32(BUCKETS - MAX_EXACT)).astype(np.int32)
    return np.where(dist < MAX_EXACT, dist, np.minimum(log_part, BUCKETS - 1))


def _distance_rows(dist):
    n = np.zeros(dist.shape, np.int64)
    for w, r in zip(WINDOWS, DILATIONS):
        n += (dist >= 0) & (dist <= w) & (dist % r == 0)
    out = np.zeros((BUCKETS + 1,) + dist.shape, np.float32)
    b = _bucket(np.maximum(dist, 0))
    for i in range(BUCKETS):
        out[i] = (b == i) & (n > 0)
    out[BUCKETS] = np.where(n > 0, np.log(np.maximum(n, 1)), NEG)
    return out


def _constants():
    p = np.arange(P)
    blocks = {}
    blocks["ident"] = np.eye(P)
    blocks["flip"] = np.eye(P)[::-1]
    blocks["tri"] = (p[:, None] < p[None, :])
    blocks["ones"] = np.ones((P, P))
    blocks["iota"] = np.broadcast_to(np.arange(P), (P, P))
    head = (p % 32) // TDEC
    blocks["headsel"] = head[:, None] == (np.arange(AW) // DH)[None, :]
    nm = np.zeros((P, 2, NS))
    ts = np.zeros((P, 2, NS))
    for g in range(2):
        seq = 4 * g + p // 32
        tok = np.arange(NS)
        nm[:, g] = np.where(seq[:, None] == tok[None, :] // TDEC, 0.0, NEG)
        ts[:, g] = (seq * TDEC + p % TDEC)[:, None] == tok[None, :]
    blocks["newmask"] = nm.reshape(P, -1)
    blocks["toksel"] = ts.reshape(P, -1)
    blocks["tokid"] = p[:, None] + P * np.arange(NT)[None, :]
    blocks["valid"] = (p[:, None] < np.array(TW)[None, :])
    row = lambda a: np.broadcast_to(np.asarray(a).reshape(1, -1), (P, np.asarray(a).size))
    blocks["first"] = row([4, 3, 2, 1])
    blocks["ebase"] = row(np.arange(NE) * P)
    blocks["exbase"] = row((NE - 1 - np.arange(NE)) * P)
    blocks["eidx"] = row(np.arange(NE))
    blocks["jidx"] = row(np.arange(EXTRA))
    blocks["tbase"] = row(np.arange(NTILE) * P)
    cols, at = {}, 0
    for k, v in blocks.items():
        blocks[k] = np.asarray(v, np.float32)
        cols[k] = (at, at + blocks[k].shape[1])
        at += blocks[k].shape[1]
    return np.concatenate(list(blocks.values()), axis=1), cols


CONST, CCOL = _constants()
_dist0 = SEQ - 1 - np.arange(640)
OH_PROMPT = _distance_rows(_dist0)
_t = np.arange(TDEC)[:, None]
_cached = PAST + _t - np.array(CROWS)[None, :]
_new = np.broadcast_to(_t - (np.arange(NS) % TDEC)[None, :], (TDEC, NS))
OH_DECODE = _distance_rows(np.concatenate([_cached, _new], axis=1)).reshape(BUCKETS + 1, TDEC * DK)

PC = {}
_at = 0
for _k, _n in (("a_re", 16), ("a_im", 16), ("log_dt", 16), ("dskip", 4), ("attg", 4), ("ssmg", 4),
               ("b_re", 256), ("b_im", 256)):
    PC[_k] = (_at, _at + _n)
    _at += _n
NPAR = _at


class Order:

    def __init__(self, eng, sem, base=0):
        self.eng, self.sem, self.n = eng, sem, base

    def __call__(self, ins):
        ins.then_inc(self.sem, 1)
        self.n += 1
        self.eng.wait_ge(self.sem, self.n)


def build(nc, I, O):
    ctx = ExitStack()
    with ctx:
        _build(nc, I, O, ctx)


def _build(nc, I, O, ctx):
    B0 = 16512

    def at(name, shape, off, dt=F32):
        assert off % 32 == 0 and B0 + off + 4 * int(np.prod(shape[1:])) <= 229368, name
        return nc.alloc_sbuf_tensor_at(name, shape, dt, offset=B0 + off)

    def sem(name):
        return ctx.enter_context(nc.semaphore(name))

    RING, E, C, SM = 0, 65536, 98304, 98304 + 6656
    HT, QK, V, U = 106496, 123904, 141312, 151552
    TAB, W = 160256, 176640

    ring = [at(f"ring{i}", [P, SLOT], RING + 16384 * i) for i in range(R1)]
    bt = [at("bt_re", [P, STT, P], E), at("bt_im", [P, STT, P], E + 8192)]
    ct = [at("ct_re", [P, STT, 32], E + 16384), at("ct_im", [P, STT, 32], E + 18432)]
    s5_at = [[E + 20480 + 2048 * i for i in range(6)],
             [QK + 2048 * i for i in range(4)] + [V + 2048 * i for i in range(2)]]
    xr, xi, gr, gi, hr, hi = [[at(f"s5_{n}{b}", [P, 4, CH], s5_at[b][i]) for b in range(2)]
                              for i, n in enumerate(("xr", "xi", "gr", "gi", "hr", "hi"))]
    ering = [at(f"ering{i}", [P, SLOT], RING + 16384 * i) for i in range(R2)]

    NCC = CONST.shape[1]
    assert NCC * 4 <= 6656, NCC
    const = at("const", [P, NCC], C)

    def cst(name, rows=P):
        a, b = CCOL[name]
        return const[0:rows, a:b]

    sm_at = [SM]

    def small(name, cols, rows=P, dt=F32):
        t = at(name, [rows, cols], sm_at[0], dt)
        sm_at[0] += (4 * cols + 31) // 32 * 32
        assert sm_at[0] <= HT, name
        return t

    mag, cth, sth = small("mag", 16), small("cth", 16), small("sth", 16)
    ctab33 = small("tab33", 8, BUCKETS + 1)
    car, cai = small("carry_re", 16), small("carry_im", 16)
    las, lai = small("last_re", 16), small("last_im", 16)
    gains = small("gains", 12)
    ctmp = small("ctmp", 16)
    stat = small("stat", 64)
    dstat = small("dstat", 64)
    rssm = small("rssm", 8)
    nbias = small("nbias", 2 * NS)

    hT = at("hT", [P, KD, NTOK], HT)
    mixT = at("mixT", [P, KD, NTOK], HT)
    h2T = at("h2T", [P, KD, NTOK], HT)
    modsb = at("modsb", [NC, 2, 512], HT)
    ohp = at("oh_prompt", [BUCKETS + 1, 640], HT + 4096)
    gsb = at("gsb", [HEADS, 640], HT + 8192)
    toep = at("toeplitz", [P, 2, SEQ], HT)
    qkT = at("qkT", [P, 8, NTOK], QK)
    adab = at("adab", [1, 6 * D], QK)
    vrow = at("vrow", [P, NT, AW], V)
    uT = at("uT", [P, 4, NTOK], U)
    ngain = at("ngain", [NC, 2, D], U)
    cosT, sinT = at("cosT", [P, STT, CH], TAB), at("sinT", [P, STT, CH], TAB + 8192)

    xt = at("xt", [P, 2, D], W)
    hb = at("hb", [P, 2, D], W + 8192)
    par = at("par", [P, NPAR], W + 8192)
    bbr, bbi = at("bbr", [P, STT, GC], W + 8192 + 2304), at("bbi", [P, STT, GC], W + 8192 + 3328)
    bt1, bt2 = at("bt1", [P, STT, GC], W + 8192 + 4352), at("bt2", [P, STT, GC], W + 8192 + 5376)
    pr = at("pr", [P, 20, 16], W + 8192 + 6400)
    assert NPAR * 4 <= 2304 and 6400 + 1280 <= 8192
    modP, modS = at("modP", [P, 2, D], W + 16384), at("modS", [NS, 2, D], W + 24576)
    bpad = [at("bpad_re", [P, STT, P], W + 16384), at("bpad_im", [P, STT, P], W + 24576)]
    cT, cE, cS = [at(n, [P, KD, NC], W + 32768 + 288 * i) for i, n in enumerate(("cT", "cE", "cS"))]
    dt1, dt2 = at("dt1", [P, STT, CH // 2], W), at("dt2", [P, STT, CH // 2], W + 4096)

    att = at("att", [P, NT, AW], W)
    dPT = at("dPT", [P, 8, P], W)
    dO = at("dO", [P, 2, AW], W + 4096)
    Sb = at("Sb", [P, 2, SEQ], W + 10240)
    qbd = at("qbd", [P, NSEQ, 4, 32], W + 32000)
    PTs = at("PTs", [P, 2, SEQ], W + 14336)
    glu = at("glu", [P, 2, 4, P], W + 14336)
    dbias = at("dbias", [P, DK], W + 18432)
    dP = at("dP", [P, DK], W + 22144)
    th = at("gelu_th", [P, 4, CH], W + 25856)
    ta, tb = at("s5_ta", [P, 4, CH], W + 27904), at("s5_tb", [P, 4, CH], W + 29952)
    yd, y2 = at("gelu_yd", [P, 4, CH], W + 10240), at("gelu_y2", [P, 4, CH], W + 12288)
    states = at("sample_states", [P, 2 * STT * NSEQ], W + 22144)
    padT = at("padT", [BUCKETS + 1, 4, P], W + 27904)
    x2 = at("x2", [P, NT, D], QK)
    mod3P = at("mod3P", [P, 3, D], QK + 20480)
    mod3S = at("mod3S", [NS, 3, D], TAB)
    xt3 = at("xt3", [P, 2, D], W)
    h2 = at("h2", [P, 2, D], W + 8192)
    pt1, pt2 = at("pt1", [P, 2, D], W + 16384), at("pt2", [P, D], W + 24576)
    rw = at("rw", [P, KD, 20], W + 28672)
    rb = at("rb", [1, 20], W + 29312)
    rt_at = [TAB + 12288]

    def rt(name, shape, dt=F32):
        n = int(np.prod(shape[1:])) * 4
        if rt_at[0] <= W < rt_at[0] + n:
            rt_at[0] = W + 29440
        t = at(name, shape, rt_at[0], dt)
        rt_at[0] += (n + 31) // 32 * 32
        return t

    lg = rt("logits", [P, NT, 20])
    g4a, g4b, g4c = [rt(n, [P, NT, 4]) for n in ("g4a", "g4b", "g4c")]
    ghot = rt("ghot", [P, NT, 4])
    gmax, gsum = rt("gmax", [P, NT]), rt("gsum", [P, NT])
    e16 = rt("e16", [P, NT, NE])
    esel, o1, o2 = [rt(n, [P, NT, 4]) for n in ("esel", "o1", "o2")]
    v1, v2, w1, w2 = [rt(n, [P, NT]) for n in ("v1", "v2", "w1", "w2")]
    E1, E2, M = [rt(n, [P, NT, NE]) for n in ("E1", "E2", "M")]
    pos = rt("pos", [P, NT, NE])
    cnt, nx, xb, nx2 = [rt(n, [P, NE]) for n in ("cnt", "nx", "xb", "nx2")]
    slot = rt("slotrow", [P, NT, NE])
    sl = [rt("slot0", [P, NT]), rt("slot1", [P, NT])]
    ms = [rt("inslot0", [P, NT]), rt("inslot1", [P, NT])]
    td = rt("tile_dist", [P, NT, NTILE])
    tt = [rt("tile_tok0", [P, NT, NTILE]), rt("tile_tok1", [P, NT, NTILE])]
    tm = rt("tile_tmp", [P, NT, NTILE])
    slot1h = at("slot1h", [P, 2, NT, P], HT + 8192)
    gidx = rt("gidx", [P, NTILE], U32)
    sidx = rt("sidx", [P, 2, NT], U32)
    eid8, eid9 = rt("eid8", [P, EXTRA, NE]), rt("eid9", [P, EXTRA, NE])
    eid = rt("eid", [P, EXTRA])
    eidi = rt("eidi", [P, EXTRA], I32)
    xtot, npair = rt("extra_tiles", [P, 1]), rt("extra_pairs", [P, 1], I32)
    wk = [w1, w2]
    xg = at("xg", [P, 2, D], W)
    xgT = at("xgT", [P, 2, KD, P], W + 8192)
    a_s = at("a_s", [P, 2, FE], W + 16384)
    a_t = at("a_t", [P, 2, FE], W + 20480)
    aT = at("aT", [P, 2, 4, P], W + 24576)
    ysb = at("ysb", [P, 2, D], HT)
    fgain = at("fgain", [P, D], QK + 20480)
    yg = at("yg", [P, NT, 2, D], RING)
    fo = at("fo", [P, 2, D], W + 16384)

    ps = nc.alloc_psum_tensor("ps", [P, 8, 512], F32)

    mod_d = nc.dram_tensor("mod_d", [NC, 6 * D], F32).ap()
    g_d = nc.dram_tensor("g_d", [HEADS, 640], F32).ap()
    h2_d = nc.dram_tensor("h2_d", [NTOK, D], F32).ap()
    y_d = nc.dram_tensor("y_d", [NTILE * P, D], F32).ap()

    made = {}

    def s(name):
        if name not in made:
            made[name] = sem("s_" + name)
        return made[name]

    rfull = [sem(f"ring_full{i}") for i in range(R1)]
    efull = [sem(f"ering_full{i}") for i in range(R2)]
    s_x = [sem(f"x_full{i}") for i in range(2)]
    s_modst = [sem(f"mod_stored{i}") for i in range(2)]
    s_toep = [sem(f"toep_full{i}") for i in range(2)]
    s_x3 = [sem(f"x3_full{i}") for i in range(2)]
    s_xg = [sem(f"xg_full{i}") for i in range(2)]
    s_yst = [sem(f"y_stored{i}") for i in range(2)]
    s_yg = [sem(f"yg_full{j}") for j in range(NT)]
    s_fst = [sem(f"out_stored{i}") for i in range(2)]
    s_h2st = [sem(f"h2_stored{i}") for i in range(2)]

    def wait_item(eng, i):
        eng.wait_ge(rfull[i % R1], 16 * (i // R1 + 1))

    def used(eng, i):
        if i < IT_WIN:
            eng.wait_ge(s("ada"), i + 1)
        elif i < IT_OH:
            it = i - IT_WIN
            if it == 2:
                eng.wait_ge(s("v"), NT)
            else:
                eng.wait_ge(s("z"), 8 * (it + 1 - (it > 2)))
        elif i == IT_OH:
            eng.wait_ge(s("dbp"), 1)
        elif i < IT_WO:
            g, c = divmod(i - IT_KV, 8)
            eng.wait_ge(s("dS") if c < 4 else s("dOp"), 4 * g + c % 4 + 1)
        else:
            eng.wait_ge(s("woS"), NT)

    def tok(j):
        return slice(j * P, j * P + TW[j])

    block = ctx.enter_context(nc.Block())

    @block.sync
    def _(sp):
        for dst, srcd in ((const[:, :], I["const"]), (par[:, :], I["par"]), (cT[:, :, :], I["cT"]),
                          (ctab33[:, :], I["tab33"]), (ohp[:, :], I["oh_prompt"]),
                          (ct[0][:, :, :], I["ct_re"]), (ct[1][:, :, :], I["ct_im"]),
                          (adab[:, :], I["ada_b"]),
                          (ngain[:, 0, :], I["norm1_g"].partition_broadcast(NC)),
                          (ngain[:, 1, :], I["norm2_g"].partition_broadcast(NC))):
            sp.dma_start(dst, srcd).then_inc(s("init"), 16)

        ada_v = I["ada_w"].rearrange("(k p) n -> p k n", p=P)
        win_v = I["w_in"].rearrange("(k p) n -> p k n", p=P)
        wo_v = I["w_out"].rearrange("(k p) n -> p k n", p=P)

        def item(i):
            if i >= R1:
                used(sp, i - R1)
            r = ring[i % R1]
            if i < IT_WIN:
                c = i - IT_ADA
                dst, src = r[:, :].rearrange("p (k n) -> p k n", k=KD), ada_v[:, :, 512 * c:512 * (c + 1)]
            elif i < IT_OH:
                c = i - IT_WIN
                dst, src = r[:, :].rearrange("p (k n) -> p k n", k=KD), win_v[:, :, 512 * c:512 * (c + 1)]
            elif i == IT_OH:
                dst, src = r[0:BUCKETS + 1, 0:TDEC * DK], I["oh_decode"]
            elif i < IT_WO:
                g, m = divmod(i - IT_KV, 8)
                n = 4 * g + m % 4
                dst, src = r[:, 0:4 * CK], I["cache_v" if m >= 4 else "cache_k"][n]
            else:
                c = i - IT_WO
                dst, src = r[:, :].rearrange("p (k n) -> p k n", k=KD), wo_v[:, :, 512 * c:512 * (c + 1)]
            sp.dma_start(dst, src).then_inc(rfull[i % R1], 16)

        def x_tile(j):
            if j >= 2:
                sp.wait_ge(s("h"), j - 1)
            sp.dma_start(xt[0:TW[j], j % 2, :], I["x"][tok(j), :]).then_inc(s_x[j % 2], 16)

        for i in range(8):
            item(i)
        sp.wait_ge(s("tables"), 1)
        for j in range(2):
            x_tile(j)
        for i in range(8, IT_OH):
            item(i)
        for b in range(2):
            sp.wait_ge(s_modst[b], 16 * N_ADA // 2)
        sp.wait_ge(s("btT"), 8)
        sp.dma_start(modP[:, :, :], mod_d[0:1, 0:2 * D].rearrange("a (v n) -> (a v) n", v=2)
                     .partition_broadcast(P)).then_inc(s("modld"), 16)
        for t in range(TDEC):
            sp.dma_start(modS[t:NS:TDEC, :, :], mod_d[1:NC, 0:2 * D].rearrange("a (v n) -> a v n", v=2))\
              .then_inc(s("modld"), 16)
        for j in range(2, NT):
            x_tile(j)
        for i in range(IT_OH, IT_KV + 2):
            item(i)
        sp.wait_ge(s("gst"), 16)
        sp.wait_ge(s("z"), 24)
        for h in range(HEADS):
            if h == 2:
                item(IT_KV + 2)
                item(IT_KV + 3)
            if h >= 2:
                sp.wait_ge(s("S"), QT * (h - 1))
            sp.dma_start(toep[:, h % 2, :], bass.AP(g_d.tensor, 640 * h, [[1, P], [1, SEQ]]))\
                .then_inc(s_toep[h % 2], 16)
        for i in range(IT_KV + 4, N_ITEMS):
            item(i)
        sp.wait_ge(s("gluo"), QT + 1)
        sp.wait_ge(s("dOp"), NSEQ)
        sp.wait_ge(s("attS"), 1)
        sp.wait_ge(s("kvst"), 48)
        sp.dma_start(mod3P[:, :, :], mod_d[0:1, 2 * D:5 * D].rearrange("a (v n) -> (a v) n", v=3)
                     .partition_broadcast(P)).then_inc(s("mod3"), 16)
        for t in range(TDEC):
            sp.dma_start(mod3S[t:NS:TDEC, :, :], mod_d[1:NC, 2 * D:5 * D].rearrange("a (v n) -> a v n", v=3))\
              .then_inc(s("mod3"), 16)
        sp.wait_ge(s("attT"), NT)
        sp.wait_ge(s("ssmst"), 32)
        sp.dma_start(rw[:, :, :], I["router_w"]).then_inc(s("mod3"), 16)
        sp.dma_start(rb[:, :], I["router_b"]).then_inc(s("mod3"), 16)
        for j in range(NT):
            if j >= 2:
                sp.wait_ge(s("x2"), j - 1)
            sp.dma_start(xt3[0:TW[j], j % 2, :], I["x"][tok(j), :]).then_inc(s_x3[j % 2], 16)

        done = (s("egate"), s("eup"), s("ey"))

        def expert(e, u):
            for w, (name, k) in enumerate((("w_gate", KD), ("w_up", KD), ("w_down", FE // P))):
                yield (w, ering[3 * u + w][:, :].rearrange("p (k n) -> p k n", k=k),
                       I[name][bass.ds(e, 1)].rearrange("a (k p) n -> p (a k) n", p=P))

        for u in range(2):
            for w, dst, src in expert(u, u):
                m = 3 * u + w
                if m < R1:
                    used(sp, N_ITEMS - R1 + (m - N_ITEMS) % R1)
                if m >= 4:
                    sp.wait_ge(s("yp"), 4 * QT + 1)
                sp.dma_start(dst, src).then_inc(efull[m], 16)
        with sp.Fori(1, NE // 2) as i:
            for u in range(2):
                for w, dst, src in expert(2 * i + u, u):
                    sp.wait_ge(done[w], 2 * i + (u - 1))
                    sp.dma_start(dst, src).then_inc(efull[3 * u + w], 16)
        sp.wait_ge(s("eid"), 1)
        pairs = sp.value_load(npair[0:1, 0:1], min_val=0, max_val=EXTRA // 2)
        with sp.Fori(0, EXTRA // 2) as i:
            with sp.If(pairs > i):
                for u in range(2):
                    e = sp.value_load(eidi[0:1, bass.ds(2 * i + u, 1)], min_val=0, max_val=NE - 1)
                    for w, dst, src in expert(e, u):
                        sp.wait_ge(done[w], 2 * i + (NE + u - 1))
                        sp.dma_start(dst, src).then_inc(efull[3 * u + w], 16)
        sp.wait_ge(s("statest"), 16)
        sp.wait_ge(s("kvst"), 48)
        sp.wait_ge(s("ssmst"), 32)
        for b in range(2):
            sp.wait_ge(s_fst[b], 16 * ((NT - b + 1) // 2))

    @block.gpsimd
    def _(pool):
        o = Order(pool, s("pool_order"))
        pool.wait_ge(s("init"), 160)
        for b in range(2):
            o(pool.memset(bpad[b][:, :, :], 0.0))
        for half in range(2):
            for r in range(4):
                for b, src in enumerate((bbr, bbi)):
                    if half == 0 and r == 0 and b == 0:
                        pool.wait_ge(s("bbar"), 1)
                    rows = slice(64 * half, 64 * half + 64)
                    c0 = 32 * r + GC * half
                    ins = pool.tensor_copy(bpad[b][rows, r::4, c0:c0 + GC], src[rows, r::4, :])
                    o(ins)
        pool.sem_inc(s("bpad"), 1)
        for n, c in enumerate((2, 3, 8, 9)):
            pool.wait_ge(s("adae"), c + 1)
            m = modsb[:, c % 2, :]
            gn = ngain[:, c // 6, 512 * (c % 2):512 * (c % 2) + 512]
            pool.tensor_tensor(m, m, gn, ALU.mult).then_inc(s("modg"), 1)
        pool.wait_ge(s("modld"), 80)
        for j in range(NT):
            w = TW[j]
            pool.wait_ge(s("hA"), j + 1)
            sh = modP[:, 0, :] if j < QT else modS[:, 0, :]
            pool.tensor_tensor(hb[0:w, j % 2, :], hb[0:w, j % 2, :], sh, ALU.add).then_inc(s("h"), 1)
        pool.wait_ge(s("hTp"), 2 * NT)
        pool.wait_ge(s("h"), NT)
        o(pool.memset(padT[:, :, :], 0.0))
        for t in range(TDEC):
            for n in range(4):
                ins = pool.tensor_copy(padT[:, t, 32 * n + t:32 * n + 32:TDEC], ctab33[:, :])
                o(ins)
        pool.sem_inc(s("padt"), 1)
        o(pool.memset(qbd[:, :, :, :], 0.0))
        pool.wait_ge(s("za"), 12)
        pool.wait_ge(s("zd"), 12)
        for h in range(HEADS):
            r = slice(64 * (h % 2), 64 * (h % 2) + 64)
            o(pool.tensor_copy(qbd[r, :, h // 2, TDEC * h:TDEC * (h + 1)],
                               qkT[r, h // 2, SEQ:NTOK].rearrange("p (n t) -> p n t", t=TDEC)))
        pool.sem_inc(s("qbd"), 1)
        flat = lambda a: a[:, :, :].rearrange("p a b -> p (a b)")
        sv = lambda a: flat(a).rearrange("p (s n t) -> p s n t", s=STT, n=NSEQ)
        h0v = lambda a: flat(a)[:, 0:STT * NSEQ].rearrange("p (s n) -> p s n", s=STT)
        tmpv = lambda i: flat(ta)[:, 128 * i:128 * i + 128].rearrange("p (s n) -> p s n", s=STT)
        pool.dma_start(h0v(gr[0]), I["h0_re"]).then_inc(s("h0"), 16)
        pool.dma_start(h0v(gi[0]), I["h0_im"]).then_inc(s("h0"), 16)
        o(pool.tensor_tensor(car[:, :], mag[:, :], cth[:, :], ALU.mult))
        o(pool.tensor_tensor(cai[:, :], mag[:, :], sth[:, :], ALU.mult))
        pool.wait_ge(s("buS"), 1)
        pool.wait_ge(s("h0"), 32)
        acr, aci = [a[:, :].unsqueeze(2).broadcast_to([P, STT, NSEQ]) for a in (car, cai)]
        for t in range(TDEC):
            pr_, pi_ = (h0v(gr[0]), h0v(gi[0])) if t == 0 else (sv(hr[0])[:, :, :, t - 1], sv(hi[0])[:, :, :, t - 1])
            t1, t2, t3, t4 = [tmpv(i) for i in range(4)]
            pool.tensor_tensor(t1, pr_, acr, ALU.mult)
            pool.tensor_tensor(t2, pi_, aci, ALU.mult)
            pool.tensor_tensor(t3, pr_, aci, ALU.mult)
            o(pool.tensor_tensor(t4, pi_, acr, ALU.mult))
            pool.tensor_tensor(t1, t1, t2, ALU.subtract)
            o(pool.tensor_tensor(t3, t3, t4, ALU.add))
            pool.tensor_tensor(sv(hr[0])[:, :, :, t], t1, sv(xr[0])[:, :, :, t], ALU.add)
            o(pool.tensor_tensor(sv(hi[0])[:, :, :, t], t3, sv(xi[0])[:, :, :, t], ALU.add))
        for n, a in enumerate((hr, hi)):
            o(pool.tensor_copy(states[:, 128 * n:128 * n + 128].rearrange("p (s n) -> p s n", s=STT),
                               sv(a[0])[:, :, :, TDEC - 1]))
        pool.sem_inc(s("hout"), 1)
        pool.wait_ge(s("sq"), NT + 1)
        pool.dma_start(glu[:, 0, :, :], I["glu_a"]).then_inc(s("glul"), 16)
        pool.dma_start(glu[:, 1, :, :], I["glu_b"]).then_inc(s("glul"), 16)
        pool.dma_start(y_d[NE * P:NTILE * P, :], I["zero"].partition_broadcast(EXTRA * P)).then_inc(s("yzero"), 16)
        pool.dma_start(O["ssm_s"], states[:, :]).then_inc(s("statest"), 16)
        pool.wait_ge(s("kvst"), 48)
        for i in range(16):
            k, q = divmod(i, 4)
            b = i % 2
            tq = slice(4 * q, 4 * q + 4)
            cs, sn = cosT[:, tq, :], sinT[:, tq, :]
            pool.wait_ge(s("scan"), i + 1)
            if i != 1:
                pool.wait_ge(s("yp"), max(i, 1))
            pool.tensor_tensor(hr[b][:, :, :], gr[b][:, :, :], cs, ALU.mult)
            pool.tensor_tensor(xr[b][:, :, :], gi[b][:, :, :], sn, ALU.mult)
            pool.tensor_tensor(hi[b][:, :, :], gr[b][:, :, :], sn, ALU.mult)
            o(pool.tensor_tensor(xi[b][:, :, :], gi[b][:, :, :], cs, ALU.mult))
            pool.tensor_tensor(hr[b][:, :, :], hr[b][:, :, :], xr[b][:, :, :], ALU.subtract)
            o(pool.tensor_tensor(hi[b][:, :, :], hi[b][:, :, :], xi[b][:, :, :], ALU.add))
            lr, li = hr[b][:, :, CH - 1], hi[b][:, :, CH - 1]
            if k == QT - 1:
                pool.tensor_copy(las[:, tq], lr)
                o(pool.tensor_copy(lai[:, tq], li))
            else:
                pool.tensor_tensor(car[:, tq], lr, cth[:, tq], ALU.mult)
                pool.tensor_tensor(ctmp[:, 0:4], li, sth[:, tq], ALU.mult)
                pool.tensor_tensor(cai[:, tq], lr, sth[:, tq], ALU.mult)
                o(pool.tensor_tensor(ctmp[:, 4:8], li, cth[:, tq], ALU.mult))
                pool.tensor_tensor(car[:, tq], car[:, tq], ctmp[:, 0:4], ALU.subtract)
                o(pool.tensor_tensor(cai[:, tq], cai[:, tq], ctmp[:, 4:8], ALU.add))
            pool.sem_inc(s("hout"), 1)
        pool.dma_start(O["ssm_p"][:, 0, :], las[:, :]).then_inc(s("ssmst"), 16)
        pool.dma_start(O["ssm_p"][:, 1, :], lai[:, :]).then_inc(s("ssmst"), 16)

        pool.wait_ge(s("mod3"), 112)
        for j in range(NT):
            w = TW[j]
            m3 = mod3P if j < QT else mod3S
            pool.wait_ge(s("wog"), j + 1)
            pool.wait_ge(s_x3[j % 2], 16 * (j // 2 + 1))
            o(pool.tensor_tensor(pt2[0:w, :], pt1[0:w, j % 2, :], m3[0:w, 0, :], ALU.mult))
            pool.tensor_tensor(x2[0:w, j, :], pt2[0:w, :], xt3[0:w, j % 2, :], ALU.add).then_inc(s("x2"), 1)
            pool.wait_ge(s("hA"), NT + j + 1)
            pool.tensor_tensor(h2[0:w, j % 2, :], h2[0:w, j % 2, :], m3[0:w, 1, :], ALU.add).then_inc(s("h"), 1)
            pool.wait_ge(s("h"), NT + j + 1)
            pool.dma_start(h2_d[tok(j), :], h2[0:w, j % 2, :]).then_inc(s_h2st[j % 2], 16)
        pool.wait_ge(s_h2st[0], 48)
        pool.wait_ge(s_h2st[1], 32)
        pool.wait_ge(s("gidx"), 1)

        def gather(t):
            u = t % 2
            if t >= 2:
                pool.wait_ge(s("xgp"), t - 1)
                pool.wait_ge(s_xg[u], 16 * (t // 2))
            pool.indirect_dma_start(xg[:, u, :], None, h2_d, bass.IndirectOffsetOnAxis(ap=gidx[:, t:t + 1], axis=0))\
                .then_inc(s_xg[u], 16)

        for t in range(NE):
            gather(t)
        pool.wait_ge(s("eid"), 1)
        pairs = pool.value_load(npair[0:1, 0:1], min_val=0, max_val=EXTRA // 2)
        for i in range(EXTRA // 2):
            with pool.If(pairs > i):
                gather(NE + 2 * i)
                gather(NE + 2 * i + 1)
        pool.wait_ge(s("y_all"), 1)
        for j in range(NT):
            w = TW[j]
            for k in range(2):
                pool.indirect_dma_start(yg[0:w, j, k, :], None, y_d,
                                        bass.IndirectOffsetOnAxis(ap=sidx[0:w, k, j:j + 1], axis=0))\
                    .then_inc(s_yg[j], 16)
        for j in range(NT):
            w = TW[j]
            g2 = mod3P[0:w, 1, :] if j < QT else mod3S[0:w, 0, :]
            pool.wait_ge(s("endld"), 96)
            pool.wait_ge(s("ysum"), j + 1)
            a = yg[0:w, j, 0, :]
            pool.tensor_tensor(a, a, g2, ALU.mult).then_inc(s("ygate"), 1)

    @block.scalar
    def _(act):
        o = Order(act, s("act_order"))

        def f(out, in_, func, **kw):
            return nc.scalar.activation(out, in_, func, **kw)

        act.wait_ge(s("init"), 160)
        f(cE[:, :, :], cT[:, :, :], ACT.Exp, scale=-1.0).then_inc(s("cexp"), 1)
        f(pr[:, 1, :], par[:, PC["log_dt"][0]:PC["log_dt"][1]], ACT.Exp).then_inc(s("dt"), 1)
        act.wait_ge(s("magin"), 1)
        f(mag[:, :], pr[:, 2, :], ACT.Exp).then_inc(s("mag"), 1)
        act.wait_ge(s("phr"), 1)
        f(pr[:, 5, :], pr[:, 4, :], ACT.Sin).then_inc(s("sin"), 1)
        f(pr[:, 6, :], pr[:, 4, :], ACT.Sin, scale=0.5).then_inc(s("sin"), 1)
        for c in range(N_ADA):
            act.wait_ge(s("ada"), c + 1)
            if c >= 2:
                act.wait_ge(s_modst[c % 2], 16 * (c // 2))
            scale_row = c in (2, 3, 8, 9)
            f(modsb[:, c % 2, :], ps[0:NC, c % 2, :], ACT.Copy, bias=1.0 if scale_row else 0.0)\
                .then_inc(s("adae"), 1)
            if scale_row:
                act.wait_ge(s("modg"), {2: 1, 3: 2, 8: 3, 9: 4}[c])
            else:
                act.wait_ge(s("adae"), c + 1)
            act.dma_start(mod_d[:, 512 * c:512 * (c + 1)], modsb[:, c % 2, :]).then_inc(s_modst[c % 2], 16)
            if c == 3:
                for n in range(8):
                    act.wait_ge(s("btT"), n + 1)
                    b, q = n // 4, n % 4
                    f(bt[b][:, 4 * q:4 * q + 4, :], ps[:, 2 + n % 2, :].rearrange("p (a b) -> p a b", a=4), ACT.Copy)\
                        .then_inc(s("btTe"), 1)
        act.wait_ge(s("gsb"), 1)
        act.dma_start(g_d, gsb[:, :]).then_inc(s("gst"), 16)
        for j in range(NT):
            w = TW[j]
            act.wait_ge(s_x[j % 2], 16 * (j // 2 + 1))
            f(ps[0:w, 6:8, :], xt[0:w, j % 2, :].rearrange("p (a b) -> p a b", a=2), ACT.Square,
              accum_out=stat[0:w, j:j + 1]).then_inc(s("sq"), 1)
            act.wait_ge(s("rin"), j + 1)
            f(stat[0:w, 16 + j:17 + j], stat[0:w, 8 + j:9 + j], ACT.Sqrt).then_inc(s("rt"), 1)
            act.wait_ge(s("hTp"), 2 * j + 1)
            act.wait_ge(s("gst"), 16)
            f(hT[:, 0:4, tok(j)], ps[:, 2 + 2 * (j % 2), 0:4 * w].rearrange("p (a b) -> p a b", a=4), ACT.Copy)\
                .then_inc(s("hTa"), 1)
        for z in range(12):
            kind, c = divmod(z, 4)
            act.wait_ge(s("z"), 2 * z + 1)
            dst = qkT[:, 4 * kind + c, 0:HALF] if kind < 2 else uT[:, c, 0:HALF]
            f(dst, ps[:, z % 2, 0:HALF], ACT.Copy, scale=DH ** -0.5 if kind == 0 else 1.0).then_inc(s("za"), 1)
        act.wait_ge(s("za"), 12)
        act.wait_ge(s("zd"), 12)
        act.wait_ge(s("ve"), NT)
        act.dma_start(O["kT"].rearrange("(c p) t -> p c t", p=P), qkT[:, 4:8, :]).then_inc(s("kvst"), 16)
        act.dma_start(O["v"][0:SEQ, :].rearrange("(j p) n -> p j n", p=P), vrow[:, 0:QT, :]).then_inc(s("kvst"), 16)
        act.dma_start(O["v"][SEQ:NTOK, :], vrow[0:NS, QT, :]).then_inc(s("kvst"), 16)
        for st in range(HEADS * QT):
            qt = st % QT
            m = P * (qt + 1)
            act.wait_ge(s("sm"), st + 1)
            if st >= 2:
                act.wait_ge(s("rd"), st - 1)
                act.wait_ge(s("pt"), st - 1)
            f(Sb[:, st % 2, 0:m], ps[:, st % 2, 0:m], ACT.Exp, bias=stat[:, 26 + st % 2:27 + st % 2],
              accum_out=stat[:, 28 + st % 2:29 + st % 2]).then_inc(s("P"), 1)
            act.wait_ge(s("pt"), st + 1)
            if st >= 2:
                act.wait_ge(s("pv"), st - 1)
            f(PTs[:, st % 2, 0:m], ps[:, 2 + st % 2, 0:m], ACT.Copy).then_inc(s("ptr"), 1)

        act.wait_ge(s("att"), HEADS * QT)
        for j in range(QT):
            ins = f((Sb, PTs)[j // 2][:, j % 2, :], att[:, j, :], ACT.Square, accum_out=stat[:, j:j + 1])
        ins.then_inc(s("sq"), 1)
        act.wait_ge(s("rin"), NT + 1)
        f(stat[:, 16:16 + QT], stat[:, 8:8 + QT], ACT.Sqrt).then_inc(s("rt"), 1)

        def gelu_in(n, w):
            act.wait_ge(s("yread"), n + 1)
            f(y2[:, :, 0:w], yd[:, :, 0:w], ACT.Square).then_inc(s("ysq"), 1)
            act.wait_ge(s("gin"), n + 1)
            f(th[:, :, 0:w], y2[:, :, 0:w], ACT.Tanh, scale=float(np.sqrt(2.0 / np.pi))).then_inc(s("gth"), 1)

        def gelu_gate(n, w):
            act.wait_ge(s("glut"), n + 1)
            f(th[:, :, 0:w], ps[:, 3, 0:4 * w].rearrange("p (a b) -> p a b", a=4), ACT.Tanh, scale=0.25)\
                .then_inc(s("gate"), 1)

        def dec_exp(g):
            act.wait_ge(s("dSm"), g + 1)
            f(dP[:, :], dP[:, :], ACT.Exp, bias=dstat[:, 4:5], accum_out=dstat[:, 5:6]).then_inc(s("dP"), 1)
            act.wait_ge(s("dPt"), g + 1)
            if g:
                act.wait_ge(s("dOp"), 4 * g)
            f(dPT[:, 4:7, :], ps[:, 3, 0:3 * P].rearrange("p (a b) -> p a b", a=3), ACT.Copy)
            f(dPT[0:NS, 7, :], ps[0:NS, 3, 3 * P:4 * P], ACT.Copy).then_inc(s("dPta"), 1)

        def wo_a(j):
            w = TW[j]
            act.wait_ge(s("woA"), j + 1)
            if j >= 2:
                act.wait_ge(s("x2"), j - 1)
            f(pt1[0:w, j % 2, :].rearrange("p (a b) -> p a b", a=2), ps[0:w, 0:2, :], ACT.Copy).then_inc(s("woa"), 1)

        gelu_in(0, NS)
        gelu_gate(0, NS)
        dec_exp(0)
        gelu_in(1, CH)
        gelu_gate(1, CH)
        gelu_in(2, CH)
        gelu_gate(2, CH)
        dec_exp(1)
        gelu_in(3, CH)
        gelu_gate(3, CH)
        gelu_in(4, CH)
        act.wait_ge(s("attS"), 1)
        f(ps[0:NS, 5, :], att[0:NS, QT, :], ACT.Square, accum_out=stat[0:NS, QT:NT]).then_inc(s("sq"), 1)
        act.wait_ge(s("rin"), NT + 2)
        f(stat[0:NS, 16 + QT:16 + NT], stat[0:NS, 8 + QT:8 + NT], ACT.Sqrt).then_inc(s("rt"), 1)
        gelu_gate(4, CH)
        act.wait_ge(s("ssin"), 1)
        f(dstat[:, 24:24 + NT], dstat[:, 16:16 + NT], ACT.Sqrt).then_inc(s("ssrt"), 1)
        for j in range(NT):
            w = TW[j]
            wo_a(j)
            act.wait_ge(s("x2"), j + 1)
            if j >= 2:
                act.wait_ge(s("hTp"), 2 * (NT + j - 1))
                act.wait_ge(s_h2st[j % 2], 16 * (j // 2))
            f(h2[0:w, j % 2, :], x2[0:w, j, :], ACT.Square,
              accum_out=stat[0:w, j:j + 1]).then_inc(s("sq"), 1)
            act.wait_ge(s("rin"), NT + 3 + j)
            f(stat[0:w, 16 + j:17 + j], stat[0:w, 8 + j:9 + j], ACT.Sqrt).then_inc(s("rt"), 1)
            act.wait_ge(s("hTp"), 2 * (NT + j) + 1)
            f(h2T[:, 0:4, tok(j)], ps[:, 6, 0:4 * w].rearrange("p (a b) -> p a b", a=4), ACT.Copy)\
                .then_inc(s("hTa"), 1)
        act.wait_ge(s("h"), 2 * NT)
        act.wait_ge(s("x2"), NT)
        act.dma_start(mod3P[:, 1, :], mod_d[0:1, 5 * D:6 * D].partition_broadcast(P)).then_inc(s("endld"), 16)
        for t in range(TDEC):
            act.dma_start(mod3S[t:NS:TDEC, 0, :], mod_d[1:NC, 5 * D:6 * D]).then_inc(s("endld"), 16)
        act.dma_start(fgain[:, :], I["final_g"].partition_broadcast(P)).then_inc(s("endld"), 16)
        act.wait_ge(s("gexpin"), 1)
        f(g4b[:, :, :], g4a[:, :, :], ACT.Exp).then_inc(s("gexp"), 1)
        act.wait_ge(s("gapin"), 1)
        f(w2[:, :], v2[:, :], ACT.Exp).then_inc(s("gapexp"), 1)

        def rows(t, u):
            act.wait_ge(s("xgp"), t + 1)
            f(xgT[:, u, 0:4, :], ps[:, 4, :].rearrange("p (a b) -> p a b", a=4), ACT.Copy).then_inc(s("xga"), 1)

        def gate(t, u):
            act.wait_ge(s("egate"), t + 1)
            f(a_t[:, u, :], ps[:, u, :], ACT.Tanh, scale=0.5).then_inc(s("eth"), 1)

        def hidden(t, u):
            act.wait_ge(s("aTp"), t + 1)
            f(aT[:, u, :, :], ps[:, u, :].rearrange("p (a b) -> p a b", a=4), ACT.Copy).then_inc(s("aTe"), 1)

        def finish(t, u, dst, waity):
            act.wait_ge(s("ey"), t + 1)
            if waity is not None:
                act.wait_ge(s_yst[u], waity)
            f(ysb[:, u, 0:512], ps[:, 6, :], ACT.Copy).then_inc(s("eya"), 1)
            act.wait_ge(s("eya"), t + 1)
            act.wait_ge(s("eyd"), t + 1)
            act.dma_start(dst, ysb[:, u, :]).then_inc(s_yst[u], 16)

        def y_tile(t):
            return y_d.rearrange("(t p) n -> t p n", p=P)[bass.ds(t, 1)].rearrange("t p n -> (t p) n")

        rows(0, 0)
        gate(0, 0)
        rows(1, 1)
        for t in (1, 2):
            u = t % 2
            gate(t, u)
            hidden(t - 1, 1 - u)
            rows(t + 1, 1 - u)
            finish(t - 1, 1 - u, y_d[P * (t - 1):P * t, :], None)
        with act.Fori(1, NE // 2 - 1) as i:
            for u in (1, 0):
                t = 2 * i + (2 - u)
                gate(t, u)
                hidden(2 * i + (1 - u), 1 - u)
                rows(2 * i + (3 - u), 1 - u)
                finish(2 * i + (1 - u), 1 - u, y_tile(2 * i + (1 - u)), 16 * i)
        gate(NE - 1, 1)
        hidden(NE - 2, 0)
        finish(NE - 2, 0, y_tile(NE - 2), 16 * (NE // 2 - 1))
        hidden(NE - 1, 1)
        finish(NE - 1, 1, y_tile(NE - 1), 16 * (NE // 2 - 1))
        act.wait_ge(s("eid"), 1)
        act.wait_ge(s("yzero"), 16)
        pairs = act.value_load(npair[0:1, 0:1], min_val=0, max_val=EXTRA // 2)
        with act.Fori(0, EXTRA // 2) as i:
            with act.If(pairs > i):
                rows(2 * i + NE, 0)
                gate(2 * i + NE, 0)
                rows(2 * i + (NE + 1), 1)
                gate(2 * i + (NE + 1), 1)
                for u in range(2):
                    hidden(2 * i + (NE + u), u)
                    finish(2 * i + (NE + u), u, y_tile(2 * i + (NE + u)), 16 * i + 16 * (NE // 2))
        for u in range(2):
            act.wait_ge(s_yst[u], 16 * pairs + 16 * (NE // 2))
        act.sem_inc(s("y_all"), 1)
        for n in range(NT + 2):
            if n < NT:
                j, w = n, TW[n]
                act.wait_ge(s_yg[j], 32)
                f(yg[0:w, j, 0, :], yg[0:w, j, 0, :], ACT.Copy, scale=w1[0:w, j:j + 1]).then_inc(s("yw"), 1)
            if n < 2:
                continue
            j = n - 2
            w = TW[j]
            act.wait_ge(s("x3"), j + 1)
            f(ps[0:w, 0:2, :], x2[0:w, j, :].rearrange("p (a b) -> p a b", a=2), ACT.Square,
              accum_out=stat[0:w, j:j + 1]).then_inc(s("sq"), 1)
            act.wait_ge(s("rin"), 2 * NT + 3 + j)
            f(stat[0:w, 16 + j:17 + j], stat[0:w, 8 + j:9 + j], ACT.Sqrt).then_inc(s("rt"), 1)
            act.wait_ge(s("fo"), j + 1)
            act.dma_start(O["y"][tok(j), :], fo[0:w, j % 2, :]).then_inc(s_fst[j % 2], 16)

    @block.vector
    def _(dve):
        o = Order(dve, s("dve_order"))
        v = nc.vector
        tt_, ts_, stt = v.tensor_tensor, v.tensor_scalar, v.scalar_tensor_tensor
        o(v.memset(stat[:, :], 1.0))
        o(v.memset(dstat[:, :], 1.0))
        dve.wait_ge(s("init"), 160)

        pa = lambda n: par[:, PC[n][0]:PC[n][1]]
        q_ = lambda i: pr[:, i, :]
        lam_re, lam_im, dt = q_(0), pa("a_im"), q_(1)
        o(ts_(lam_re, pa("a_re"), -1e-4, None, ALU.min))
        dve.wait_ge(s("dt"), 1)
        tt_(q_(2), lam_re, dt, ALU.mult).then_inc(s("magin"), 1)
        o(tt_(q_(3), lam_im, dt, ALU.mult))
        big = float(3 << 22)
        c1 = 6.28125
        o(ts_(q_(7), q_(3), 1.0 / (2 * np.pi), big, ALU.mult, ALU.add))
        o(ts_(q_(7), q_(7), -big, None, ALU.add))
        o(stt(out=q_(4), in0=q_(7), scalar=-c1, in1=q_(3), op0=ALU.mult, op1=ALU.add))
        o(stt(out=q_(4), in0=q_(7), scalar=-(2 * np.pi - c1), in1=q_(4), op0=ALU.mult, op1=ALU.add))
        ts_(q_(4), q_(4), 3.1415925, -3.1415925, ALU.min, ALU.max).then_inc(s("phr"), 1)
        dve.wait_ge(s("cexp"), 1)
        o(ts_(cE[:, :, :], cE[:, :, :], 1.0, None, ALU.add))
        o(v.reciprocal(cE[:, :, :], cE[:, :, :]))
        tt_(cS[:, :, :], cT[:, :, :], cE[:, :, :], ALU.mult).then_inc(s("cs"), 1)
        dve.wait_ge(s("sin"), 2)
        o(v.tensor_copy(sth[:, :], q_(5)))
        o(tt_(q_(8), q_(6), q_(6), ALU.mult))
        o(ts_(cth[:, :], q_(8), -2.0, 1.0, ALU.mult, ALU.add))
        dve.wait_ge(s("mag"), 1)
        o(tt_(q_(9), mag[:, :], cth[:, :], ALU.mult))
        o(tt_(q_(10), mag[:, :], sth[:, :], ALU.mult))
        o(ts_(q_(11), q_(9), -1.0, None, ALU.add))
        o(tt_(q_(12), lam_re, lam_re, ALU.mult))
        o(tt_(q_(13), lam_im, lam_im, ALU.mult))
        o(tt_(q_(12), q_(12), q_(13), ALU.add))
        o(v.reciprocal(q_(12), q_(12)))
        o(tt_(q_(13), q_(11), lam_re, ALU.mult))
        o(tt_(q_(14), q_(10), lam_im, ALU.mult))
        o(tt_(q_(13), q_(13), q_(14), ALU.add))
        o(tt_(q_(13), q_(13), q_(12), ALU.mult))
        o(tt_(q_(14), q_(10), lam_re, ALU.mult))
        o(tt_(q_(15), q_(11), lam_im, ALU.mult))
        o(tt_(q_(14), q_(14), q_(15), ALU.subtract))
        o(tt_(q_(14), q_(14), q_(12), ALU.mult))
        crb = q_(13).unsqueeze(2).broadcast_to([P, STT, GC])
        cib = q_(14).unsqueeze(2).broadcast_to([P, STT, GC])
        b_re, b_im = [pa(n).rearrange("p (a b) -> p a b", a=STT) for n in ("b_re", "b_im")]
        o(tt_(bt1[:, :, :], b_re, crb, ALU.mult))
        o(tt_(bt2[:, :, :], b_im, cib, ALU.mult))
        o(tt_(bbr[:, :, :], bt1[:, :, :], bt2[:, :, :], ALU.subtract))
        o(tt_(bt1[:, :, :], b_im, crb, ALU.mult))
        o(tt_(bt2[:, :, :], b_re, cib, ALU.mult))
        tt_(bbi[:, :, :], bt1[:, :, :], bt2[:, :, :], ALU.add).then_inc(s("bbar"), 1)
        o(v.tensor_copy(gains[:, :], par[:, PC["dskip"][0]:PC["ssmg"][1]]))
        o(ts_(gains[:, 8:12], gains[:, 8:12], 0.25, None, ALU.mult))
        o(ts_(ct[1][:, :, :], ct[1][:, :, :], -1.0, None, ALU.mult))
        o(v.memset(cosT[:, :, 0:1], 1.0))
        o(v.memset(sinT[:, :, 0:1], 0.0))
        cm, sm_, c2, s2, c3, s3 = [q_(i) for i in (2, 3, 4, 5, 6, 7)]
        o(v.tensor_copy(cm, cth[:, :]))
        o(v.tensor_copy(sm_, sth[:, :]))
        m = 1
        while m < CH:
            cb, sb_ = [a.unsqueeze(2).broadcast_to([P, STT, m]) for a in (cm, sm_)]
            C_, S_ = cosT[:, :, 0:m], sinT[:, :, 0:m]
            Cn, Sn = cosT[:, :, m:2 * m], sinT[:, :, m:2 * m]
            o(tt_(Cn, C_, cb, ALU.mult))
            o(tt_(dt1[:, :, 0:m], S_, sb_, ALU.mult))
            o(tt_(Cn, Cn, dt1[:, :, 0:m], ALU.subtract))
            o(tt_(Sn, C_, sb_, ALU.mult))
            o(tt_(dt2[:, :, 0:m], S_, cb, ALU.mult))
            o(tt_(Sn, Sn, dt2[:, :, 0:m], ALU.add))
            o(tt_(c2, cm, cm, ALU.mult))
            o(tt_(c3, sm_, sm_, ALU.mult))
            o(tt_(s2, cm, sm_, ALU.mult))
            o(tt_(cm, c2, c3, ALU.subtract))
            o(ts_(sm_, s2, 2.0, None, ALU.mult))
            m *= 2
        dve.sem_inc(s("tables"), 1)
        dve.wait_ge(s("gp"), 1)
        v.tensor_copy(gsb[:, :], ps[0:HEADS, 6:8, :].rearrange("p a b -> p (a b)")[:, 0:640]).then_inc(s("gsb"), 1)

        def rstd(j, w, width, n):
            dve.wait_ge(s("sq"), n)
            ts_(stat[0:w, 8 + j:9 + j], stat[0:w, j:j + 1], 1.0 / width, EPS, ALU.mult, ALU.add).then_inc(s("rin"), 1)
            dve.wait_ge(s("rt"), n)
            o(v.reciprocal(stat[0:w, 56 + j:57 + j], stat[0:w, 16 + j:17 + j]))

        dve.wait_ge(s("bpad"), 1)
        for j in range(NT):
            w = TW[j]
            rstd(j, w, D, j + 1)
            dve.wait_ge(s("modld"), 80)
            if j >= 2:
                dve.wait_ge(s("hTp"), 2 * (j - 1))
            A = modP[:, 1, :] if j < QT else modS[:, 1, :]
            stt(out=hb[0:w, j % 2, :], in0=xt[0:w, j % 2, :], scalar=stat[0:w, 56 + j:57 + j], in1=A,
                op0=ALU.mult, op1=ALU.mult).then_inc(s("hA"), 1)
            dve.wait_ge(s("gst"), 16)
            dve.wait_ge(s("hTp"), 2 * j + 2)
            v.tensor_copy(hT[:, 4:8, tok(j)], ps[:, 3 + 2 * (j % 2), 0:4 * w].rearrange("p (a b) -> p a b", a=4))\
                .then_inc(s("hTd"), 1)

        def z_half(z):
            kind, c = divmod(z, 4)
            dve.wait_ge(s("z"), 2 * z + 2)
            dst = qkT[:, 4 * kind + c, HALF:NTOK] if kind < 2 else uT[:, c, HALF:NTOK]
            ts_(dst, ps[:, 6 + z % 2, 0:HALF], DH ** -0.5 if kind == 0 else 1.0, None, ALU.mult).then_inc(s("zd"), 1)

        for z in range(8):
            z_half(z)
        for j in range(NT):
            w = TW[j]
            dve.wait_ge(s("v"), j + 1)
            v.tensor_copy(vrow[0:w, j, :], ps[0:w, 2 + j % 2, :]).then_inc(s("ve"), 1)
        for z in range(8, 12):
            z_half(z)
        dve.wait_ge(s("dbp"), 1)
        o(v.tensor_copy(dbias[:, :], ps[:, 2:4, :].rearrange("p a b -> p (a b)")[:, 0:DK]))
        for g in range(2):
            o(tt_(nbias[:, NS * g:NS * g + NS], dbias[:, CK:DK], cst("newmask")[:, NS * g:NS * g + NS], ALU.add))
        dve.sem_inc(s("dbias"), 1)
        dve.wait_ge(s("buSp"), 1)
        v.tensor_copy(xr[0][:, :, :].rearrange("p a b -> p (a b)"), ps[:, 5, :])
        v.tensor_copy(xi[0][:, :, :].rearrange("p a b -> p (a b)"), ps[:, 6, :]).then_inc(s("buS"), 1)

        NST = HEADS * QT

        def row_max(st):
            h, qt = divmod(st, QT)
            b, m = st % 2, P * (qt + 1)
            dve.wait_ge(s("S"), st + 1)
            o(v.tensor_reduce(stat[:, 24 + b:25 + b], ps[:, b, 0:m], AX.X, ALU.max))
            ts_(stat[:, 26 + b:27 + b], stat[:, 24 + b:25 + b], -1.0, None, ALU.mult).then_inc(s("sm"), 1)

        def head_out(st):
            h, qt = divmod(st, QT)
            b = st % 2
            dve.wait_ge(s("P"), st + 1)
            v.reciprocal(stat[:, 30 + b:31 + b], stat[:, 28 + b:29 + b]).then_inc(s("rd"), 1)
            dve.wait_ge(s("rd"), st + 1)
            dve.wait_ge(s("pv"), st + 1)
            ts_(att[:, qt, DH * h:DH * (h + 1)], ps[:, 4 + qt, DH * h:DH * (h + 1)], stat[:, 30 + b:31 + b], None,
                ALU.mult).then_inc(s("att"), 1)

        for st in range(NST + 2):
            if st < NST:
                row_max(st)
            if st >= 2:
                head_out(st - 2)

        def att_out(j):
            w = TW[j]
            bank = 2 + j % 2 if j < QT else 5
            dve.wait_ge(s("attT"), j + 1)
            tt_(mixT[:, 0:4, tok(j)], ps[:, bank, 0:4 * w].rearrange("p (a b) -> p a b", a=4),
                gains[:, 4:8].unsqueeze(2).broadcast_to([P, 4, w]), ALU.mult).then_inc(s("attTe"), 1)

        def turn_in(i):
            q, b = i % 4, i % 2
            cs, sn = cosT[:, 4 * q:4 * q + 4, :], sinT[:, 4 * q:4 * q + 4, :]
            bre, bim = [ps[:, 5 + n, :].rearrange("p (a b) -> p a b", a=4) for n in range(2)]
            if i == 1:
                dve.wait_ge(s("qbd"), 1)
            else:
                dve.wait_ge(s("hout"), max(i, 1))
            dve.wait_ge(s("bu"), i + 1)
            tt_(xr[b][:, :, :], bre, cs, ALU.mult)
            tt_(ta[:, :, :], bim, sn, ALU.mult)
            tt_(xi[b][:, :, :], bim, cs, ALU.mult)
            tt_(tb[:, :, :], bre, sn, ALU.mult).then_inc(s("buread"), 1)
            dve.wait_ge(s("buread"), i + 1)
            tt_(xr[b][:, :, :], xr[b][:, :, :], ta[:, :, :], ALU.add)
            tt_(xi[b][:, :, :], xi[b][:, :, :], tb[:, :, :], ALU.subtract).then_inc(s("xadd"), 1)

        def scans(i):
            k, q = divmod(i, 4)
            b = i % 2
            dve.wait_ge(s("xadd"), i + 1)
            for r in range(4):
                t = 4 * q + r
                m = mag[:, t:t + 1].broadcast_to([P, CH])
                v.tensor_tensor_scan(gr[b][:, r, :], m, xr[b][:, r, :], 0.0 if k == 0 else car[:, t:t + 1],
                                     ALU.mult, ALU.add)
                ins = v.tensor_tensor_scan(gi[b][:, r, :], m, xi[b][:, r, :], 0.0 if k == 0 else cai[:, t:t + 1],
                                           ALU.mult, ALU.add)
            ins.then_inc(s("scan"), 1)

        def chunk(n):
            return (CH, CH * (n - 1)) if n else (NS, SEQ)

        def gelu_skip(n):
            w, t0 = chunk(n)
            dve.wait_ge(s("yp"), 4 * n + 1)
            for q in range(4):
                ins = stt(out=yd[:, q, 0:w], in0=uT[:, q, t0:t0 + w], scalar=gains[:, q:q + 1],
                          in1=ps[:, 7, w * q:w * (q + 1)], op0=ALU.mult, op1=ALU.add)
            ins.then_inc(s("yread"), 1)

        def gelu_cubic(n):
            w, t0 = chunk(n)
            dve.wait_ge(s("ysq"), n + 1)
            o(ts_(y2[:, :, 0:w], y2[:, :, 0:w], 0.044715, 1.0, ALU.mult, ALU.add))
            tt_(y2[:, :, 0:w], y2[:, :, 0:w], yd[:, :, 0:w], ALU.mult).then_inc(s("gin"), 1)

        def gelu_out(n):
            w, t0 = chunk(n)
            dve.wait_ge(s("gth"), n + 1)
            stt(out=y2[:, :, 0:w], in0=th[:, :, 0:w], scalar=1.0, in1=yd[:, :, 0:w], op0=ALU.add, op1=ALU.mult)\
                .then_inc(s("gel"), 1)

        def gated(n):
            w, t0 = chunk(n)
            dve.wait_ge(s("gate"), n + 1)
            ga = ps[:, 2, 0:4 * w].rearrange("p (a b) -> p a b", a=4)
            o(stt(out=y2[:, :, 0:w], in0=th[:, :, 0:w], scalar=1.0, in1=ga, op0=ALU.add, op1=ALU.mult))
            stt(out=yd[:, :, 0:w], in0=y2[:, :, 0:w], scalar=0.0625, in1=y2[:, :, 0:w], op0=ALU.mult, op1=ALU.mult)\
                .then_inc(s("gsq"), 1)
            tt_(mixT[:, 4:8, t0:t0 + w], y2[:, :, 0:w], gains[:, 8:12].unsqueeze(2).broadcast_to([P, 4, w]), ALU.mult)

        def ssum(n):
            w = chunk(n)[0]
            j = n - 1 if n else QT
            dve.wait_ge(s("ssp"), n + 1)
            v.tensor_copy(dstat[0:w, 8 + j:9 + j], ps[0:w, 2, 0:1]).then_inc(s("gluo"), 1)

        def dec_softmax(g):
            dve.wait_ge(s("dS"), 4 * (g + 1))
            if g == 0:
                dve.wait_ge(s("statest"), 16)
            if g:
                dve.wait_ge(s("dPt"), g)
            flat = ps[:, 0:2, :].rearrange("p a b -> p (a b)")
            o(v.tensor_tensor_reduce(out=dP[:, 0:CK], in0=flat[:, 0:CK], in1=dbias[:, 0:CK], scale=1.0,
                                     scalar=-3.0e38, op0=ALU.add, op1=ALU.max, accum_out=dstat[:, 0:1]))
            o(v.tensor_tensor_reduce(out=dP[:, CK:DK], in0=flat[:, CK:DK], in1=nbias[:, NS * g:NS * g + NS], scale=1.0,
                                     scalar=-3.0e38, op0=ALU.add, op1=ALU.max, accum_out=dstat[:, 1:2]))
            o(tt_(dstat[:, 2:3], dstat[:, 0:1], dstat[:, 1:2], ALU.max))
            ts_(dstat[:, 4:5], dstat[:, 2:3], -1.0, None, ALU.mult).then_inc(s("dSm"), 1)

        def dec_probs(g):
            dve.wait_ge(s("dP"), g + 1)
            o(v.reciprocal(dstat[:, 6:7], dstat[:, 5:6]))
            dve.wait_ge(s("dPt"), g + 1)
            if g:
                dve.wait_ge(s("dOp"), 4 * g)
            v.tensor_copy(dPT[:, 0:4, :], ps[:, 2, :].rearrange("p (a b) -> p a b", a=4)).then_inc(s("dPtd"), 1)

        def dec_out(g):
            dve.wait_ge(s("dOp"), 4 * (g + 1))
            stt(out=dO[:, g, :], in0=ps[:, 4, :], scalar=dstat[:, 6:7], in1=cst("headsel"),
                op0=ALU.mult, op1=ALU.mult).then_inc(s("dOe"), 1)

        dve.wait_ge(s("att"), NST)
        dve.wait_ge(s("sq"), NT + 1)
        ts_(stat[:, 8:8 + QT], stat[:, 0:QT], 1.0 / AW, EPS, ALU.mult, ALU.add).then_inc(s("rin"), 1)
        for i in range(16):
            n, part = divmod(i, 4)
            if i == 4 or (part == 0 and n >= 2):
                ssum(n - 1)
            if i == 1:
                gelu_skip(0)
            if i == 2:
                gelu_out(0)
            if part == 2 and n:
                gelu_out(n)
            if i == 8:
                dec_out(0)
            if i in (4, 12):
                dec_probs(n // 2)
            turn_in(i)
            if i == 0:
                dve.wait_ge(s("rt"), NT + 1)
                o(v.reciprocal(stat[:, 56:56 + QT], stat[:, 16:16 + QT]))
                for j in range(QT):
                    ts_(att[:, j, :], att[:, j, :], stat[:, 56 + j:57 + j], None, ALU.mult).then_inc(s("attn"), 1)
            if part == 1 and n:
                gelu_skip(n)
            if part == 3:
                gated(n)
            scans(i)
            if i == 0:
                for j in range(QT):
                    att_out(j)
            if part == 1:
                gelu_cubic(n)
            if i in (3, 11):
                dec_softmax(n // 2)
        ssum(3)
        dec_out(1)
        gelu_skip(4)
        gelu_cubic(4)
        dve.wait_ge(s("attSp"), 1)
        v.tensor_copy(att[0:NS, QT, :], ps[0:NS, 4, :]).then_inc(s("attS"), 1)
        gelu_out(4)
        rstd(QT, NS, AW, NT + 2)
        ts_(att[0:NS, QT, :], att[0:NS, QT, :], stat[0:NS, 56 + QT:57 + QT], None, ALU.mult).then_inc(s("attn"), 1)
        att_out(QT)
        gated(4)
        ssum(4)
        dve.wait_ge(s("gluo"), NT)
        ts_(dstat[:, 16:16 + NT], dstat[:, 8:8 + NT], 1.0 / (D - AW), EPS, ALU.mult, ALU.add).then_inc(s("ssin"), 1)
        dve.wait_ge(s("ssrt"), 1)
        o(v.reciprocal(rssm[:, 0:NT], dstat[:, 24:24 + NT]))
        o(v.memset(lg[:, :, :], 0.0))

        dve.wait_ge(s("mod3"), 112)

        def join(j):
            w = TW[j]
            dve.wait_ge(s("woa"), j + 1)
            dve.wait_ge(s("woS"), j + 1)
            a = pt1[0:w, j % 2, :].rearrange("p (a b) -> p a b", a=2)
            stt(out=a, in0=ps[0:w, 2:4, :], scalar=rssm[0:w, j:j + 1], in1=a, op0=ALU.mult, op1=ALU.add)\
                .then_inc(s("wog"), 1)

        for j in range(NT):
            w = TW[j]
            m3 = mod3P if j < QT else mod3S
            join(j)
            rstd(j, w, D, NT + 3 + j)
            stt(out=h2[0:w, j % 2, :], in0=x2[0:w, j, :], scalar=stat[0:w, 56 + j:57 + j], in1=m3[0:w, 2, :],
                op0=ALU.mult, op1=ALU.mult).then_inc(s("hA"), 1)
            dve.wait_ge(s("hTp"), 2 * (NT + j) + 2)
            v.tensor_copy(h2T[:, 4:8, tok(j)], ps[:, 7, 0:4 * w].rearrange("p (a b) -> p a b", a=4))\
                .then_inc(s("hTd"), 1)
            dve.wait_ge(s("lg"), j + 1)
            o(v.tensor_copy(lg[0:w, j, :], ps[0:w, 4, 20 * j:20 * j + 20]))

        G = lg[:, :, 0:4]
        Lv = lg[:, :, 4:20].rearrange("p j (g e) -> p j g e", g=NG)
        b4 = lambda a: a[:, :].unsqueeze(2).broadcast_to([P, NT, 4])
        first = cst("first").unsqueeze(1).broadcast_to([P, NT, 4])

        def first_max(hot, vals, top, t1):
            o(v.tensor_reduce(top[:, :], vals, AX.X, ALU.max))
            o(tt_(t1[:, :, :], vals, b4(top), ALU.is_equal))
            o(tt_(t1[:, :, :], t1[:, :, :], first, ALU.mult))
            o(v.tensor_reduce(gmax[:, :], t1[:, :, :], AX.X, ALU.max))
            o(tt_(hot[:, :, :], t1[:, :, :], b4(gmax), ALU.is_equal))

        first_max(ghot, G, gsum, g4c)
        tt_(g4a[:, :, :], G, b4(gsum), ALU.subtract).then_inc(s("gexpin"), 1)
        o(tt_(ghot[:, :, :], ghot[:, :, :], b4(cst("valid")), ALU.mult))
        e44 = lambda a: a[:, :, :].rearrange("p j (g e) -> p j g e", g=NG)
        gh4 = ghot[:, :, :].unsqueeze(3).broadcast_to([P, NT, NG, EPG])
        o(tt_(e44(e16), Lv, gh4, ALU.mult))
        o(v.tensor_reduce(esel[:, :, :], e16[:, :, :].rearrange("p j (g e) -> p j e g", g=NG), AX.X, ALU.add))
        first_max(o1, esel[:, :, :], v1, g4c)
        o(stt(out=esel[:, :, :], in0=o1[:, :, :], scalar=NEG, in1=esel[:, :, :], op0=ALU.mult, op1=ALU.add))
        first_max(o2, esel[:, :, :], v2, g4c)
        tt_(v2[:, :], v2[:, :], v1[:, :], ALU.subtract).then_inc(s("gapin"), 1)
        for E_, o_ in ((E1, o1), (E2, o2)):
            o(tt_(e44(E_), gh4, o_[:, :, :].unsqueeze(2).broadcast_to([P, NT, NG, EPG]), ALU.mult))
        tt_(M[:, :, :], E1[:, :, :], E2[:, :, :], ALU.add).then_inc(s("rM"), 1)
        dve.wait_ge(s("gexp"), 1)
        o(v.tensor_reduce(gsum[:, :], g4b[:, :, :], AX.X, ALU.add))
        dve.wait_ge(s("gapexp"), 1)
        o(ts_(w1[:, :], w2[:, :], 1.0, None, ALU.add))
        o(tt_(w1[:, :], w1[:, :], gsum[:, :], ALU.mult))
        o(v.reciprocal(w1[:, :], w1[:, :]))
        o(tt_(w2[:, :], w2[:, :], w1[:, :], ALU.mult))
        dve.wait_ge(s("posp"), 1)
        o(v.tensor_copy(pos[:, :, :], ps[:, 0, 0:NT * NE].rearrange("p (j e) -> p j e", j=NT)))
        o(v.tensor_copy(cnt[:, :], ps[:, 1, 0:NE]))
        o(ts_(nx[:, :], cnt[:, :], float(P), None, ALU.is_gt))
        for i in range(2, -(-NTOK // P)):
            o(stt(out=nx[:, :], in0=cnt[:, :], scalar=float(P * i), in1=nx[:, :], op0=ALU.is_gt, op1=ALU.add))
        o(v.tensor_tensor_scan(xb[:, :], cst("ones")[:, 0:NE], nx[:, :], 0.0, ALU.mult, ALU.add))
        o(tt_(xb[:, :], xb[:, :], nx[:, :], ALU.subtract))
        be = lambda a: a[:, :].unsqueeze(1).broadcast_to([P, EXTRA, NE])
        jb = cst("jidx").unsqueeze(2).broadcast_to([P, EXTRA, NE])
        o(tt_(eid8[:, :, :], be(xb), jb, ALU.subtract))
        o(tt_(eid9[:, :, :], eid8[:, :, :], be(nx), ALU.add))
        o(ts_(eid9[:, :, :], eid9[:, :, :], 0.0, None, ALU.is_gt))
        o(stt(out=eid9[:, :, :], in0=eid8[:, :, :], scalar=0.0, in1=eid9[:, :, :], op0=ALU.is_le, op1=ALU.mult))
        o(tt_(eid9[:, :, :], eid9[:, :, :], be(cst("eidx")), ALU.mult))
        o(v.tensor_reduce(eid[:, :], eid9[:, :, :], AX.X, ALU.add))
        o(v.tensor_copy(eidi[:, :], eid[:, :]))
        o(v.tensor_reduce(xtot[:, :], nx[:, :], AX.X, ALU.add))
        o(ts_(eid[:, 0:EXTRA // 2], cst("jidx")[:, 0:EXTRA:2], xtot[:, 0:1], None, ALU.is_lt))
        o(v.tensor_reduce(xtot[:, :], eid[:, 0:EXTRA // 2], AX.X, ALU.add))
        v.tensor_copy(npair[:, :], xtot[:, :]).then_inc(s("eid"), 1)
        o(stt(out=nx2[:, :], in0=xb[:, :], scalar=float(P), in1=cst("exbase"), op0=ALU.mult, op1=ALU.add))
        bj = lambda a: a[:, :].unsqueeze(1).broadcast_to([P, NT, NE])
        o(ts_(slot[:, :, :], pos[:, :, :], float(P), None, ALU.is_ge))
        o(tt_(slot[:, :, :], slot[:, :, :], bj(nx2), ALU.mult))
        o(tt_(slot[:, :, :], slot[:, :, :], pos[:, :, :], ALU.add))
        o(tt_(slot[:, :, :], slot[:, :, :], bj(cst("ebase")), ALU.add))
        tbb = cst("tbase").unsqueeze(1).broadcast_to([P, NT, NTILE])
        bt_ = lambda a: a[:, :].unsqueeze(2).broadcast_to([P, NT, NTILE])
        for k, E_ in enumerate((E1, E2)):
            o(tt_(e16[:, :, :], E_[:, :, :], slot[:, :, :], ALU.mult))
            o(v.tensor_reduce(sl[k][:, :], e16[:, :, :], AX.X, ALU.add))
            o(v.tensor_copy(sidx[:, k, :], sl[k][:, :]))
            o(tt_(td[:, :, :], tbb, bt_(sl[k]), ALU.subtract))
            o(ts_(tm[:, :, :], td[:, :, :], -float(P), None, ALU.is_gt))
            o(stt(out=tt[k][:, :, :], in0=td[:, :, :], scalar=0.0, in1=tm[:, :, :], op0=ALU.is_le, op1=ALU.mult))
            o(tt_(tm[:, :, :], tt[k][:, :, :], td[:, :, :], ALU.mult))
            o(v.tensor_reduce(ms[k][:, :], tm[:, :, :], AX.X, ALU.add))
            o(ts_(ms[k][:, :], ms[k][:, :], -1.0, None, ALU.mult))
            o(tt_(slot1h[:, k, :, :], cst("iota").unsqueeze(1).broadcast_to([P, NT, P]),
                  ms[k][:, :].unsqueeze(2).broadcast_to([P, NT, P]), ALU.is_equal))
            o(tt_(tt[k][:, :, :], tt[k][:, :, :], bt_(cst("tokid")), ALU.mult))
            ins = tt_(tt[k][:, :, :], tt[k][:, :, :], bt_(cst("valid")), ALU.mult)
            ins.then_inc(s("oneh"), 1)
        dve.wait_ge(s("idxp"), 1)
        v.tensor_copy(gidx[:, :], ps[:, 2, 0:NTILE]).then_inc(s("gidx"), 1)

        def rows(t, u):
            dve.wait_ge(s("xgp"), t + 1)
            v.tensor_copy(xgT[:, u, 4:8, :], ps[:, 5, :].rearrange("p (a b) -> p a b", a=4)).then_inc(s("xgd"), 1)

        def hidden(t, u):
            dve.wait_ge(s("eth"), t + 1)
            stt(out=a_s[:, u, :], in0=a_t[:, u, :], scalar=1.0, in1=ps[:, u, :], op0=ALU.add, op1=ALU.mult)\
                .then_inc(s("esilu"), 1)
            dve.wait_ge(s("esilu"), t + 1)
            dve.wait_ge(s("eup"), t + 1)
            stt(out=a_t[:, u, :], in0=a_s[:, u, :], scalar=0.5, in1=ps[:, 2 + u, :], op0=ALU.mult, op1=ALU.mult)\
                .then_inc(s("ahid"), 1)

        def finish(t, u, wait_store):
            dve.wait_ge(s("ey"), t + 1)
            if wait_store is not None:
                dve.wait_ge(s_yst[u], wait_store)
            v.tensor_copy(ysb[:, u, 512:1024], ps[:, 7, :]).then_inc(s("eyd"), 1)

        rows(0, 0)
        hidden(0, 0)
        rows(1, 1)
        for t in (1, 2):
            u = t % 2
            hidden(t, u)
            rows(t + 1, 1 - u)
            finish(t - 1, 1 - u, None)
        with dve.Fori(1, NE // 2 - 1) as i:
            for u in (1, 0):
                hidden(2 * i + (2 - u), u)
                rows(2 * i + (3 - u), 1 - u)
                finish(2 * i + (1 - u), 1 - u, 16 * i)
        hidden(NE - 1, 1)
        finish(NE - 2, 0, 16 * (NE // 2 - 1))
        finish(NE - 1, 1, 16 * (NE // 2 - 1))
        dve.wait_ge(s("eid"), 1)
        pairs = dve.value_load(npair[0:1, 0:1], min_val=0, max_val=EXTRA // 2)
        with dve.Fori(0, EXTRA // 2) as i:
            with dve.If(pairs > i):
                for u in range(2):
                    rows(2 * i + (NE + u), u)
                    if u:
                        hidden(2 * i + NE, 0)
                hidden(2 * i + (NE + 1), 1)
                for u in range(2):
                    finish(2 * i + (NE + u), u, 16 * i + 16 * (NE // 2))

        for n in range(NT + 2):
            if n < NT:
                j, w = n, TW[n]
                dve.wait_ge(s("yw"), j + 1)
                a, b = yg[0:w, j, 0, :], yg[0:w, j, 1, :]
                stt(out=a, in0=b, scalar=w2[0:w, j:j + 1], in1=a, op0=ALU.mult, op1=ALU.add).then_inc(s("ysum"), 1)
            if 1 <= n <= NT:
                j, w = n - 1, TW[n - 1]
                dve.wait_ge(s("ygate"), j + 1)
                tt_(x2[0:w, j, :], x2[0:w, j, :], yg[0:w, j, 0, :], ALU.add).then_inc(s("x3"), 1)
            if n >= 2:
                j, w = n - 2, TW[n - 2]
                rstd(j, w, D, 2 * NT + 3 + j)
                if j >= 2:
                    dve.wait_ge(s_fst[j % 2], 16 * (j // 2))
                stt(out=fo[0:w, j % 2, :], in0=x2[0:w, j, :], scalar=stat[0:w, 56 + j:57 + j], in1=fgain[0:w, :],
                    op0=ALU.mult, op1=ALU.mult).then_inc(s("fo"), 1)

    @block.tensor
    def _(pe):
        t_ = nc.tensor
        mm = t_.matmul
        ident = cst("ident")

        def tr(out, in_):
            n = in_.shape[0]
            return mm(out, lhsT=in_, rhs=ident[0:n, 0:n], start=True, stop=True, is_transpose=True)

        pe.wait_ge(s("init"), 160)
        mm(ps[0:HEADS, 6, :], ctab33[:, :], ohp[:, 0:512], start=True, stop=True)
        mm(ps[0:HEADS, 7, 0:128], ctab33[:, :], ohp[:, 512:640], start=True, stop=True).then_inc(s("gp"), 1)

        pe.wait_ge(s("cs"), 1)
        for c in range(N_ADA):
            if c >= 2:
                pe.wait_ge(s("adae"), c - 1)
            out = ps[0:NC, c % 2, :]
            mm(out, cst("ones", 1)[:, 0:NC], adab[:, 512 * c:512 * (c + 1)], start=True, stop=False)
            wait_item(pe, IT_ADA + c)
            r = ring[(IT_ADA + c) % R1]
            for k in range(KD):
                ins = mm(out, cS[:, k, :], r[:, 512 * k:512 * (k + 1)], start=False, stop=k == KD - 1)
            ins.then_inc(s("ada"), 1)
            if c == 3:
                pe.wait_ge(s("bpad"), 1)
                for n in range(8):
                    b, q = n // 4, n % 4
                    if n >= 2:
                        pe.wait_ge(s("btTe"), n - 1)
                    for r_ in range(4):
                        ins = tr(ps[:, 2 + n % 2, P * r_:P * (r_ + 1)], bpad[b][:, 4 * q + r_, :])
                    ins.then_inc(s("btT"), 1)
        pe.wait_ge(s("btTe"), 8)

        for j in range(NT):
            w = TW[j]
            pe.wait_ge(s("h"), j + 1)
            if j >= 2:
                pe.wait_ge(s("hTa"), j - 1)
                pe.wait_ge(s("hTd"), j - 1)
            for half in range(2):
                for c in range(4):
                    k = 4 * half + c
                    ins = tr(ps[:, 2 + 2 * (j % 2) + half, w * c:w * (c + 1)], hb[0:w, j % 2, P * k:P * (k + 1)])
                ins.then_inc(s("hTp"), 1)

        pe.wait_ge(s("hTa"), NT)
        pe.wait_ge(s("hTd"), NT)
        pe.wait_ge(s("adae"), N_ADA)
        pe.wait_ge(s("gsb"), 1)
        pe.wait_ge(s("sq"), NT)
        zi = 0
        for it in range(N_WIN):
            i = IT_WIN + it
            wait_item(pe, i)
            r = ring[i % R1]
            if it == 2:
                for j in range(NT):
                    w = TW[j]
                    if j >= 2:
                        pe.wait_ge(s("ve"), j - 1)
                    for k in range(KD):
                        ins = mm(ps[0:w, 2 + j % 2, :], hT[:, k, tok(j)], r[:, 512 * k:512 * (k + 1)],
                                 start=k == 0, stop=k == KD - 1)
                    ins.then_inc(s("v"), 1)
                continue
            for c in range(4):
                if zi >= 2:
                    pe.wait_ge(s("za"), zi - 1)
                    pe.wait_ge(s("zd"), zi - 1)
                for n, out in enumerate((ps[:, zi % 2, 0:HALF], ps[:, 6 + zi % 2, 0:HALF])):
                    cols = slice(HALF * n, HALF * (n + 1))
                    for k in range(KD):
                        ins = mm(out, r[:, 512 * k + P * c:512 * k + P * (c + 1)], hT[:, k, cols],
                                 start=k == 0, stop=k == KD - 1)
                    ins.then_inc(s("z"), 1)
                zi += 1

        wait_item(pe, IT_OH)
        pe.wait_ge(s("padt"), 1)
        pe.wait_ge(s("ve"), NT)
        r = ring[IT_OH % R1]
        for b, (c0, c1) in enumerate(((0, 512), (512, DK))):
            for t in range(TDEC):
                ins = mm(ps[:, 2 + b, 0:c1 - c0], padT[:, t, :], r[0:BUCKETS + 1, DK * t + c0:DK * t + c1],
                         start=t == 0, stop=t == TDEC - 1)
        ins.then_inc(s("dbp"), 1)
        pe.wait_ge(s("za"), 12)
        pe.wait_ge(s("zd"), 12)
        for n in range(2):
            for t in range(STT):
                ins = mm(ps[:, 5 + n, NS * t:NS * (t + 1)], bt[n][:, t, :], uT[:, t // 4, SEQ:NTOK],
                         start=True, stop=True)
        ins.then_inc(s("buSp"), 1)

        NST = HEADS * QT
        pe.wait_ge(s("dbias"), 1)

        def scores(st):
            h, qt = divmod(st, QT)
            rows = slice(64 * (h % 2), 64 * (h % 2) + 64)
            if st >= 2:
                pe.wait_ge(s("P"), st - 1)
            m = P * (qt + 1)
            mm(ps[:, st % 2, 0:m], qkT[rows, h // 2, P * qt:m], qkT[rows, 4 + h // 2, 0:m], start=True, stop=False)
            pe.wait_ge(s_toep[h % 2], 16 * (h // 2 + 1))
            mm(ps[:, st % 2, 0:m], cst("flip"), toep[:, h % 2, SEQ - m:SEQ], start=False, stop=True)\
                .then_inc(s("S"), 1)

        def probs_t(st):
            qt = st % QT
            pe.wait_ge(s("P"), st + 1)
            if st >= 2:
                pe.wait_ge(s("ptr"), st - 1)
            for kt in range(qt + 1):
                ins = tr(ps[:, 2 + st % 2, P * kt:P * (kt + 1)], Sb[:, st % 2, P * kt:P * (kt + 1)])
            ins.then_inc(s("pt"), 1)

        def pv(st):
            h, qt = divmod(st, QT)
            pe.wait_ge(s("ptr"), st + 1)
            for kt in range(qt + 1):
                ins = mm(ps[:, 4 + qt, DH * h:DH * (h + 1)], PTs[:, st % 2, P * kt:P * (kt + 1)],
                         vrow[:, kt, DH * h:DH * (h + 1)], start=kt == 0, stop=kt == qt)
            ins.then_inc(s("pv"), 1)

        for st in range(NST + 2):
            if st < NST:
                scores(st)
            if 1 <= st <= NST:
                probs_t(st - 1)
            if st == 2:
                pe.wait_ge(s("buS"), 1)
            if st >= 2:
                pv(st - 2)

        def att_t(j):
            w = TW[j]
            pe.wait_ge(s("attn"), j + 1)
            if j >= 2:
                pe.wait_ge(s("attTe"), j - 1)
            bank = 2 + j % 2 if j < QT else 5
            for c in range(4):
                ins = tr(ps[:, bank, w * c:w * (c + 1)], att[0:w, j, P * c:P * (c + 1)])
            ins.then_inc(s("attT"), 1)

        pe.wait_ge(s("qbd"), 1)
        pe.wait_ge(s("att"), NST)

        def dec_item(m):
            g, c = divmod(m, 8)
            n4 = c % 4
            n = 4 * g + n4
            rows = slice(32 * n4, 32 * n4 + 32)
            wait_item(pe, IT_KV + m)
            r = ring[(IT_KV + m) % R1]
            if c < 4:
                if c == 0 and g:
                    pe.wait_ge(s("dSm"), g)
                for out, c0, c1 in ((ps[rows, 0, :], 0, 512), (ps[rows, 1, 0:CK - 512], 512, CK)):
                    for q in range(4):
                        mm(out, qbd[:, n, q, :], r[:, CK * q + c0:CK * q + c1], start=q == 0, stop=q == 3,
                           tile_position=(0, 32 * n4))
                for q in range(4):
                    ins = mm(ps[rows, 1, CK - 512:DK - 512], qbd[:, n, q, :], qkT[:, 4 + q, SEQ:NTOK],
                             start=q == 0, stop=q == 3, tile_position=(0, 32 * n4))
                ins.then_inc(s("dS"), 1)
            else:
                if c == 4:
                    pe.wait_ge(s("dPtd"), g + 1)
                    pe.wait_ge(s("dPta"), g + 1)
                    if g:
                        pe.wait_ge(s("dOe"), g)
                for b in range(CB):
                    mm(ps[rows, 4, :], dPT[:, b, rows], r[:, AW * b:AW * (b + 1)], start=b == 0, stop=False,
                       tile_position=(0, 32 * n4))
                mm(ps[rows, 4, :], dPT[0:NS, CB, rows], vrow[0:NS, QT, :], start=False, stop=True,
                   tile_position=(0, 32 * n4)).then_inc(s("dOp"), 1)

        def dec_probs_t(g):
            pe.wait_ge(s("dP"), g + 1)
            for b in range(CB):
                tr(ps[:, 2 + b // 4, P * (b % 4):P * (b % 4 + 1)], dP[:, P * b:P * (b + 1)])
            tr(ps[0:NS, 3, 3 * P:4 * P], dP[:, CK:DK]).then_inc(s("dPt"), 1)

        def s5_in(i):
            k, q = divmod(i, 4)
            if i >= 1:
                pe.wait_ge(s("buread"), i)
            for n in range(2):
                for r_ in range(4):
                    ins = mm(ps[:, 5 + n, CH * r_:CH * (r_ + 1)], bt[n][:, 4 * q + r_, :],
                             uT[:, q, CH * k:CH * (k + 1)], start=True, stop=True)
            ins.then_inc(s("bu"), 1)

        def s5_out(i):
            k, q = divmod(i, 4)
            pe.wait_ge(s("hout"), i + 2)
            if q == 0:
                pe.wait_ge(s("yread"), k + 1)
            for r_ in range(4):
                for n, a in enumerate((hr, hi)):
                    ins = mm(ps[32 * r_:32 * r_ + 32, 7, CH * q:CH * (q + 1)], ct[n][:, 4 * q + r_, :],
                             a[i % 2][:, r_, :], start=n == 0, stop=n == 1, tile_position=(0, 32 * r_))
            ins.then_inc(s("yp"), 1)

        def s5_glu(n, w):
            pe.wait_ge(s("gel"), n + 1)
            for a in range(2):
                for q in range(4):
                    ins = mm(ps[:, 2 + a, w * q:w * (q + 1)], glu[:, a, q, :], y2[:, q, 0:w], start=True, stop=True)
            ins.then_inc(s("glut"), 1)

        def s5_sum(n, w):
            pe.wait_ge(s("gsq"), n + 1)
            for q in range(4):
                ins = mm(ps[0:w, 2, 0:1], yd[:, q, 0:w], cst("ones")[:, 0:1], start=q == 0, stop=q == 3)
            ins.then_inc(s("ssp"), 1)

        pe.wait_ge(s("hout"), 1)
        hs = [a[0][:, :, :].rearrange("p a b -> p (a b)") for a in (hr, hi)]
        for t in range(STT):
            r_, q = t % 4, t // 4
            for n in range(2):
                ins = mm(ps[32 * r_:32 * r_ + 32, 7, NS * q:NS * (q + 1)], ct[n][:, t, :], hs[n][:, NS * t:NS * (t + 1)],
                         start=n == 0, stop=n == 1, tile_position=(0, 32 * r_))
        ins.then_inc(s("yp"), 1)
        for i in range(16):
            s5_in(i)
            if i >= 2:
                s5_out(i - 2)
            if i in (4, 12):
                pe.wait_ge(s("gluo"), 1 if i == 4 else 3)
                dec_probs_t(i // 8)
            dec_item(i)
            if i == 0:
                for j in range(QT):
                    att_t(j)
            if i == 2:
                pe.wait_ge(s("attTe"), QT)
                pe.wait_ge(s("glul"), 32)
                s5_glu(0, NS)
            if i in (6, 10, 14):
                s5_glu(i // 4, CH)
            if i == 3:
                s5_sum(0, NS)
            if i in (7, 11, 15):
                s5_sum(i // 4, CH)

        def wo(j, half):
            w = TW[j]
            if j:
                pe.wait_ge((s("woa"), s("wog"))[half], j)
            for n in range(2):
                wait_item(pe, IT_WO + n)
                r = ring[(IT_WO + n) % R1]
                for k in range(4 * half, 4 * half + 4):
                    ins = mm(ps[0:w, 2 * half + n, :], mixT[:, k, tok(j)], r[:, 512 * k:512 * (k + 1)],
                             start=k % 4 == 0, stop=k % 4 == 3)
            ins.then_inc((s("woA"), s("woS"))[half], 1)

        pe.wait_ge(s("dSm"), 2)
        s5_out(14)
        wo(0, 0)
        s5_out(15)
        pe.wait_ge(s("dOe"), 2)
        for g in range(2):
            ins = mm(ps[0:NS, 4, :], cst("toksel")[:, NS * g:NS * (g + 1)], dO[:, g, :], start=g == 0, stop=g == 1)
        ins.then_inc(s("attSp"), 1)
        att_t(QT)
        s5_glu(4, CH)
        s5_sum(4, CH)

        pe.wait_ge(s("attTe"), NT)
        pe.wait_ge(s("gluo"), NT)

        def h2_t(j):
            w = TW[j]
            pe.wait_ge(s("h"), NT + j + 1)
            if j:
                pe.wait_ge(s("hTa"), NT + j)
                pe.wait_ge(s("hTd"), NT + j)
            for half in range(2):
                for c in range(4):
                    k = 4 * half + c
                    ins = tr(ps[:, 6 + half, w * c:w * (c + 1)], h2[0:w, j % 2, P * k:P * (k + 1)])
                ins.then_inc(s("hTp"), 1)

        def logits(j):
            w = TW[j]
            pe.wait_ge(s("hTa"), NT + j + 1)
            pe.wait_ge(s("hTd"), NT + j + 1)
            if j == 0:
                pe.wait_ge(s("mod3"), 112)
            out = ps[0:w, 4, 20 * j:20 * j + 20]
            mm(out, cst("ones", 1)[:, 0:w], rb[:, :], start=True, stop=False)
            for k in range(KD):
                ins = mm(out, h2T[:, k, tok(j)], rw[:, k, :], start=False, stop=k == KD - 1)
            ins.then_inc(s("lg"), 1)

        for j in range(NT):
            for half in range(2):
                if j or half:
                    wo(j, half)
            if j:
                h2_t(j - 1)
                logits(j - 1)
        h2_t(NT - 1)
        logits(NT - 1)

        pe.wait_ge(s("rM"), 1)
        for j in range(NT):
            for j2 in range(j + 1):
                mm(ps[:, 0, NE * j:NE * (j + 1)], cst("tri") if j2 == j else cst("ones"), M[:, j2, :],
                   start=j2 == 0, stop=j2 == j)
        for j in range(NT):
            ins = mm(ps[:, 1, 0:NE], cst("ones"), M[:, j, :], start=j == 0, stop=j == NT - 1)
        ins.then_inc(s("posp"), 1)
        pe.wait_ge(s("oneh"), 2)
        for k in range(2):
            for j in range(NT):
                ins = mm(ps[:, 2, 0:NTILE], slot1h[:, k, j, :], tt[k][:, j, :], start=k + j == 0,
                         stop=(k, j) == (1, NT - 1))
        ins.then_inc(s("idxp"), 1)

        def rows_t(t, u, wait_gather):
            pe.wait_ge(s_xg[u], wait_gather)
            for c in range(KD):
                ins = tr(ps[:, 4 + c // 4, P * (c % 4):P * (c % 4 + 1)], xg[:, u, P * c:P * (c + 1)])
            ins.then_inc(s("xgp"), 1)

        def weights(w, u, turn):
            pe.wait_ge(efull[3 * u + w], 16 * turn)
            return ering[3 * u + w]

        def half_in(t, u, w, turn, old=True):
            if w == 0:
                pe.wait_ge(s("xga"), t + 1)
                pe.wait_ge(s("xgd"), t + 1)
                if old:
                    pe.wait_ge(s("aTe"), t - 1)
            r = weights(w, u, turn)
            for k in range(KD):
                ins = mm(ps[:, 2 * w + u, :], xgT[:, u, k, :], r[:, 512 * k:512 * (k + 1)],
                         start=k == 0, stop=k == KD - 1)
            ins.then_inc(s("egate") if w == 0 else s("eup"), 1)

        def hidden_t(t, u):
            pe.wait_ge(s("ahid"), t + 1)
            for c in range(4):
                ins = tr(ps[:, u, P * c:P * (c + 1)], a_t[:, u, P * c:P * (c + 1)])
            ins.then_inc(s("aTp"), 1)

        def down(t, u, turn, old=True):
            pe.wait_ge(s("aTe"), t + 1)
            if old:
                pe.wait_ge(s("eya"), t)
                pe.wait_ge(s("eyd"), t)
            r = weights(2, u, turn)
            for n in range(2):
                for c in range(4):
                    ins = mm(ps[:, 6 + n, :], aT[:, u, c, :], r[:, D * c + 512 * n:D * c + 512 * (n + 1)],
                             start=c == 0, stop=c == 3)
            ins.then_inc(s("ey"), 1)

        pe.wait_ge(s("gidx"), 1)
        rows_t(0, 0, 16)
        half_in(0, 0, 0, 1, old=False)
        half_in(0, 0, 1, 1)
        rows_t(1, 1, 16)
        for t in (1, 2):
            u = t % 2
            half_in(t, u, 0, 1 + t // 2, old=t >= 2)
            hidden_t(t - 1, 1 - u)
            half_in(t, u, 1, 1 + t // 2)
            rows_t(t + 1, 1 - u, 32)
            down(t - 1, 1 - u, 1, old=t >= 2)
        with pe.Fori(1, NE // 2 - 1) as i:
            for u in (1, 0):
                t = 2 * i + (2 - u)
                half_in(t, u, 0, i + (2 - u))
                hidden_t(2 * i + (1 - u), 1 - u)
                half_in(t, u, 1, i + (2 - u))
                rows_t(2 * i + (3 - u), 1 - u, 16 * i + 32)
                down(2 * i + (1 - u), 1 - u, i + 1)
        half_in(NE - 1, 1, 0, NE // 2)
        hidden_t(NE - 2, 0)
        half_in(NE - 1, 1, 1, NE // 2)
        down(NE - 2, 0, NE // 2)
        hidden_t(NE - 1, 1)
        down(NE - 1, 1, NE // 2)
        pe.wait_ge(s("eid"), 1)
        pairs = pe.value_load(npair[0:1, 0:1], min_val=0, max_val=EXTRA // 2)
        with pe.Fori(0, EXTRA // 2) as i:
            with pe.If(pairs > i):
                t, turn = 2 * i + NE, i + (NE // 2 + 1)
                rows_t(t, 0, 16 * i + 16 * (NE // 2 + 1))
                half_in(t, 0, 0, turn)
                half_in(t, 0, 1, turn)
                rows_t(t + 1, 1, 16 * i + 16 * (NE // 2 + 1))
                half_in(t + 1, 1, 0, turn)
                hidden_t(t, 0)
                half_in(t + 1, 1, 1, turn)
                down(t, 0, turn)
                hidden_t(t + 1, 1)
                down(t + 1, 1, turn)


def kernel(**inputs):
    import concourse.bacc as bacc
    from concourse.bass_utils import run_bass_kernel_spmd

    x = {k: np.asarray(v) for k, v in inputs.items()}
    nc = bacc.Bacc("TRN2", target_bir_lowering=False, num_devices=1)

    def state(a):
        return np.ascontiguousarray(a.reshape((STT, P) + a.shape[2:]).swapaxes(0, 1))

    def channel(a):
        return np.ascontiguousarray(a.reshape(4, P).T)

    def blocks(a, n):
        g, r, c = a.shape
        out = np.zeros((g // n, n, r, n, c), a.dtype)
        for i in range(n):
            out[:, i, :, i, :] = a.reshape(g // n, n, r, c)[:, i]
        return out.reshape(g // n, n * r, n * c)

    c_all = np.concatenate([x["c_prompt"], x["c_sample"]])
    par = [state(x["ssm_a_re"][0]), state(x["ssm_a_im"][0]),
           state(np.broadcast_to(x["ssm_log_dt"][0][:, None], (GRP, ST))),
           channel(x["ssm_d"][0].reshape(-1)), channel(x["attn_out_g"][0]), channel(x["ssm_out_g"][0]),
           state(x["ssm_b_re"][0]).reshape(P, -1), state(x["ssm_b_im"][0]).reshape(P, -1)]
    ck = x["cache_k"][0][:, CROWS]
    cv = x["cache_v"][0][:, CROWS]
    A = {
        "zero": np.zeros(D, np.float32),
        "const": CONST,
        "par": np.concatenate(par, axis=1),
        "cT": c_all.reshape(NC, KD, P).transpose(2, 1, 0),
        "tab33": np.concatenate([x["rel_bias"], np.ones((1, HEADS), np.float32)]),
        "oh_prompt": OH_PROMPT, "oh_decode": OH_DECODE,
        "ct_re": blocks(x["ssm_c_re"][0].transpose(0, 2, 1), 2).transpose(1, 0, 2),
        "ct_im": blocks(x["ssm_c_im"][0].transpose(0, 2, 1), 2).transpose(1, 0, 2),
        "glu_a": blocks(x["glu_a"][0], 8).transpose(1, 0, 2),
        "glu_b": blocks(x["glu_b"][0], 8).transpose(1, 0, 2),
        "ada_w": x["ada_w"][0], "ada_b": x["ada_b"],
        "norm1_g": x["norm1_g"][0], "norm2_g": x["norm2_g"][0], "final_g": x["final_norm_g"],
        "w_in": x["w_in"][0], "w_out": x["w_out"][0],
        "x": np.concatenate([x["x_prompt"][0], x["x_sample"].reshape(NS, D)]),
        "cache_k": ck.reshape(NSEQ, CK, 4, P).transpose(0, 3, 2, 1).reshape(NSEQ, P, 4 * CK),
        "cache_v": cv.reshape(NSEQ, CB, P, AW).transpose(0, 2, 1, 3).reshape(NSEQ, P, CB * AW),
        "h0_re": state(x["state_ssm_re"][0].transpose(1, 2, 0)), "h0_im": state(x["state_ssm_im"][0].transpose(1, 2, 0)),
        "router_w": np.concatenate([x["router_g_w"][0], x["router_e_w"][0].transpose(1, 0, 2).reshape(D, NE)], axis=1)
        .reshape(KD, P, NG + NE).transpose(1, 0, 2),
        "router_b": np.concatenate([x["router_g_b"][0], x["router_e_b"][0].reshape(-1)])[None, :],
        "w_gate": x["w_gate"][0].reshape(NE, D, FE), "w_up": x["w_up"][0].reshape(NE, D, FE),
        "w_down": x["w_down"][0].reshape(NE, FE, D),
    }
    A = {k: np.ascontiguousarray(a) for k, a in A.items()}
    I = {k: nc.dram_tensor("in_" + k, a.shape, mybir.dt.from_np(a.dtype), kind="ExternalInput").ap()
         for k, a in A.items()}
    shapes = {"y": (NTOK, D), "kT": (AW, NTOK), "v": (NTOK, AW), "ssm_p": (P, 2, STT), "ssm_s": (P, 2 * STT * NSEQ)}
    O = {k: nc.dram_tensor("out_" + k, shp, F32, kind="ExternalOutput").ap() for k, shp in shapes.items()}
    build(nc, I, O)
    r = run_bass_kernel_spmd(nc, [{"in_" + k: a for k, a in A.items()}], core_ids=[0]).results[0]
    y, kT, v, sp, ss = (np.asarray(r["out_" + k]) for k in ("y", "kT", "v", "ssm_p", "ssm_s"))
    k = kT.T
    heads = lambda a, lead: np.ascontiguousarray(a.reshape(lead + (HEADS, DH)))
    sp = sp.transpose(1, 2, 0).reshape(2, 1, 1, GRP, ST)
    ss = ss.reshape(P, 2, STT, NSEQ).transpose(1, 3, 2, 0).reshape(2, 1, NSEQ, GRP, ST)
    c = np.ascontiguousarray
    return (c(y[:SEQ].reshape(1, SEQ, D)), c(y[SEQ:].reshape(NSEQ, TDEC, D)),
            heads(k[:SEQ], (1, 1, SEQ)), heads(v[:SEQ], (1, 1, SEQ)),
            heads(k[SEQ:], (1, NSEQ, TDEC)), heads(v[SEQ:], (1, NSEQ, TDEC)),
            c(sp[0]), c(sp[1]), c(ss[0]), c(ss[1]))
```

```python
from contextlib import ExitStack

import numpy as np

import concourse.bass as bass
from concourse import mybir

F32 = mybir.dt.float32
U32 = mybir.dt.uint32
I32 = mybir.dt.int32
ALU = mybir.AluOpType
ACT = mybir.ActivationFunctionType
AX = mybir.AxisListType

P = 128
D = 1024
KD = D // P
SEQ = 512
NSEQ, TDEC = 8, 4
NS = NSEQ * TDEC
NTOK = SEQ + NS
HALF = NTOK // 2
TW = [P] * (SEQ // P) + [NS]
NT = len(TW)
QT = SEQ // P
ORDER3 = (0, 1, 2, QT, 3)
HEADS, DH = 8, 64
AW = HEADS * DH
NC = NSEQ + 1
PAST = 2048
WINDOWS, DILATIONS = (128, 512, 2048), (1, 4, 16)
BUCKETS, MAX_EXACT = 32, 16
GRP, GC, ST = 32, 16, 64
STT = GRP * ST // P
CH = 128
NG, EPG = 4, 4
NE = NG * EPG
FE = 512
EPS = 1e-6
EXTRA = 8
NTILE = NE + EXTRA
NEG = -1.0e30

CROWS = [r for r in range(PAST) if r >= PAST - WINDOWS[1] or r % DILATIONS[2] < TDEC]
CK = len(CROWS)
CB = CK // P
DK = CK + NS
SLOT = 4096
R1 = 4
R2 = 6
N_ADA, N_WIN = 12, 4
IT_ADA, IT_WIN = 0, N_ADA
IT_OH = IT_WIN + N_WIN
IT_KV = IT_OH + 1
IT_WO = IT_KV + 2 * NSEQ
N_ITEMS = IT_WO + 2


def _bucket(dist):
    d = np.maximum(dist, MAX_EXACT).astype(np.float32)
    log_part = MAX_EXACT + (np.log(d / np.float32(MAX_EXACT)) / np.float32(np.log(PAST / MAX_EXACT))
                            * np.float32(BUCKETS - MAX_EXACT)).astype(np.int32)
    return np.where(dist < MAX_EXACT, dist, np.minimum(log_part, BUCKETS - 1))


def _distance_rows(dist):
    n = np.zeros(dist.shape, np.int64)
    for w, r in zip(WINDOWS, DILATIONS):
        n += (dist >= 0) & (dist <= w) & (dist % r == 0)
    out = np.zeros((BUCKETS + 1,) + dist.shape, np.float32)
    b = _bucket(np.maximum(dist, 0))
    for i in range(BUCKETS):
        out[i] = (b == i) & (n > 0)
    out[BUCKETS] = np.where(n > 0, np.log(np.maximum(n, 1)), NEG)
    return out


def _constants():
    p = np.arange(P)
    blocks = {}
    blocks["ident"] = np.eye(P)
    blocks["flip"] = np.eye(P)[::-1]
    blocks["tri"] = (p[:, None] < p[None, :])
    blocks["ones"] = np.ones((P, P))
    blocks["iotaneg"] = np.broadcast_to(-np.arange(P), (P, P))
    head = (p % 32) // TDEC
    blocks["headsel"] = head[:, None] == (np.arange(AW) // DH)[None, :]
    nm = np.zeros((P, 2, NS))
    ts = np.zeros((P, 2, NS))
    for g in range(2):
        seq = 4 * g + p // 32
        tok = np.arange(NS)
        nm[:, g] = np.where(seq[:, None] == tok[None, :] // TDEC, 0.0, NEG)
        ts[:, g] = (seq * TDEC + p % TDEC)[:, None] == tok[None, :]
    blocks["newmask"] = nm.reshape(P, -1)
    blocks["toksel"] = ts.reshape(P, -1)
    blocks["valid"] = (p[:, None] < np.array(TW)[None, :])
    blocks["tokv"] = (p[:, None] + P * np.arange(NT)[None, :]) * blocks["valid"]
    row = lambda a: np.broadcast_to(np.asarray(a).reshape(1, -1), (P, np.asarray(a).size))
    blocks["first"] = row([4, 3, 2, 1])
    blocks["ebase"] = row(np.arange(NE) * P)
    blocks["exbase"] = row((NE - 1 - np.arange(NE)) * P)
    blocks["eidx"] = row(np.arange(NE))
    blocks["jidx"] = row(np.arange(EXTRA))
    blocks["tbase"] = row(np.arange(NTILE) * P)
    cols, at = {}, 0
    for k, v in blocks.items():
        blocks[k] = np.asarray(v, np.float32)
        cols[k] = (at, at + blocks[k].shape[1])
        at += blocks[k].shape[1]
    return np.concatenate(list(blocks.values()), axis=1), cols


CONST, CCOL = _constants()
_dist0 = SEQ - 1 - np.arange(640)
OH_PROMPT = _distance_rows(_dist0)
_t = np.arange(TDEC)[:, None]
_cached = PAST + _t - np.array(CROWS)[None, :]
_new = np.broadcast_to(_t - (np.arange(NS) % TDEC)[None, :], (TDEC, NS))
OH_DECODE = _distance_rows(np.concatenate([_cached, _new], axis=1)).reshape(BUCKETS + 1, TDEC * DK)

PC = {}
_at = 0
for _k, _n in (("a_re", 16), ("a_im", 16), ("log_dt", 16), ("dskip", 4), ("attg", 4), ("ssmg", 4),
               ("b_re", 256), ("b_im", 256)):
    PC[_k] = (_at, _at + _n)
    _at += _n
NPAR = _at


class Order:

    def __init__(self, eng, sem, base=0):
        self.eng, self.sem, self.n = eng, sem, base

    def __call__(self, ins):
        ins.then_inc(self.sem, 1)
        self.n += 1
        self.eng.wait_ge(self.sem, self.n)


def build(nc, I, O):
    ctx = ExitStack()
    with ctx:
        _build(nc, I, O, ctx)


def _build(nc, I, O, ctx):
    B0 = 16512

    def at(name, shape, off, dt=F32):
        assert off % 32 == 0 and B0 + off + 4 * int(np.prod(shape[1:])) <= 229368, name
        return nc.alloc_sbuf_tensor_at(name, shape, dt, offset=B0 + off)

    def sem(name):
        return ctx.enter_context(nc.semaphore(name))

    RING, E, C, SM = 0, 65536, 98304, 98304 + 6656
    HT, QK, V, U = 106496, 123904, 141312, 151552
    TAB, W = 160256, 176640

    ring = [at(f"ring{i}", [P, SLOT], RING + 16384 * i) for i in range(R1)]
    bt = [at("bt_re", [P, STT, P], E), at("bt_im", [P, STT, P], E + 8192)]
    ct = [at("ct_re", [P, STT, 32], E + 16384), at("ct_im", [P, STT, 32], E + 18432)]
    s5_at = [[E + 20480 + 2048 * i for i in range(6)],
             [QK + 2048 * i for i in range(4)] + [V + 2048 * i for i in range(2)]]
    ctn = at("ct_re_negated", [P, STT, 32], V + 4096)
    xr, xi, gr, gi, hr, hi = [[at(f"s5_{n}{b}", [P, 4, CH], s5_at[b][i]) for b in range(2)]
                              for i, n in enumerate(("xr", "xi", "gr", "gi", "hr", "hi"))]
    ering = [at(f"ering{i}", [P, SLOT], RING + 16384 * i) for i in range(R2)]

    NCC = CONST.shape[1]
    assert NCC * 4 <= 6656, NCC
    const = at("const", [P, NCC], C)

    def cst(name, rows=P):
        a, b = CCOL[name]
        return const[0:rows, a:b]

    sm_at = [SM]

    def small(name, cols, rows=P, dt=F32):
        t = at(name, [rows, cols], sm_at[0], dt)
        sm_at[0] += (4 * cols + 31) // 32 * 32
        assert sm_at[0] <= HT, name
        return t

    mag, cth, sth = small("mag", 16), small("cth", 16), small("sth", 16)
    ctab33 = small("tab33", 8, BUCKETS + 1)
    car, cai = small("carry_re", 16), small("carry_im", 16)
    las, lai = small("last_re", 16), small("last_im", 16)
    gains = small("gains", 12)
    ctmp = small("ctmp", 16)
    c128, s128 = small("c128", 16), small("s128", 16)
    stat = small("stat", 64)
    dstat = small("dstat", 64)
    epst = stat[:, 63:64]
    rssm = small("rssm", 8)
    nbias = small("nbias", 2 * NS)

    hT = at("hT", [P, KD, NTOK], HT)
    mixT = at("mixT", [P, KD, NTOK], HT)
    h2T = at("h2T", [P, KD, NTOK], HT)
    modsb = at("modsb", [P, N_ADA, P], E + 20480)
    rot = at("rotation_powers", [P, 6, 16], E + 31232)
    cS = at("silu_c", [P, KD, 32], E + 31616)
    ohp = at("oh_prompt", [BUCKETS + 1, 640], E + 28672)
    gsb = at("gsb", [HEADS, 640], W + 33632)
    toep = at("toeplitz", [P, 2, SEQ], HT)
    qkT = at("qkT", [P, 8, NTOK], QK)
    modrow = at("modrow", [P, N_ADA + 4, P], QK)
    vrow = at("vrow", [P, NT, AW], V)
    uT = at("uT", [P, 4, NTOK], U)
    cosT, sinT = at("cosT", [P, STT, CH], TAB), at("sinT", [P, STT, CH], TAB + 8192)

    xt = at("xt", [P, NT, D], QK + 8192)
    hb = at("hb", [P, 2, D], W + 8192)
    par = at("par", [P, NPAR], W + 8192)
    bbr, bbi = at("bbr", [P, STT, GC], W + 8192 + 2304), at("bbi", [P, STT, GC], W + 8192 + 3328)
    bt1, bt2 = at("bt1", [P, STT, GC], W + 8192 + 4352), at("bt2", [P, STT, GC], W + 8192 + 5376)
    pr = at("pr", [P, 20, 16], W + 8192 + 6400)
    assert NPAR * 4 <= 2304 and 6400 + 1280 <= 8192
    modP, modS = at("modP", [P, 2, D], W + 16384), at("modS", [NS, 2, D], W + 24576)
    bpad = [at("bpad_re", [P, STT, P], W + 16384), at("bpad_im", [P, STT, P], W + 24576)]
    cT, cE = [at(n, [P, KD, NC], W + 32768 + 288 * i) for i, n in enumerate(("cT", "cE"))]
    dt1, dt2 = at("dt1", [P, STT, CH // 2], W), at("dt2", [P, STT, CH // 2], W + 4096)

    att = at("att", [P, NT, AW], W)
    dPT = at("dPT", [P, 8, P], W)
    dO = at("dO", [P, 2, AW], W + 4096)
    Sb = at("Sb", [P, 2, SEQ], W + 10240)
    qbd = at("qbd", [P, NSEQ, 4, 32], W + 32000)
    PTs = at("PTs", [P, 2, SEQ], W + 14336)
    glu = at("glu", [P, 2, 4, P], W + 14336)
    dbias = at("dbias", [P, DK], W + 18432)
    dP = at("dP", [P, DK], W + 22144)
    th = at("gelu_th", [P, 4, CH], W + 25856)
    ta, tb = at("s5_ta", [P, 4, CH], W + 27904), at("s5_tb", [P, 4, CH], W + 29952)
    yd, y2 = at("gelu_yd", [P, 4, CH], W + 10240), at("gelu_y2", [P, 4, CH], W + 12288)
    states = at("sample_states", [P, 2 * STT * NSEQ], W + 22144)
    padT = at("padT", [BUCKETS + 1, 4, P], W + 27904)
    x2 = at("x2", [P, NT, D], QK)
    mod3P = at("mod3P", [P, 3, D], QK + 20480)
    mod3S = at("mod3S", [NS, 3, D], TAB)
    xt3 = at("xt3", [P, 2, D], W)
    h2 = at("h2", [P, 2, D], W + 8192)
    pt1 = at("pt1", [P, 2, D], W + 16384)
    spread = at("sample_spread", [P, 256], W + 24576)
    rw = at("rw", [P, KD, 20], W + 28672)
    rb = at("rb", [1, 20], W + 29312)
    rt_at = [TAB + 12288]

    def rt(name, shape, dt=F32):
        n = int(np.prod(shape[1:])) * 4
        if rt_at[0] <= W < rt_at[0] + n:
            rt_at[0] = W + 29440
        t = at(name, shape, rt_at[0], dt)
        rt_at[0] += (n + 31) // 32 * 32
        return t

    lg = rt("logits", [P, NT, 20])
    g4a, g4b, g4c = [rt(n, [P, NT, 4]) for n in ("g4a", "g4b", "g4c")]
    ghot = rt("ghot", [P, NT, 4])
    gmax, gsum = rt("gmax", [P, NT]), rt("gsum", [P, NT])
    e16 = rt("e16", [P, NT, NE])
    esel, o1, o2 = [rt(n, [P, NT, 4]) for n in ("esel", "o1", "o2")]
    v1, v2, w1, w2 = [rt(n, [P, NT]) for n in ("v1", "v2", "w1", "w2")]
    E12, M = rt("E12", [P, 2, NT, NE]), rt("M", [P, NT, NE])
    pos = rt("pos", [P, NT, NE])
    cnt, nx, xb, nx2 = [rt(n, [P, NE]) for n in ("cnt", "nx", "xb", "nx2")]
    slot = rt("slotrow", [P, NT, NE])
    sl, ms = rt("token_slot", [P, 2, NT]), rt("in_tile", [P, 2, NT])
    td, tt, tm = [rt(n, [P, 2, NT, NTILE]) for n in ("tile_dist", "tile_tok", "tile_tmp")]
    slot1h = at("slot1h", [P, 2, NT, P], HT + 8192)
    gidx = rt("gidx", [P, NTILE], U32)
    sidx = rt("sidx", [P, 2, NT], U32)
    eid8, eid9 = rt("eid8", [P, EXTRA, NE]), rt("eid9", [P, EXTRA, NE])
    eid = rt("eid", [P, EXTRA])
    eidi = rt("eidi", [P, EXTRA], I32)
    xtot, npair = rt("extra_tiles", [P, 1]), rt("extra_pairs", [P, 1], I32)
    xg = at("xg", [P, 2, D], W)
    xgT = at("xgT", [P, 2, KD, P], W + 8192)
    a_s = at("a_s", [P, 2, FE], W + 16384)
    a_t = at("a_t", [P, 2, FE], W + 20480)
    aT = at("aT", [P, 2, 4, P], W + 24576)
    ysb = at("ysb", [P, 2, D], HT)
    fgain = at("fgain", [P, D], QK + 20480)
    yg = at("yg", [P, NT, 2, D], RING)
    fo = at("fo", [P, NT, D], RING + 40960)

    ps = nc.alloc_psum_tensor("ps", [P, 8, 512], F32)

    mod_d = nc.dram_tensor("mod_d", [N_ADA, P, P], F32).ap()
    g_d = nc.dram_tensor("g_d", [HEADS, 640], F32).ap()
    h2_d = nc.dram_tensor("h2_d", [NTOK, D], F32).ap()
    y_d = nc.dram_tensor("y_d", [NTILE * P, D], F32).ap()

    made = {}

    def s(name):
        if name not in made:
            made[name] = sem("s_" + name)
        return made[name]

    rfull = [sem(f"ring_full{i}") for i in range(R1)]
    efull = [sem(f"ering_full{i}") for i in range(R2)]
    s_modst = [sem(f"mod_stored{i}") for i in range(3)]
    s_toep = [sem(f"toep_full{i}") for i in range(2)]
    s_x3 = [sem(f"x3_full{i}") for i in range(2)]
    s_xg = [sem(f"xg_full{i}") for i in range(2)]
    s_yst = [sem(f"y_stored{i}") for i in range(2)]
    s_yg = [sem(f"yg_full{j}") for j in range(NT)]
    s_h2st = [sem(f"h2_stored{i}") for i in range(2)]

    def mod_rows(n, first):
        return bass.AP(mod_d.tensor, 2 * first * P * P, [[0, P], [P * P, 2 * n], [32 * P, 4], [1, P]])

    def mod_rows_seq(n, first):
        return bass.AP(mod_d.tensor, P + 2 * first * P * P, [[P, NSEQ], [P * P, 2 * n], [32 * P, 4], [1, P]])

    def wait_item(eng, i):
        eng.wait_ge(rfull[i % R1], 16 * (i // R1 + 1))

    def used(eng, i):
        if i < IT_WIN:
            eng.wait_ge(s("ada"), i + 1)
        elif i < IT_OH:
            it = i - IT_WIN
            if it == 2:
                eng.wait_ge(s("v"), NT)
            else:
                eng.wait_ge(s("z"), 8 * (it + 1 - (it > 2)))
        elif i == IT_OH:
            eng.wait_ge(s("dbp"), 1)
        elif i < IT_WO:
            g, c = divmod(i - IT_KV, 8)
            eng.wait_ge(s("dS") if c < 4 else s("dOp"), 4 * g + c % 4 + 1)
        else:
            eng.wait_ge(s("woS"), NT)

    def tok(j):
        return slice(j * P, j * P + TW[j])

    block = ctx.enter_context(nc.Block())

    @block.sync
    def _(sp):
        ada_v = I["ada_w"].rearrange("(k p) n -> p k n", p=P)
        win_v = I["w_in"].rearrange("(k p) n -> p k n", p=P)
        wo_v = I["w_out"].rearrange("(k p) n -> p k n", p=P)
        sp.dma_start(cT[:, :, :], I["cT"]).then_inc(s("cld"), 16)
        sp.dma_start(ring[0][:, :].rearrange("p (k n) -> p k n", k=KD), ada_v[:, :, 0:512]).then_inc(rfull[0], 16)
        for dst, srcd in ((par[:, :], I["par"]), (const[:, :], I["const"]),
                          (ctab33[:, :], I["tab33"]), (ohp[:, :], I["oh_prompt"]),
                          (ct[0][:, :, :], I["ct_re"]), (ct[1][:, :, :], I["ct_im"]),
                          *((modrow[32 * j:32 * j + 32, :, :].rearrange("p a b -> p (a b)"),
                             I["modrow"][j].partition_broadcast(32)) for j in range(4))):
            sp.dma_start(dst, srcd).then_inc(s("init"), 16)

        def item(i):
            if i >= R1:
                used(sp, i - R1)
            r = ring[i % R1]
            if i < IT_WIN:
                c = i - IT_ADA
                dst, src = r[:, :].rearrange("p (k n) -> p k n", k=KD), ada_v[:, :, 512 * c:512 * (c + 1)]
            elif i < IT_OH:
                c = i - IT_WIN
                dst, src = r[:, :].rearrange("p (k n) -> p k n", k=KD), win_v[:, :, 512 * c:512 * (c + 1)]
            elif i == IT_OH:
                dst, src = r[0:BUCKETS + 1, 0:TDEC * DK], I["oh_decode"]
            elif i < IT_WO:
                g, m = divmod(i - IT_KV, 8)
                n = 4 * g + m % 4
                dst, src = r[:, 0:4 * CK], I["cache_v" if m >= 4 else "cache_k"][n]
            else:
                c = i - IT_WO
                dst, src = r[:, :].rearrange("p (k n) -> p k n", k=KD), wo_v[:, :, 512 * c:512 * (c + 1)]
            sp.dma_start(dst, src).then_inc(rfull[i % R1], 16)

        item(1)
        sp.dma_start(xt[:, 0:QT, :], I["x"][0:SEQ, :].rearrange("(j p) n -> p j n", p=P)).then_inc(s("x"), 16)
        sp.dma_start(xt[0:NS, QT, :], I["x"][SEQ:NTOK, :]).then_inc(s("x"), 16)
        for i in range(2, 7):
            item(i)
        sp.wait_ge(s_modst[0], 64)
        sp.wait_ge(s("btT"), 8)
        sp.dma_start(modP[:, :, :].rearrange("p v (c j n) -> p (v c) j n", c=2, j=4),
                     mod_rows(2, 0)).then_inc(s("modld"), 16)
        for t in range(TDEC):
            sp.dma_start(modS[t:NS:TDEC, :, :].rearrange("p v (c j n) -> p (v c) j n", c=2, j=4),
                         mod_rows_seq(2, 0)).then_inc(s("modld"), 16)
        for i in range(7, IT_OH):
            item(i)
        for i in range(IT_OH, IT_KV + 2):
            item(i)
        sp.wait_ge(s("gst"), 16)
        sp.wait_ge(s("z"), 24)
        for h in range(HEADS):
            if h == 2:
                item(IT_KV + 2)
                item(IT_KV + 3)
            if h >= 2:
                sp.wait_ge(s("S"), QT * (h - 1))
            sp.dma_start(toep[:, h % 2, :], bass.AP(g_d.tensor, 640 * h, [[1, P], [1, SEQ]]))\
                .then_inc(s_toep[h % 2], 16)
        for i in range(IT_KV + 4, N_ITEMS):
            item(i)
        sp.wait_ge(s("gluo"), QT + 1)
        sp.wait_ge(s("dOp"), NSEQ)
        sp.wait_ge(s("attS"), 1)
        sp.wait_ge(s("kvst"), 48)
        for b in range(3):
            sp.wait_ge(s_modst[b], 64)
        sp.dma_start(mod3P[:, :, :].rearrange("p v (c j n) -> p (v c) j n", c=2, j=4),
                     mod_rows(3, 2)).then_inc(s("mod3"), 16)
        for t in range(TDEC):
            sp.dma_start(mod3S[t:NS:TDEC, :, :].rearrange("p v (c j n) -> p (v c) j n", c=2, j=4),
                         mod_rows_seq(3, 2)).then_inc(s("mod3"), 16)
        sp.wait_ge(s("attT"), NT)
        sp.wait_ge(s("ssmst"), 32)
        sp.dma_start(rw[:, :, :], I["router_w"]).then_inc(s("mod3"), 16)
        sp.dma_start(rb[:, :], I["router_b"]).then_inc(s("mod3"), 16)
        for p, j in enumerate(ORDER3):
            if p >= 2:
                sp.wait_ge(s("x2"), p - 1)
            sp.dma_start(xt3[0:TW[j], p % 2, :], I["x"][tok(j), :]).then_inc(s_x3[p % 2], 16)

        done = (s("egate"), s("eup"), s("ey"))

        def expert(e, u):
            for w, (name, k) in enumerate((("w_gate", KD), ("w_up", KD), ("w_down", FE // P))):
                yield (w, ering[3 * u + w][:, :].rearrange("p (k n) -> p k n", k=k),
                       I[name][bass.ds(e, 1)].rearrange("a (k p) n -> p (a k) n", p=P))

        for u in range(2):
            for w, dst, src in expert(u, u):
                m = 3 * u + w
                if m < R1:
                    used(sp, N_ITEMS - R1 + (m - N_ITEMS) % R1)
                if m >= 4:
                    sp.wait_ge(s("yp"), 4 * QT + 1)
                sp.dma_start(dst, src).then_inc(efull[m], 16)
        with sp.Fori(1, NE // 2) as i:
            for u in range(2):
                for w, dst, src in expert(2 * i + u, u):
                    sp.wait_ge(done[w], 2 * i + (u - 1))
                    sp.dma_start(dst, src).then_inc(efull[3 * u + w], 16)
        sp.wait_ge(s("eid"), 1)
        pairs = sp.value_load(npair[0:1, 0:1], min_val=0, max_val=EXTRA // 2)
        with sp.Fori(0, EXTRA // 2) as i:
            with sp.If(pairs > i):
                for u in range(2):
                    e = sp.value_load(eidi[0:1, bass.ds(2 * i + u, 1)], min_val=0, max_val=NE - 1)
                    for w, dst, src in expert(e, u):
                        sp.wait_ge(done[w], 2 * i + (NE + u - 1))
                        sp.dma_start(dst, src).then_inc(efull[3 * u + w], 16)
        for j in range(NT):
            sp.wait_ge(s("fo"), j + 1)
            sp.dma_start(O["y"][tok(j), :], fo[0:TW[j], j, :]).then_inc(s("out_stored"), 16)
        sp.wait_ge(s("statest"), 16)
        sp.wait_ge(s("kvst"), 48)
        sp.wait_ge(s("ssmst"), 32)
        sp.wait_ge(s("out_stored"), 16 * NT)

    @block.gpsimd
    def _(pool):
        o = Order(pool, s("pool_order"))
        for b in range(2):
            o(pool.memset(bpad[b][:, :, :], 0.0))
        pool.wait_ge(s("init"), 160)

        def mod_chunk(c):
            pool.wait_ge(s("adae"), c + 1)
            m = modsb[:, c, :]
            ins = pool.tensor_tensor(m, m, modrow[:, c, :], ALU.add)
            if c in (2, 3, 8, 9):
                o(ins)
                ins = pool.tensor_tensor(m, m, modrow[:, N_ADA + 2 * (c // 6) + c % 2, :], ALU.mult)
            ins.then_inc(s("modg"), 1)

        pool.wait_ge(s("bbar"), 1)
        for half in range(2):
            for r in range(4):
                for b, src in enumerate((bbr, bbi)):
                    rows = slice(64 * half, 64 * half + 64)
                    c0 = 32 * r + GC * half
                    o(pool.tensor_copy(bpad[b][rows, r::4, c0:c0 + GC], src[rows, r::4, :]))
        pool.sem_inc(s("bpad"), 1)
        for c in range(5):
            mod_chunk(c)
        pool.wait_ge(s("modld"), 80)
        for j in range(NT):
            w = TW[j]
            pool.wait_ge(s("hA"), j + 1)
            sh = modP[:, 0, :] if j < QT else modS[:, 0, :]
            pool.tensor_tensor(hb[0:w, j % 2, :], hb[0:w, j % 2, :], sh, ALU.add).then_inc(s("h"), 1)
            mod_chunk(5 + j)
        for c in range(5 + NT, N_ADA):
            mod_chunk(c)
        pool.wait_ge(s("hTp"), 2 * NT)
        pool.wait_ge(s("h"), NT)
        o(pool.memset(padT[:, :, :], 0.0))
        for t in range(TDEC):
            for n in range(4):
                ins = pool.tensor_copy(padT[:, t, 32 * n + t:32 * n + 32:TDEC], ctab33[:, :])
                o(ins)
        pool.sem_inc(s("padt"), 1)
        pool.wait_ge(s("gst"), 16)
        o(pool.memset(qbd[:, :, :, :], 0.0))
        pool.wait_ge(s("za"), 12)
        pool.wait_ge(s("zd"), 12)
        for h in range(HEADS):
            r = slice(64 * (h % 2), 64 * (h % 2) + 64)
            o(pool.tensor_copy(qbd[r, :, h // 2, TDEC * h:TDEC * (h + 1)],
                               qkT[r, h // 2, SEQ:NTOK].rearrange("p (n t) -> p n t", t=TDEC)))
        pool.sem_inc(s("qbd"), 1)
        flat = lambda a: a[:, :, :].rearrange("p a b -> p (a b)")
        sv = lambda a: flat(a).rearrange("p (s n t) -> p s n t", s=STT, n=NSEQ)
        h0v = lambda a: flat(a)[:, 0:STT * NSEQ].rearrange("p (s n) -> p s n", s=STT)
        tmpv = lambda i: flat(ta)[:, 128 * i:128 * i + 128].rearrange("p (s n) -> p s n", s=STT)
        for b in range(3):
            pool.wait_ge(s_modst[b], 64)
        pool.dma_start(h0v(gr[0]), I["h0_re"]).then_inc(s("h0"), 16)
        pool.dma_start(h0v(gi[0]), I["h0_im"]).then_inc(s("h0"), 16)
        o(pool.tensor_tensor(car[:, :], mag[:, :], cth[:, :], ALU.mult))
        o(pool.tensor_tensor(cai[:, :], mag[:, :], sth[:, :], ALU.mult))
        pool.wait_ge(s("buS"), 1)
        pool.wait_ge(s("tables"), 1)
        pool.wait_ge(s("h0"), 32)
        acr, aci = [a[:, :].unsqueeze(2).broadcast_to([P, STT, NSEQ]) for a in (car, cai)]
        for t in range(TDEC):
            pr_, pi_ = (h0v(gr[0]), h0v(gi[0])) if t == 0 else (sv(hr[0])[:, :, :, t - 1], sv(hi[0])[:, :, :, t - 1])
            t1, t2, t3, t4 = [tmpv(i) for i in range(4)]
            pool.tensor_tensor(t1, pr_, acr, ALU.mult)
            pool.tensor_tensor(t2, pi_, aci, ALU.mult)
            pool.tensor_tensor(t3, pr_, aci, ALU.mult)
            o(pool.tensor_tensor(t4, pi_, acr, ALU.mult))
            pool.tensor_tensor(t1, t1, t2, ALU.subtract)
            o(pool.tensor_tensor(t3, t3, t4, ALU.add))
            pool.tensor_tensor(sv(hr[0])[:, :, :, t], t1, sv(xr[0])[:, :, :, t], ALU.add)
            o(pool.tensor_tensor(sv(hi[0])[:, :, :, t], t3, sv(xi[0])[:, :, :, t], ALU.add))
        for n, a in enumerate((hr, hi)):
            o(pool.tensor_copy(states[:, 128 * n:128 * n + 128].rearrange("p (s n) -> p s n", s=STT),
                               sv(a[0])[:, :, :, TDEC - 1]))
        pool.sem_inc(s("hout"), 1)
        pool.wait_ge(s("sq"), NT + 1)
        pool.dma_start(glu[:, 0, :, :], I["glu_a"]).then_inc(s("glul"), 16)
        pool.dma_start(glu[:, 1, :, :], I["glu_b"]).then_inc(s("glul"), 16)
        pool.dma_start(y_d[NE * P:NTILE * P, :], I["zero"].partition_broadcast(EXTRA * P)).then_inc(s("yzero"), 16)
        pool.dma_start(O["ssm_s"], states[:, :]).then_inc(s("statest"), 16)

        def turned(out_re, out_im, cs, sn, b, tq):
            lr, li = gr[b][:, :, CH - 1], gi[b][:, :, CH - 1]
            pool.tensor_tensor(out_re[:, tq], lr, cs, ALU.mult)
            pool.tensor_tensor(ctmp[:, 0:4], li, sn, ALU.mult)
            pool.tensor_tensor(out_im[:, tq], lr, sn, ALU.mult)
            o(pool.tensor_tensor(ctmp[:, 4:8], li, cs, ALU.mult))
            pool.tensor_tensor(out_re[:, tq], out_re[:, tq], ctmp[:, 0:4], ALU.subtract)
            o(pool.tensor_tensor(out_im[:, tq], out_im[:, tq], ctmp[:, 4:8], ALU.add))

        for i in range(16):
            k, q = divmod(i, 4)
            b = i % 2
            tq = slice(4 * q, 4 * q + 4)
            cs, sn = cosT[:, tq, :], sinT[:, tq, :]
            pool.wait_ge(s("scan"), i + 1)
            if k == QT - 1:
                turned(las, lai, cosT[:, tq, CH - 1], sinT[:, tq, CH - 1], b, tq)
            else:
                turned(car, cai, c128[:, tq], s128[:, tq], b, tq)
            if i != 1:
                pool.wait_ge(s("yp"), max(i, 1))
            pool.tensor_tensor(hr[b][:, :, :], gr[b][:, :, :], cs, ALU.mult)
            pool.tensor_tensor(hi[b][:, :, :], gi[b][:, :, :], sn, ALU.mult)
            pool.tensor_tensor(gr[b][:, :, :], gr[b][:, :, :], sn, ALU.mult)
            pool.tensor_tensor(gi[b][:, :, :], gi[b][:, :, :], cs, ALU.mult).then_inc(s("hout"), 1)
        pool.dma_start(O["ssm_p"][:, 0, :], las[:, :]).then_inc(s("ssmst"), 16)
        pool.dma_start(O["ssm_p"][:, 1, :], lai[:, :]).then_inc(s("ssmst"), 16)

        for p, j in enumerate(ORDER3):
            pool.wait_ge(s("h"), NT + p + 1)
            pool.dma_start(h2_d[tok(j), :], h2[0:TW[j], p % 2, :]).then_inc(s_h2st[p % 2], 16)
        pool.wait_ge(s_h2st[0], 48)
        pool.wait_ge(s_h2st[1], 32)
        pool.wait_ge(s("gidx"), 1)

        def gather(t):
            u = t % 2
            if t >= 2:
                pool.wait_ge(s("xgp"), t - 1)
                pool.wait_ge(s_xg[u], 16 * (t // 2))
            pool.indirect_dma_start(xg[:, u, :], None, h2_d, bass.IndirectOffsetOnAxis(ap=gidx[:, t:t + 1], axis=0))\
                .then_inc(s_xg[u], 16)

        for t in range(NE):
            gather(t)
        pool.wait_ge(s("eid"), 1)
        pairs = pool.value_load(npair[0:1, 0:1], min_val=0, max_val=EXTRA // 2)
        for i in range(EXTRA // 2):
            with pool.If(pairs > i):
                gather(NE + 2 * i)
                gather(NE + 2 * i + 1)
        pool.wait_ge(s("y_all"), 1)
        for j in range(NT):
            w = TW[j]
            for k in range(2):
                pool.indirect_dma_start(yg[0:w, j, k, :], None, y_d,
                                        bass.IndirectOffsetOnAxis(ap=sidx[0:w, k, j:j + 1], axis=0))\
                    .then_inc(s_yg[j], 16)
        for j in range(NT):
            w = TW[j]
            g2 = mod3P[0:w, 1, :] if j < QT else mod3S[0:w, 0, :]
            pool.wait_ge(s("endld"), 96)
            pool.wait_ge(s("ysum"), j + 1)
            a = yg[0:w, j, 0, :]
            pool.tensor_tensor(a, a, g2, ALU.mult).then_inc(s("ygate"), 1)

    @block.scalar
    def _(act):
        o = Order(act, s("act_order"))

        def f(out, in_, func, **kw):
            return nc.scalar.activation(out, in_, func, **kw)

        def root(a, b, w, width):
            return f(stat[0:w, 16 + a:16 + b], stat[0:w, a:b], ACT.Sqrt, scale=1.0 / width, bias=epst[0:w, :])

        act.wait_ge(s("cld"), 16)
        f(cE[:, :, :], cT[:, :, :], ACT.Exp, scale=-1.0).then_inc(s("cexp"), 1)
        act.wait_ge(s("init"), 160)
        f(pr[:, 1, :], par[:, PC["log_dt"][0]:PC["log_dt"][1]], ACT.Exp).then_inc(s("par_act"), 1)
        act.wait_ge(s("par_dve"), 1)
        f(mag[:, :], pr[:, 2, :], ACT.Exp).then_inc(s("par_act"), 1)
        act.wait_ge(s("par_dve"), 2)
        f(pr[:, 5, :], pr[:, 4, :], ACT.Sin).then_inc(s("par_act"), 1)
        f(pr[:, 6, :], pr[:, 4, :], ACT.Sin, scale=0.5).then_inc(s("par_act"), 1)

        def mod_chunk(c):
            act.wait_ge(s("ada"), c + 1)
            f(modsb[:, c, :], ps[:, c % 2, 0:P], ACT.Copy, bias=1.0 if c in (2, 3, 8, 9) else 0.0)\
                .then_inc(s("adae"), 1)
            act.wait_ge(s("modg"), c + 1)
            act.dma_start(mod_d[c], modsb[:, c, :]).then_inc(s_modst[c // 4], 16)

        for c in range(4):
            mod_chunk(c)
        for n in range(8):
            act.wait_ge(s("btT"), n + 1)
            b, q = n // 4, n % 4
            f(bt[b][:, 4 * q:4 * q + 4, :], ps[:, 2 + n % 2, :].rearrange("p (a b) -> p a b", a=4), ACT.Copy)\
                .then_inc(s("btTe"), 1)
        act.wait_ge(s("gsb"), 1)
        act.dma_start(g_d, gsb[:, :]).then_inc(s("gst"), 16)
        for c in range(4, N_ADA):
            j = c - 4
            if j < NT:
                w = TW[j]
                act.wait_ge(s("x"), 32)
                f(ps[0:w, 6:8, :], xt[0:w, j, :].rearrange("p (a b) -> p a b", a=2), ACT.Square,
                  accum_out=stat[0:w, j:j + 1]).then_inc(s("sq"), 1)
                act.wait_ge(s("sq"), j + 1)
                root(j, j + 1, w, D).then_inc(s("rt"), 1)
            mod_chunk(c)
            j = c - 6
            if 0 <= j < NT:
                w = TW[j]
                act.wait_ge(s("hTp"), 2 * j + 1)
                f(hT[:, 0:4, tok(j)], ps[:, 2 + 2 * (j % 2), 0:4 * w].rearrange("p (a b) -> p a b", a=4), ACT.Copy)\
                    .then_inc(s("hTa"), 1)
        for z in range(12):
            kind, c = divmod(z, 4)
            act.wait_ge(s("z"), 2 * z + 1)
            dst = qkT[:, 4 * kind + c, 0:HALF] if kind < 2 else uT[:, c, 0:HALF]
            f(dst, ps[:, z % 2, 0:HALF], ACT.Copy, scale=DH ** -0.5 if kind == 0 else 1.0).then_inc(s("za"), 1)
        act.wait_ge(s("za"), 12)
        act.wait_ge(s("zd"), 12)
        act.wait_ge(s("ve"), NT)
        act.dma_start(O["kT"].rearrange("(c p) t -> p c t", p=P), qkT[:, 4:8, :]).then_inc(s("kvst"), 16)
        act.dma_start(O["v"][0:SEQ, :].rearrange("(j p) n -> p j n", p=P), vrow[:, 0:QT, :]).then_inc(s("kvst"), 16)
        act.dma_start(O["v"][SEQ:NTOK, :], vrow[0:NS, QT, :]).then_inc(s("kvst"), 16)
        for st in range(HEADS * QT):
            qt = st % QT
            m = P * (qt + 1)
            act.wait_ge(s("sm"), st + 1)
            if st >= 2:
                act.wait_ge(s("rd"), st - 1)
                act.wait_ge(s("pt"), st - 1)
            f(Sb[:, st % 2, 0:m], ps[:, st % 2, 0:m], ACT.Exp, bias=stat[:, 26 + st % 2:27 + st % 2],
              accum_out=stat[:, 28 + st % 2:29 + st % 2]).then_inc(s("P"), 1)
            act.wait_ge(s("pt"), st + 1)
            if st >= 2:
                act.wait_ge(s("pv"), st - 1)
            f(PTs[:, st % 2, 0:m], ps[:, 2 + st % 2, 0:m], ACT.Copy).then_inc(s("ptr"), 1)

        act.wait_ge(s("att"), HEADS * QT)
        for j in range(QT):
            ins = f((Sb, PTs)[j // 2][:, j % 2, :], att[:, j, :], ACT.Square, accum_out=stat[:, j:j + 1])
        ins.then_inc(s("sq"), 1)
        act.wait_ge(s("sq"), NT + 1)
        root(0, QT, P, AW).then_inc(s("rt"), 1)

        def gelu_in(n, w):
            act.wait_ge(s("yread"), n + 1)
            f(y2[:, :, 0:w], yd[:, :, 0:w], ACT.Square, scale=float(np.sqrt(0.044715))).then_inc(s("ysq"), 1)
            act.wait_ge(s("gin"), n + 1)
            f(th[:, :, 0:w], y2[:, :, 0:w], ACT.Tanh, scale=float(np.sqrt(2.0 / np.pi))).then_inc(s("gth"), 1)

        def gelu_gate(n, w):
            act.wait_ge(s("glut"), n + 1)
            f(th[:, :, 0:w], ps[:, 3, 0:4 * w].rearrange("p (a b) -> p a b", a=4), ACT.Tanh, scale=0.25)\
                .then_inc(s("gate"), 1)

        def gelu_end(n, w, t0):
            act.wait_ge(s("gated"), n + 1)
            for q in range(4):
                f(mixT[:, 4 + q, t0:t0 + w], y2[:, q, 0:w], ACT.Copy, scale=gains[:, 8 + q:9 + q])
            f(yd[:, :, 0:w], y2[:, :, 0:w], ACT.Square, scale=0.25).then_inc(s("gsq"), 1)

        def dec_exp(g):
            act.wait_ge(s("dSm"), g + 1)
            f(dP[:, :], dP[:, :], ACT.Exp, bias=dstat[:, 4:5], accum_out=dstat[:, 5:6]).then_inc(s("dP"), 1)

        def dec_probs(g):
            act.wait_ge(s("dPt"), g + 1)
            if g:
                act.wait_ge(s("dOp"), 4 * g)
            f(dPT[:, 4:7, :], ps[:, 1, 0:3 * P].rearrange("p (a b) -> p a b", a=3), ACT.Copy)
            f(dPT[0:NS, 7, :], ps[0:NS, 1, 3 * P:4 * P], ACT.Copy).then_inc(s("dPta"), 1)

        def wo_a(p):
            act.wait_ge(s("woA"), p + 1)
            if p >= 2:
                act.wait_ge(s("x2"), p - 1)
            if ORDER3[p] < QT:
                ins = f(pt1[:, p % 2, :].rearrange("p (a b) -> p a b", a=2), ps[:, 0:2, :], ACT.Copy)
            else:
                ins = f(spread[:, :], ps[:, 0, 0:256], ACT.Copy)
            ins.then_inc(s("woa"), 1)

        act.wait_ge(s("kvst"), 48)
        f(ctn[:, :, :], ct[0][:, :, :], ACT.Copy, scale=-1.0).then_inc(s("ctn"), 1)
        for n in range(QT):
            w, t0 = (CH, CH * (n - 1)) if n else (NS, SEQ)
            gelu_in(n, w)
            if n == 0:
                dec_exp(0)
            if n == 3:
                dec_probs(1)
            gelu_gate(n, w)
            gelu_end(n, w, t0)
            if n == 0:
                dec_probs(0)
            if n == 2:
                dec_exp(1)
        gelu_in(4, CH)
        act.wait_ge(s("attS"), 1)
        f(ps[0:NS, 5, :], att[0:NS, QT, :], ACT.Square, accum_out=stat[0:NS, QT:NT]).then_inc(s("sq"), 1)
        act.wait_ge(s("sq"), NT + 2)
        root(QT, NT, NS, AW).then_inc(s("rt"), 1)
        gelu_gate(4, CH)
        gelu_end(4, CH, CH * (QT - 1))
        act.wait_ge(s("gluo"), NT)
        f(dstat[:, 24:24 + NT], dstat[:, 8:8 + NT], ACT.Sqrt, scale=1.0 / (D - AW), bias=epst[:, :])\
            .then_inc(s("ssrt"), 1)
        def h2T_half(p):
            j = ORDER3[p]
            act.wait_ge(s("hTp"), 2 * (NT + p) + 1)
            f(h2T[:, 0:4, tok(j)], ps[:, 6, 0:4 * TW[j]].rearrange("p (a b) -> p a b", a=4), ACT.Copy)\
                .then_inc(s("hTa"), 1)

        for p, j in enumerate(ORDER3):
            w = TW[j]
            wo_a(p)
            if p:
                h2T_half(p - 1)
            act.wait_ge(s("x2"), p + 1)
            if p >= 2:
                act.wait_ge(s("hTp"), 2 * (NT + p - 1))
                act.wait_ge(s_h2st[p % 2], 16 * (p // 2))
            f(h2[0:w, p % 2, :], x2[0:w, j, :], ACT.Square,
              accum_out=stat[0:w, j:j + 1]).then_inc(s("sq"), 1)
            act.wait_ge(s("sq"), NT + 3 + p)
            root(j, j + 1, w, D).then_inc(s("rt"), 1)
        h2T_half(NT - 1)
        act.wait_ge(s("h"), 2 * NT)
        act.wait_ge(s("x2"), NT)
        act.dma_start(mod3P[:, 1:2, :].rearrange("p v (c j n) -> p (v c) j n", c=2, j=4),
                     mod_rows(1, 5)).then_inc(s("endld"), 16)
        for t in range(TDEC):
            act.dma_start(mod3S[t:NS:TDEC, 0:1, :].rearrange("p v (c j n) -> p (v c) j n", c=2, j=4),
                         mod_rows_seq(1, 5)).then_inc(s("endld"), 16)
        act.dma_start(fgain[:, :], I["final_g"].partition_broadcast(P)).then_inc(s("endld"), 16)
        act.wait_ge(s("gexpin"), 1)
        f(g4b[:, :, :], g4a[:, :, :], ACT.Exp).then_inc(s("gexp"), 1)
        act.wait_ge(s("gexpin"), 2)
        f(w2[:, :], v2[:, :], ACT.Exp).then_inc(s("gexp"), 1)

        def rows(t, u):
            act.wait_ge(s("xgp"), t + 1)
            f(xgT[:, u, 0:4, :], ps[:, 4, :].rearrange("p (a b) -> p a b", a=4), ACT.Copy).then_inc(s("xga"), 1)

        def gate(t, u):
            act.wait_ge(s("egate"), t + 1)
            f(a_t[:, u, :], ps[:, u, :], ACT.Tanh, scale=0.5).then_inc(s("eth"), 1)

        def hidden(t, u):
            act.wait_ge(s("aTp"), t + 1)
            f(aT[:, u, :, :], ps[:, u, :].rearrange("p (a b) -> p a b", a=4), ACT.Copy).then_inc(s("aTe"), 1)

        def finish(t, u, dst, waity):
            act.wait_ge(s("ey"), t + 1)
            if waity is not None:
                act.wait_ge(s_yst[u], waity)
            f(ysb[:, u, 0:512], ps[:, 6, :], ACT.Copy).then_inc(s("eya"), 1)
            act.wait_ge(s("eya"), t + 1)
            act.wait_ge(s("eyd"), t + 1)
            act.dma_start(dst, ysb[:, u, :]).then_inc(s_yst[u], 16)

        def y_tile(t):
            return y_d.rearrange("(t p) n -> t p n", p=P)[bass.ds(t, 1)].rearrange("t p n -> (t p) n")

        rows(0, 0)
        gate(0, 0)
        rows(1, 1)
        for t in (1, 2):
            u = t % 2
            gate(t, u)
            hidden(t - 1, 1 - u)
            rows(t + 1, 1 - u)
            finish(t - 1, 1 - u, y_d[P * (t - 1):P * t, :], None)
        with act.Fori(1, NE // 2 - 1) as i:
            for u in (1, 0):
                t = 2 * i + (2 - u)
                gate(t, u)
                hidden(2 * i + (1 - u), 1 - u)
                rows(2 * i + (3 - u), 1 - u)
                finish(2 * i + (1 - u), 1 - u, y_tile(2 * i + (1 - u)), 16 * i)
        gate(NE - 1, 1)
        hidden(NE - 2, 0)
        finish(NE - 2, 0, y_tile(NE - 2), 16 * (NE // 2 - 1))
        hidden(NE - 1, 1)
        finish(NE - 1, 1, y_tile(NE - 1), 16 * (NE // 2 - 1))
        act.wait_ge(s("eid"), 1)
        act.wait_ge(s("yzero"), 16)
        pairs = act.value_load(npair[0:1, 0:1], min_val=0, max_val=EXTRA // 2)
        with act.Fori(0, EXTRA // 2) as i:
            with act.If(pairs > i):
                rows(2 * i + NE, 0)
                gate(2 * i + NE, 0)
                rows(2 * i + (NE + 1), 1)
                gate(2 * i + (NE + 1), 1)
                for u in range(2):
                    hidden(2 * i + (NE + u), u)
                    finish(2 * i + (NE + u), u, y_tile(2 * i + (NE + u)), 16 * i + 16 * (NE // 2))
        f(stat[0:1, 62:63], epst[0:1, :], ACT.Sqrt)
        for u in range(2):
            act.wait_ge(s_yst[u], 16 * pairs + 16 * (NE // 2))
        act.sem_inc(s("y_all"), 1)
        def scale_first(j):
            w = TW[j]
            act.wait_ge(s_yg[j], 32)
            f(yg[0:w, j, 0, :], yg[0:w, j, 0, :], ACT.Copy, scale=w1[0:w, j:j + 1]).then_inc(s("yw"), 1)

        def last_root(j):
            w = TW[j]
            act.wait_ge(s("x3"), j + 1)
            f(ps[0:w, 0:2, :], x2[0:w, j, :].rearrange("p (a b) -> p a b", a=2), ACT.Square,
              accum_out=stat[0:w, j:j + 1]).then_inc(s("sq"), 1)
            act.wait_ge(s("sq"), 2 * NT + 3 + j)
            root(j, j + 1, w, D).then_inc(s("rt"), 1)

        for j in range(NT):
            scale_first(j)
        for j in range(NT):
            last_root(j)

    @block.vector
    def _(dve):
        o = Order(dve, s("dve_order"))
        v = nc.vector
        tt_, ts_, stt = v.tensor_tensor, v.tensor_scalar, v.scalar_tensor_tensor
        o(v.memset(stat[:, :], 1.0))
        o(v.memset(dstat[:, :], 1.0))
        o(v.memset(epst[:, :], EPS))
        o(v.memset(cS[:, :, :], 0.0))
        dve.wait_ge(s("cexp"), 1)
        o(ts_(cE[:, :, :], cE[:, :, :], 1.0, None, ALU.add))
        o(v.reciprocal(cE[:, :, :], cE[:, :, :]))
        tt_(cS[:, :, 0:NC], cT[:, :, :], cE[:, :, :], ALU.mult).then_inc(s("cs"), 1)
        dve.wait_ge(s("init"), 160)

        pa = lambda n: par[:, PC[n][0]:PC[n][1]]
        q_ = lambda i: pr[:, i, :]
        lam_re, lam_im, dt = q_(0), pa("a_im"), q_(1)
        o(ts_(lam_re, pa("a_re"), -1e-4, None, ALU.min))
        dve.wait_ge(s("par_act"), 1)
        tt_(q_(2), lam_re, dt, ALU.mult).then_inc(s("par_dve"), 1)
        o(tt_(q_(3), lam_im, dt, ALU.mult))
        big = float(3 << 22)
        c1 = 6.28125
        o(ts_(q_(7), q_(3), 1.0 / (2 * np.pi), big, ALU.mult, ALU.add))
        o(ts_(q_(7), q_(7), -big, None, ALU.add))
        o(stt(out=q_(4), in0=q_(7), scalar=-c1, in1=q_(3), op0=ALU.mult, op1=ALU.add))
        o(stt(out=q_(4), in0=q_(7), scalar=-(2 * np.pi - c1), in1=q_(4), op0=ALU.mult, op1=ALU.add))
        ts_(q_(4), q_(4), 3.1415925, -3.1415925, ALU.min, ALU.max).then_inc(s("par_dve"), 1)
        dve.wait_ge(s("par_act"), 4)
        o(v.tensor_copy(sth[:, :], q_(5)))
        o(tt_(q_(8), q_(6), q_(6), ALU.mult))
        o(ts_(cth[:, :], q_(8), -2.0, 1.0, ALU.mult, ALU.add))
        o(tt_(q_(9), mag[:, :], cth[:, :], ALU.mult))
        o(tt_(q_(10), mag[:, :], sth[:, :], ALU.mult))
        o(ts_(q_(11), q_(9), -1.0, None, ALU.add))
        o(tt_(q_(12), lam_re, lam_re, ALU.mult))
        o(tt_(q_(13), lam_im, lam_im, ALU.mult))
        o(tt_(q_(12), q_(12), q_(13), ALU.add))
        o(v.reciprocal(q_(12), q_(12)))
        o(tt_(q_(13), q_(11), lam_re, ALU.mult))
        o(tt_(q_(14), q_(10), lam_im, ALU.mult))
        o(tt_(q_(13), q_(13), q_(14), ALU.add))
        o(tt_(q_(13), q_(13), q_(12), ALU.mult))
        o(tt_(q_(14), q_(10), lam_re, ALU.mult))
        o(tt_(q_(15), q_(11), lam_im, ALU.mult))
        o(tt_(q_(14), q_(14), q_(15), ALU.subtract))
        o(tt_(q_(14), q_(14), q_(12), ALU.mult))
        crb = q_(13).unsqueeze(2).broadcast_to([P, STT, GC])
        cib = q_(14).unsqueeze(2).broadcast_to([P, STT, GC])
        b_re, b_im = [pa(n).rearrange("p (a b) -> p a b", a=STT) for n in ("b_re", "b_im")]
        o(tt_(bt1[:, :, :], b_re, crb, ALU.mult))
        o(tt_(bt2[:, :, :], b_im, cib, ALU.mult))
        o(tt_(bbr[:, :, :], bt1[:, :, :], bt2[:, :, :], ALU.subtract))
        o(tt_(bt1[:, :, :], b_im, crb, ALU.mult))
        o(tt_(bt2[:, :, :], b_re, cib, ALU.mult))
        tt_(bbi[:, :, :], bt1[:, :, :], bt2[:, :, :], ALU.add).then_inc(s("bbar"), 1)
        o(v.tensor_copy(gains[:, :], par[:, PC["dskip"][0]:PC["ssmg"][1]]))
        o(ts_(gains[:, 8:12], gains[:, 8:12], 0.25, None, ALU.mult))
        o(ts_(ct[1][:, :, :], ct[1][:, :, :], -1.0, None, ALU.mult))
        dve.wait_ge(s("gp"), 1)
        v.tensor_copy(gsb[:, :], ps[0:HEADS, 6:8, :].rearrange("p a b -> p (a b)")[:, 0:640]).then_inc(s("gsb"), 1)

        def rstd(j, w, width, n):
            dve.wait_ge(s("sq"), n)
            dve.wait_ge(s("rt"), n)
            o(v.reciprocal(stat[0:w, 56 + j:57 + j], stat[0:w, 16 + j:17 + j]))

        def hT_half(j):
            w = TW[j]
            dve.wait_ge(s("hTp"), 2 * j + 2)
            v.tensor_copy(hT[:, 4:8, tok(j)], ps[:, 3 + 2 * (j % 2), 0:4 * w].rearrange("p (a b) -> p a b", a=4))\
                .then_inc(s("hTd"), 1)

        dve.wait_ge(s("bpad"), 1)
        for j in range(NT):
            w = TW[j]
            rstd(j, w, D, j + 1)
            dve.wait_ge(s("modld"), 80)
            if j >= 2:
                dve.wait_ge(s("hTp"), 2 * (j - 1))
            A = modP[:, 1, :] if j < QT else modS[:, 1, :]
            stt(out=hb[0:w, j % 2, :], in0=xt[0:w, j, :], scalar=stat[0:w, 56 + j:57 + j], in1=A,
                op0=ALU.mult, op1=ALU.mult).then_inc(s("hA"), 1)
            if j:
                hT_half(j - 1)
        hT_half(NT - 1)

        cm, sm_, c2, s2, c3 = [rot[:, i, :] for i in range(5)]

        def doubling(m):
            if m == 1:
                o(v.memset(cosT[:, :, 0:1], 1.0))
                o(v.memset(sinT[:, :, 0:1], 0.0))
                o(v.tensor_copy(cm, cth[:, :]))
                o(v.tensor_copy(sm_, sth[:, :]))
            cb, sb_ = [a.unsqueeze(2).broadcast_to([P, STT, m]) for a in (cm, sm_)]
            C_, S_ = cosT[:, :, 0:m], sinT[:, :, 0:m]
            Cn, Sn = cosT[:, :, m:2 * m], sinT[:, :, m:2 * m]
            tt_(Cn, C_, cb, ALU.mult)
            tt_(dt1[:, :, 0:m], S_, sb_, ALU.mult)
            tt_(Sn, C_, sb_, ALU.mult)
            o(tt_(dt2[:, :, 0:m], S_, cb, ALU.mult))
            tt_(Cn, Cn, dt1[:, :, 0:m], ALU.subtract)
            tt_(Sn, Sn, dt2[:, :, 0:m], ALU.add)
            tt_(c2, cm, cm, ALU.mult)
            tt_(c3, sm_, sm_, ALU.mult)
            o(tt_(s2, cm, sm_, ALU.mult))
            tt_(cm, c2, c3, ALU.subtract)
            o(ts_(sm_, s2, 2.0, None, ALU.mult))
            if m == CH // 2:
                v.tensor_copy(c128[:, :], cm)
                v.tensor_copy(s128[:, :], sm_).then_inc(s("tables"), 1)

        dve.wait_ge(s("modg"), N_ADA)
        def z_half(z):
            kind, c = divmod(z, 4)
            dve.wait_ge(s("z"), 2 * z + 2)
            dst = qkT[:, 4 * kind + c, HALF:NTOK] if kind < 2 else uT[:, c, HALF:NTOK]
            ts_(dst, ps[:, 6 + z % 2, 0:HALF], DH ** -0.5 if kind == 0 else 1.0, None, ALU.mult).then_inc(s("zd"), 1)

        for z in range(8):
            z_half(z)
            if z < 6:
                doubling(1 << z)
        for j in range(NT):
            w = TW[j]
            dve.wait_ge(s("v"), j + 1)
            if j < QT:
                ins = v.tensor_copy(vrow[:, j, :], ps[:, 2 + j % 2, :])
            else:
                for c in range(4):
                    ins = v.tensor_copy(vrow[0:NS, j, P * c:P * (c + 1)], ps[32 * c:32 * c + 32, 2, 0:P])
            ins.then_inc(s("ve"), 1)
            if j == 0:
                doubling(CH // 2)
        for z in range(8, 12):
            z_half(z)
        dve.wait_ge(s("dbp"), 1)
        o(v.tensor_copy(dbias[:, :], ps[:, 2:4, :].rearrange("p a b -> p (a b)")[:, 0:DK]))
        for g in range(2):
            o(tt_(nbias[:, NS * g:NS * g + NS], dbias[:, CK:DK], cst("newmask")[:, NS * g:NS * g + NS], ALU.add))
        dve.sem_inc(s("dbias"), 1)
        dve.wait_ge(s("buSp"), 1)
        for b in range(3):
            dve.wait_ge(s_modst[b], 64)
        v.tensor_copy(xr[0][:, :, :].rearrange("p a b -> p (a b)"), ps[:, 5, :])
        v.tensor_copy(xi[0][:, :, :].rearrange("p a b -> p (a b)"), ps[:, 6, :]).then_inc(s("buS"), 1)

        NST = HEADS * QT

        def row_max(st):
            h, qt = divmod(st, QT)
            b, m = st % 2, P * (qt + 1)
            dve.wait_ge(s("S"), st + 1)
            o(v.tensor_reduce(stat[:, 24 + b:25 + b], ps[:, b, 0:m], AX.X, ALU.max))
            ts_(stat[:, 26 + b:27 + b], stat[:, 24 + b:25 + b], -1.0, None, ALU.mult).then_inc(s("sm"), 1)

        def head_out(st):
            h, qt = divmod(st, QT)
            b = st % 2
            dve.wait_ge(s("P"), st + 1)
            v.reciprocal(stat[:, 30 + b:31 + b], stat[:, 28 + b:29 + b]).then_inc(s("rd"), 1)
            dve.wait_ge(s("rd"), st + 1)
            dve.wait_ge(s("pv"), st + 1)
            ts_(att[:, qt, DH * h:DH * (h + 1)], ps[:, 4 + qt, DH * h:DH * (h + 1)], stat[:, 30 + b:31 + b], None,
                ALU.mult).then_inc(s("att"), 1)

        for st in range(NST + 2):
            if st < NST:
                row_max(st)
            if st >= 2:
                head_out(st - 2)

        def att_out(j):
            w = TW[j]
            bank = 2 + j % 2 if j < QT else 5
            dve.wait_ge(s("attT"), j + 1)
            tt_(mixT[:, 0:4, tok(j)], ps[:, bank, 0:4 * w].rearrange("p (a b) -> p a b", a=4),
                gains[:, 4:8].unsqueeze(2).broadcast_to([P, 4, w]), ALU.mult).then_inc(s("attTe"), 1)

        def turn_in(i):
            q, b = i % 4, i % 2
            cs, sn = cosT[:, 4 * q:4 * q + 4, :], sinT[:, 4 * q:4 * q + 4, :]
            bre, bim = [ps[:, 5 + n, :].rearrange("p (a b) -> p a b", a=4) for n in range(2)]
            if i == 1:
                dve.wait_ge(s("kvst"), 48)
                dve.wait_ge(s("qbd"), 1)
            elif i == 0:
                dve.wait_ge(s("hout"), 1)
            else:
                dve.wait_ge(s("scan"), i - 1)
            dve.wait_ge(s("bu"), i + 1)
            tt_(xr[b][:, :, :], bre, cs, ALU.mult)
            tt_(ta[:, :, :], bim, sn, ALU.mult)
            tt_(xi[b][:, :, :], bim, cs, ALU.mult)
            tt_(tb[:, :, :], bre, sn, ALU.mult).then_inc(s("buread"), 1)
            dve.wait_ge(s("buread"), i + 1)
            tt_(xr[b][:, :, :], xr[b][:, :, :], ta[:, :, :], ALU.add)
            tt_(xi[b][:, :, :], xi[b][:, :, :], tb[:, :, :], ALU.subtract).then_inc(s("xadd"), 1)

        def scans(i):
            k, q = divmod(i, 4)
            b = i % 2
            dve.wait_ge(s("xadd"), i + 1)
            if i >= 2:
                dve.wait_ge(s("yp"), i)
            for r in range(4):
                t = 4 * q + r
                m = mag[:, t:t + 1].broadcast_to([P, CH])
                v.tensor_tensor_scan(gr[b][:, r, :], m, xr[b][:, r, :], 0.0 if k == 0 else car[:, t:t + 1],
                                     ALU.mult, ALU.add)
                ins = v.tensor_tensor_scan(gi[b][:, r, :], m, xi[b][:, r, :], 0.0 if k == 0 else cai[:, t:t + 1],
                                           ALU.mult, ALU.add)
            ins.then_inc(s("scan"), 1)

        def chunk(n):
            return (CH, CH * (n - 1)) if n else (NS, SEQ)

        def gelu_skip(n):
            w, t0 = chunk(n)
            dve.wait_ge(s("yp"), 4 * n + 1)
            for q in range(4):
                ins = stt(out=yd[:, q, 0:w], in0=uT[:, q, t0:t0 + w], scalar=gains[:, q:q + 1],
                          in1=ps[:, 7, w * q:w * (q + 1)], op0=ALU.mult, op1=ALU.add)
            ins.then_inc(s("yread"), 1)

        def gelu_cubic(n):
            w, t0 = chunk(n)
            dve.wait_ge(s("ysq"), n + 1)
            stt(out=y2[:, :, 0:w], in0=y2[:, :, 0:w], scalar=1.0, in1=yd[:, :, 0:w], op0=ALU.add, op1=ALU.mult)\
                .then_inc(s("gin"), 1)

        def gelu_out(n):
            w, t0 = chunk(n)
            dve.wait_ge(s("gth"), n + 1)
            stt(out=y2[:, :, 0:w], in0=th[:, :, 0:w], scalar=1.0, in1=yd[:, :, 0:w], op0=ALU.add, op1=ALU.mult)\
                .then_inc(s("gel"), 1)

        def gated(n):
            w, t0 = chunk(n)
            dve.wait_ge(s("gate"), n + 1)
            ga = ps[:, 2, 0:4 * w].rearrange("p (a b) -> p a b", a=4)
            stt(out=y2[:, :, 0:w], in0=th[:, :, 0:w], scalar=1.0, in1=ga, op0=ALU.add, op1=ALU.mult)\
                .then_inc(s("gated"), 1)

        def ssum(n):
            j = n - 1 if n else QT
            dve.wait_ge(s("ssp"), n + 1)
            v.tensor_copy(dstat[:, 8 + j:9 + j], ps[:, 2, 0:1]).then_inc(s("gluo"), 1)

        def dec_softmax(g):
            dve.wait_ge(s("dS"), 4 * (g + 1))
            if g == 0:
                dve.wait_ge(s("statest"), 16)
            if g:
                dve.wait_ge(s("dPt"), g)
            flat = ps[:, 0:2, :].rearrange("p a b -> p (a b)")
            o(v.tensor_tensor_reduce(out=dP[:, 0:CK], in0=flat[:, 0:CK], in1=dbias[:, 0:CK], scale=1.0,
                                     scalar=-3.0e38, op0=ALU.add, op1=ALU.max, accum_out=dstat[:, 0:1]))
            o(v.tensor_tensor_reduce(out=dP[:, CK:DK], in0=flat[:, CK:DK], in1=nbias[:, NS * g:NS * g + NS], scale=1.0,
                                     scalar=-3.0e38, op0=ALU.add, op1=ALU.max, accum_out=dstat[:, 1:2]))
            o(tt_(dstat[:, 2:3], dstat[:, 0:1], dstat[:, 1:2], ALU.max))
            ts_(dstat[:, 4:5], dstat[:, 2:3], -1.0, None, ALU.mult).then_inc(s("dSm"), 1)

        def dec_probs(g):
            dve.wait_ge(s("dP"), g + 1)
            o(v.reciprocal(dstat[:, 6:7], dstat[:, 5:6]))
            dve.wait_ge(s("dPt"), g + 1)
            if g:
                dve.wait_ge(s("dOp"), 4 * g)
            v.tensor_copy(dPT[:, 0:4, :], ps[:, 0, :].rearrange("p (a b) -> p a b", a=4)).then_inc(s("dPtd"), 1)

        def dec_out(g):
            dve.wait_ge(s("dOp"), 4 * (g + 1))
            stt(out=dO[:, g, :], in0=ps[:, 4, :], scalar=dstat[:, 6:7], in1=cst("headsel"),
                op0=ALU.mult, op1=ALU.mult).then_inc(s("dOe"), 1)

        dve.wait_ge(s("att"), NST)
        for i in range(16):
            n, part = divmod(i, 4)
            if i == 8:
                dec_out(0)
            if i == 4:
                dec_probs(0)
            turn_in(i)
            if i == 14:
                dec_probs(1)
            if i == 0:
                dve.wait_ge(s("rt"), NT + 1)
                o(v.reciprocal(stat[:, 56:56 + QT], stat[:, 16:16 + QT]))
                for j in range(QT):
                    ts_(att[:, j, :], att[:, j, :], stat[:, 56 + j:57 + j], None, ALU.mult).then_inc(s("attn"), 1)
            if part == 1:
                if n:
                    ssum(n - 1)
                gelu_skip(n)
            if part == 2:
                gelu_out(n)
            scans(i)
            if i == 0:
                for j in range(QT):
                    att_out(j)
            if part == 1:
                gelu_cubic(n)
            if part == 3:
                gated(n)
            if i in (2, 12):
                dec_softmax(i // 8)
        dec_out(1)
        ssum(3)
        gelu_skip(4)
        gelu_cubic(4)
        dve.wait_ge(s("attSp"), 1)
        v.tensor_copy(att[0:NS, QT, :], ps[0:NS, 4, :]).then_inc(s("attS"), 1)
        gelu_out(4)
        rstd(QT, NS, AW, NT + 2)
        ts_(att[0:NS, QT, :], att[0:NS, QT, :], stat[0:NS, 56 + QT:57 + QT], None, ALU.mult).then_inc(s("attn"), 1)
        att_out(QT)
        gated(4)
        ssum(4)
        dve.wait_ge(s("gluo"), NT)
        dve.wait_ge(s("ssrt"), 1)
        o(v.reciprocal(rssm[:, 0:NT], dstat[:, 24:24 + NT]))
        o(v.memset(lg[:, :, :], 0.0))

        dve.wait_ge(s("mod3"), 112)

        def join(p):
            j = ORDER3[p]
            w = TW[j]
            dve.wait_ge(s("woa"), p + 1)
            dve.wait_ge(s("woS"), p + 1)
            m3 = mod3P if j < QT else mod3S
            p1 = pt1[0:w, p % 2, :]
            a = p1.rearrange("p (a b) -> p a b", a=2)
            if j < QT:
                stt(out=a, in0=ps[:, 2:4, :], scalar=rssm[:, j:j + 1], in1=a, op0=ALU.mult, op1=ALU.add)\
                    .then_inc(s("wog"), 1)
                dve.wait_ge(s("wog"), p + 1)
            else:
                o(stt(out=spread[:, :], in0=ps[:, 2, 0:256], scalar=rssm[:, j:j + 1], in1=spread[:, :],
                      op0=ALU.mult, op1=ALU.add))
                for c in range(4):
                    ins = v.tensor_copy(p1[:, 256 * c:256 * (c + 1)], spread[32 * c:32 * c + 32, :])
                ins.then_inc(s("wog"), 1)
                dve.wait_ge(s("wog"), p + 1)
            o(tt_(p1, p1, m3[0:w, 0, :], ALU.mult))
            dve.wait_ge(s_x3[p % 2], 16 * (p // 2 + 1))
            tt_(x2[0:w, j, :], p1, xt3[0:w, p % 2, :], ALU.add).then_inc(s("x2"), 1)

        def h2T_half(p):
            j = ORDER3[p]
            dve.wait_ge(s("hTp"), 2 * (NT + p) + 2)
            v.tensor_copy(h2T[:, 4:8, tok(j)], ps[:, 7, 0:4 * TW[j]].rearrange("p (a b) -> p a b", a=4))\
                .then_inc(s("hTd"), 1)

        def keep_logits(p):
            j = ORDER3[p]
            dve.wait_ge(s("lg"), p + 1)
            o(v.tensor_copy(lg[0:TW[j], j, :], ps[0:TW[j], 4 + p % 2, 0:20]))

        for p, j in enumerate(ORDER3):
            w = TW[j]
            m3 = mod3P if j < QT else mod3S
            join(p)
            if p:
                h2T_half(p - 1)
            rstd(j, w, D, NT + 3 + p)
            stt(out=h2[0:w, p % 2, :], in0=x2[0:w, j, :], scalar=stat[0:w, 56 + j:57 + j], in1=m3[0:w, 2, :],
                op0=ALU.mult, op1=ALU.mult).then_inc(s("hA"), 1)
            dve.wait_ge(s("hA"), NT + p + 1)
            tt_(h2[0:w, p % 2, :], h2[0:w, p % 2, :], m3[0:w, 1, :], ALU.add).then_inc(s("h"), 1)
            if p >= 2:
                keep_logits(p - 2)
        keep_logits(NT - 2)
        h2T_half(NT - 1)
        keep_logits(NT - 1)

        G = lg[:, :, 0:4]
        Lv = lg[:, :, 4:20].rearrange("p j (g e) -> p j g e", g=NG)
        b4 = lambda a: a[:, :].unsqueeze(2).broadcast_to([P, NT, 4])
        first = cst("first").unsqueeze(1).broadcast_to([P, NT, 4])

        def first_max(hot, vals, top, t1):
            o(v.tensor_reduce(top[:, :], vals, AX.X, ALU.max))
            o(tt_(t1[:, :, :], vals, b4(top), ALU.is_equal))
            o(tt_(t1[:, :, :], t1[:, :, :], first, ALU.mult))
            o(v.tensor_reduce(gmax[:, :], t1[:, :, :], AX.X, ALU.max))
            o(tt_(hot[:, :, :], t1[:, :, :], b4(gmax), ALU.is_equal))

        first_max(ghot, G, gsum, g4c)
        tt_(g4a[:, :, :], G, b4(gsum), ALU.subtract).then_inc(s("gexpin"), 1)
        o(tt_(ghot[:, :, :], ghot[:, :, :], b4(cst("valid")), ALU.mult))
        e44 = lambda a: a[:, :, :].rearrange("p j (g e) -> p j g e", g=NG)
        gh4 = ghot[:, :, :].unsqueeze(3).broadcast_to([P, NT, NG, EPG])
        o(tt_(e44(e16), Lv, gh4, ALU.mult))
        o(v.tensor_reduce(esel[:, :, :], e16[:, :, :].rearrange("p j (g e) -> p j e g", g=NG), AX.X, ALU.add))
        first_max(o1, esel[:, :, :], v1, g4c)
        o(stt(out=esel[:, :, :], in0=o1[:, :, :], scalar=NEG, in1=esel[:, :, :], op0=ALU.mult, op1=ALU.add))
        first_max(o2, esel[:, :, :], v2, g4c)
        tt_(v2[:, :], v2[:, :], v1[:, :], ALU.subtract).then_inc(s("gexpin"), 1)
        for k, o_ in enumerate((o1, o2)):
            tt_(E12[:, k, :, :].rearrange("p j (g e) -> p j g e", g=NG), gh4,
                o_[:, :, :].unsqueeze(2).broadcast_to([P, NT, NG, EPG]), ALU.mult).then_inc(s("e12"), 1)
        dve.wait_ge(s("e12"), 2)
        tt_(M[:, :, :], E12[:, 0, :, :], E12[:, 1, :, :], ALU.add).then_inc(s("rM"), 1)
        dve.wait_ge(s("gexp"), 1)
        o(v.tensor_reduce(gsum[:, :], g4b[:, :, :], AX.X, ALU.add))
        dve.wait_ge(s("gexp"), 2)
        o(ts_(w1[:, :], w2[:, :], 1.0, None, ALU.add))
        o(tt_(w1[:, :], w1[:, :], gsum[:, :], ALU.mult))
        o(v.reciprocal(w1[:, :], w1[:, :]))
        o(tt_(w2[:, :], w2[:, :], w1[:, :], ALU.mult))
        dve.wait_ge(s("posp"), 1)
        v.tensor_copy(pos[:, :, :], ps[:, 0, 0:NT * NE].rearrange("p (j e) -> p j e", j=NT))
        o(v.tensor_copy(cnt[:, :], ps[:, 1, 0:NE]))
        o(ts_(nx[:, :], cnt[:, :], float(P), None, ALU.is_gt))
        for i in range(2, -(-NTOK // P)):
            o(stt(out=nx[:, :], in0=cnt[:, :], scalar=float(P * i), in1=nx[:, :], op0=ALU.is_gt, op1=ALU.add))
        o(v.tensor_tensor_scan(xb[:, :], cst("ones")[:, 0:NE], nx[:, :], 0.0, ALU.mult, ALU.add))
        o(tt_(xb[:, :], xb[:, :], nx[:, :], ALU.subtract))
        o(stt(out=nx2[:, :], in0=xb[:, :], scalar=float(P), in1=cst("exbase"), op0=ALU.mult, op1=ALU.add))
        bj = lambda a: a[:, :].unsqueeze(1).broadcast_to([P, NT, NE])
        o(stt(out=slot[:, :, :], in0=pos[:, :, :], scalar=float(P), in1=bj(nx2), op0=ALU.is_ge, op1=ALU.mult))
        o(tt_(slot[:, :, :], slot[:, :, :], pos[:, :, :], ALU.add))
        o(tt_(slot[:, :, :], slot[:, :, :], bj(cst("ebase")), ALU.add))
        tbb = cst("tbase").unsqueeze(1).broadcast_to([P, NT, NTILE])
        bt_ = lambda a: a[:, :].unsqueeze(2).broadcast_to([P, NT, NTILE])
        both = [P, 2, NT, NE]
        o(tt_(E12[:, :, :, :], E12[:, :, :, :], slot[:, :, :].unsqueeze(1).broadcast_to(both), ALU.mult))
        o(v.tensor_reduce(sl[:, :, :], E12[:, :, :, :], AX.X, ALU.add))
        kjt = [P, 2, NT, NTILE]
        per_tok = lambda a: a.unsqueeze(1).broadcast_to([P, 2, NT]).unsqueeze(3).broadcast_to(kjt)
        o(tt_(td[:, :, :, :], cst("tbase").unsqueeze(1).unsqueeze(1).broadcast_to(kjt),
              sl[:, :, :].unsqueeze(3).broadcast_to(kjt), ALU.subtract))
        o(ts_(tm[:, :, :, :], td[:, :, :, :], -float(P), None, ALU.is_gt))
        o(stt(out=tt[:, :, :, :], in0=td[:, :, :, :], scalar=0.0, in1=tm[:, :, :, :], op0=ALU.is_le, op1=ALU.mult))
        o(tt_(tm[:, :, :, :], tt[:, :, :, :], td[:, :, :, :], ALU.mult))
        tt_(tt[:, :, :, :], tt[:, :, :, :], per_tok(cst("tokv")), ALU.mult)
        o(v.tensor_reduce(ms[:, :, :], tm[:, :, :, :], AX.X, ALU.add))
        tt_(slot1h[:, :, :, :], cst("iotaneg").unsqueeze(1).unsqueeze(1).broadcast_to([P, 2, NT, P]),
            ms[:, :, :].unsqueeze(3).broadcast_to([P, 2, NT, P]), ALU.is_equal).then_inc(s("oneh"), 1)
        dve.wait_ge(s("idxp"), 1)
        v.tensor_copy(gidx[:, :], ps[:, 2, 0:NTILE]).then_inc(s("gidx"), 1)
        o(v.tensor_copy(sidx[:, :, :], sl[:, :, :]))
        be = lambda a: a[:, :].unsqueeze(1).broadcast_to([P, EXTRA, NE])
        jb = cst("jidx").unsqueeze(2).broadcast_to([P, EXTRA, NE])
        o(tt_(eid8[:, :, :], be(xb), jb, ALU.subtract))
        o(tt_(eid9[:, :, :], eid8[:, :, :], be(nx), ALU.add))
        o(ts_(eid9[:, :, :], eid9[:, :, :], 0.0, None, ALU.is_gt))
        o(stt(out=eid9[:, :, :], in0=eid8[:, :, :], scalar=0.0, in1=eid9[:, :, :], op0=ALU.is_le, op1=ALU.mult))
        o(tt_(eid9[:, :, :], eid9[:, :, :], be(cst("eidx")), ALU.mult))
        o(v.tensor_reduce(eid[:, :], eid9[:, :, :], AX.X, ALU.add))
        o(v.tensor_copy(eidi[:, :], eid[:, :]))
        o(v.tensor_reduce(xtot[:, :], nx[:, :], AX.X, ALU.add))
        o(ts_(eid[:, 0:EXTRA // 2], cst("jidx")[:, 0:EXTRA:2], xtot[:, 0:1], None, ALU.is_lt))
        o(v.tensor_reduce(xtot[:, :], eid[:, 0:EXTRA // 2], AX.X, ALU.add))
        v.tensor_copy(npair[:, :], xtot[:, :]).then_inc(s("eid"), 1)

        def rows(t, u):
            dve.wait_ge(s("xgp"), t + 1)
            v.tensor_copy(xgT[:, u, 4:8, :], ps[:, 5, :].rearrange("p (a b) -> p a b", a=4)).then_inc(s("xgd"), 1)

        def hidden(t, u):
            dve.wait_ge(s("eth"), t + 1)
            stt(out=a_s[:, u, :], in0=a_t[:, u, :], scalar=1.0, in1=ps[:, u, :], op0=ALU.add, op1=ALU.mult)\
                .then_inc(s("esilu"), 1)
            dve.wait_ge(s("esilu"), t + 1)
            dve.wait_ge(s("eup"), t + 1)
            stt(out=a_t[:, u, :], in0=a_s[:, u, :], scalar=0.5, in1=ps[:, 2 + u, :], op0=ALU.mult, op1=ALU.mult)\
                .then_inc(s("ahid"), 1)

        def finish(t, u, wait_store):
            dve.wait_ge(s("ey"), t + 1)
            if wait_store is not None:
                dve.wait_ge(s_yst[u], wait_store)
            v.tensor_copy(ysb[:, u, 512:1024], ps[:, 7, :]).then_inc(s("eyd"), 1)

        rows(0, 0)
        hidden(0, 0)
        rows(1, 1)
        for t in (1, 2):
            u = t % 2
            hidden(t, u)
            rows(t + 1, 1 - u)
            finish(t - 1, 1 - u, None)
        with dve.Fori(1, NE // 2 - 1) as i:
            for u in (1, 0):
                hidden(2 * i + (2 - u), u)
                rows(2 * i + (3 - u), 1 - u)
                finish(2 * i + (1 - u), 1 - u, 16 * i)
        hidden(NE - 1, 1)
        finish(NE - 2, 0, 16 * (NE // 2 - 1))
        finish(NE - 1, 1, 16 * (NE // 2 - 1))
        dve.wait_ge(s("eid"), 1)
        pairs = dve.value_load(npair[0:1, 0:1], min_val=0, max_val=EXTRA // 2)
        with dve.Fori(0, EXTRA // 2) as i:
            with dve.If(pairs > i):
                for u in range(2):
                    rows(2 * i + (NE + u), u)
                    if u:
                        hidden(2 * i + NE, 0)
                hidden(2 * i + (NE + 1), 1)
                for u in range(2):
                    finish(2 * i + (NE + u), u, 16 * i + 16 * (NE // 2))

        def weigh(j):
            w = TW[j]
            a, b = yg[0:w, j, 0, :], yg[0:w, j, 1, :]
            dve.wait_ge(s("yw"), j + 1)
            stt(out=a, in0=b, scalar=w2[0:w, j:j + 1], in1=a, op0=ALU.mult, op1=ALU.add).then_inc(s("ysum"), 1)

        def residual(j):
            w = TW[j]
            dve.wait_ge(s("ygate"), j + 1)
            tt_(x2[0:w, j, :], x2[0:w, j, :], yg[0:w, j, 0, :], ALU.add).then_inc(s("x3"), 1)

        def final_norm(j):
            w = TW[j]
            rstd(j, w, D, 2 * NT + 3 + j)
            stt(out=fo[0:w, j, :], in0=x2[0:w, j, :], scalar=stat[0:w, 56 + j:57 + j], in1=fgain[0:w, :],
                op0=ALU.mult, op1=ALU.mult).then_inc(s("fo"), 1)

        weigh(0)
        weigh(1)
        for j in range(NT):
            residual(j)
            if j + 2 < NT:
                weigh(j + 2)
            if j >= 1:
                final_norm(j - 1)
        final_norm(NT - 1)

    @block.tensor
    def _(pe):
        t_ = nc.tensor
        mm = t_.matmul
        ident = cst("ident")

        def tr(out, in_):
            n = in_.shape[0]
            return mm(out, lhsT=in_, rhs=ident[0:n, 0:n], start=True, stop=True, is_transpose=True)

        def ada(c):
            if c >= 2:
                pe.wait_ge(s("adae"), c - 1)
            wait_item(pe, IT_ADA + c)
            r = ring[(IT_ADA + c) % R1]
            for k in range(KD):
                for j in range(4):
                    ins = mm(ps[32 * j:32 * j + 32, c % 2, 0:P], cS[:, k, :],
                             r[:, 512 * k + P * j:512 * k + P * (j + 1)], start=k == 0, stop=k == KD - 1,
                             tile_position=(0, 32 * j))
            ins.then_inc(s("ada"), 1)

        def h_t(j):
            w = TW[j]
            pe.wait_ge(s("h"), j + 1)
            if j >= 2:
                pe.wait_ge(s("hTa"), j - 1)
                pe.wait_ge(s("hTd"), j - 1)
            for half in range(2):
                for c in range(4):
                    k = 4 * half + c
                    ins = tr(ps[:, 2 + 2 * (j % 2) + half, w * c:w * (c + 1)], hb[0:w, j % 2, P * k:P * (k + 1)])
                ins.then_inc(s("hTp"), 1)

        pe.wait_ge(s("cs"), 1)
        ada(0)
        ada(1)
        pe.wait_ge(s("init"), 160)
        mm(ps[0:HEADS, 6, :], ctab33[:, :], ohp[:, 0:512], start=True, stop=True)
        mm(ps[0:HEADS, 7, 0:128], ctab33[:, :], ohp[:, 512:640], start=True, stop=True).then_inc(s("gp"), 1)
        ada(2)
        ada(3)
        ada(4)
        pe.wait_ge(s("bpad"), 1)
        for n in range(8):
            b, q = n // 4, n % 4
            if n >= 2:
                pe.wait_ge(s("btTe"), n - 1)
            for r_ in range(4):
                ins = tr(ps[:, 2 + n % 2, P * r_:P * (r_ + 1)], bpad[b][:, 4 * q + r_, :])
            ins.then_inc(s("btT"), 1)
        pe.wait_ge(s("btTe"), 8)
        ada(5)
        for j in range(NT):
            ada(6 + j)
            h_t(j)
        for c in range(6 + NT, N_ADA):
            ada(c)

        pe.wait_ge(s("hTa"), NT)
        pe.wait_ge(s("hTd"), NT)
        pe.wait_ge(s("adae"), N_ADA)
        pe.wait_ge(s("gsb"), 1)
        pe.wait_ge(s("sq"), NT)
        zi = 0
        for it in range(N_WIN):
            i = IT_WIN + it
            wait_item(pe, i)
            r = ring[i % R1]
            if it == 2:
                for j in range(NT):
                    w = TW[j]
                    if j >= 2:
                        pe.wait_ge(s("ve"), j - 1)
                    for k in range(KD):
                        if j < QT:
                            ins = mm(ps[:, 2 + j % 2, :], hT[:, k, tok(j)], r[:, 512 * k:512 * (k + 1)],
                                     start=k == 0, stop=k == KD - 1)
                            continue
                        for c in range(4):
                            ins = mm(ps[32 * c:32 * c + 32, 2, 0:P], hT[:, k, tok(j)],
                                     r[:, 512 * k + P * c:512 * k + P * (c + 1)], start=k == 0, stop=k == KD - 1,
                                     tile_position=(0, 32 * c))
                    ins.then_inc(s("v"), 1)
                continue
            for c in range(4):
                if zi >= 2:
                    pe.wait_ge(s("za"), zi - 1)
                    pe.wait_ge(s("zd"), zi - 1)
                for n, out in enumerate((ps[:, zi % 2, 0:HALF], ps[:, 6 + zi % 2, 0:HALF])):
                    cols = slice(HALF * n, HALF * (n + 1))
                    for k in range(KD):
                        ins = mm(out, r[:, 512 * k + P * c:512 * k + P * (c + 1)], hT[:, k, cols],
                                 start=k == 0, stop=k == KD - 1)
                    ins.then_inc(s("z"), 1)
                zi += 1

        wait_item(pe, IT_OH)
        pe.wait_ge(s("padt"), 1)
        pe.wait_ge(s("ve"), NT)
        r = ring[IT_OH % R1]
        for b, (c0, c1) in enumerate(((0, 512), (512, DK))):
            for t in range(TDEC):
                ins = mm(ps[:, 2 + b, 0:c1 - c0], padT[:, t, :], r[0:BUCKETS + 1, DK * t + c0:DK * t + c1],
                         start=t == 0, stop=t == TDEC - 1)
        ins.then_inc(s("dbp"), 1)
        pe.wait_ge(s("za"), 12)
        pe.wait_ge(s("zd"), 12)
        for n in range(2):
            for t in range(STT):
                ins = mm(ps[:, 5 + n, NS * t:NS * (t + 1)], bt[n][:, t, :], uT[:, t // 4, SEQ:NTOK],
                         start=True, stop=True)
        ins.then_inc(s("buSp"), 1)

        NST = HEADS * QT
        pe.wait_ge(s("dbias"), 1)

        def scores(st):
            h, qt = divmod(st, QT)
            rows = slice(64 * (h % 2), 64 * (h % 2) + 64)
            if st >= 2:
                pe.wait_ge(s("P"), st - 1)
            m = P * (qt + 1)
            mm(ps[:, st % 2, 0:m], qkT[rows, h // 2, P * qt:m], qkT[rows, 4 + h // 2, 0:m], start=True, stop=False)
            pe.wait_ge(s_toep[h % 2], 16 * (h // 2 + 1))
            mm(ps[:, st % 2, 0:m], cst("flip"), toep[:, h % 2, SEQ - m:SEQ], start=False, stop=True)\
                .then_inc(s("S"), 1)

        def probs_t(st):
            qt = st % QT
            pe.wait_ge(s("P"), st + 1)
            if st >= 2:
                pe.wait_ge(s("ptr"), st - 1)
            for kt in range(qt + 1):
                ins = tr(ps[:, 2 + st % 2, P * kt:P * (kt + 1)], Sb[:, st % 2, P * kt:P * (kt + 1)])
            ins.then_inc(s("pt"), 1)

        def pv(st):
            h, qt = divmod(st, QT)
            pe.wait_ge(s("ptr"), st + 1)
            for kt in range(qt + 1):
                ins = mm(ps[:, 4 + qt, DH * h:DH * (h + 1)], PTs[:, st % 2, P * kt:P * (kt + 1)],
                         vrow[:, kt, DH * h:DH * (h + 1)], start=kt == 0, stop=kt == qt)
            ins.then_inc(s("pv"), 1)

        for st in range(NST + 2):
            if st < NST:
                scores(st)
            if 1 <= st <= NST:
                probs_t(st - 1)
            if st == 2:
                pe.wait_ge(s("buS"), 1)
            if st >= 2:
                pv(st - 2)

        def att_t(j):
            w = TW[j]
            pe.wait_ge(s("attn"), j + 1)
            if j >= 2:
                pe.wait_ge(s("attTe"), j - 1)
            bank = 2 + j % 2 if j < QT else 5
            for c in range(4):
                ins = tr(ps[:, bank, w * c:w * (c + 1)], att[0:w, j, P * c:P * (c + 1)])
            ins.then_inc(s("attT"), 1)

        pe.wait_ge(s("qbd"), 1)
        pe.wait_ge(s("att"), NST)

        def dec_keys(g, part):
            if part == 0 and g:
                pe.wait_ge(s("dSm"), g)
            for q in range(4):
                for n4 in range(4):
                    if part == 0 and q == 0:
                        wait_item(pe, IT_KV + 8 * g + n4)
                    rows = slice(32 * n4, 32 * n4 + 32)
                    r = ring[(IT_KV + n4) % R1]
                    c0, c1 = ((0, 512), (512, CK))[part]
                    mm(ps[rows, part, 0:c1 - c0], qbd[:, 4 * g + n4, q, :], r[:, CK * q + c0:CK * q + c1],
                       start=q == 0, stop=q == 3, tile_position=(0, 32 * n4))
            if part == 0:
                return
            for q in range(4):
                for n4 in range(4):
                    rows = slice(32 * n4, 32 * n4 + 32)
                    ins = mm(ps[rows, 1, CK - 512:DK - 512], qbd[:, 4 * g + n4, q, :], qkT[:, 4 + q, SEQ:NTOK],
                             start=q == 0, stop=q == 3, tile_position=(0, 32 * n4))
                    if q == 3:
                        ins.then_inc(s("dS"), 1)

        def dec_values(g, part):
            if part == 0:
                pe.wait_ge(s("dPtd"), g + 1)
                pe.wait_ge(s("dPta"), g + 1)
                if g:
                    pe.wait_ge(s("dOe"), g)
            for b in range(4) if part == 0 else range(4, CB):
                for n4 in range(4):
                    if b == 0:
                        wait_item(pe, IT_KV + 8 * g + 4 + n4)
                    rows = slice(32 * n4, 32 * n4 + 32)
                    mm(ps[rows, 4, :], dPT[:, b, rows], ring[(IT_KV + n4) % R1][:, AW * b:AW * (b + 1)],
                       start=b == 0, stop=False, tile_position=(0, 32 * n4))
            if part == 1:
                for n4 in range(4):
                    rows = slice(32 * n4, 32 * n4 + 32)
                    mm(ps[rows, 4, :], dPT[0:NS, CB, rows], vrow[0:NS, QT, :], start=False, stop=True,
                       tile_position=(0, 32 * n4)).then_inc(s("dOp"), 1)

        def dec_probs_t(g):
            pe.wait_ge(s("dP"), g + 1)
            for b in range(CB):
                tr(ps[:, b // 4, P * (b % 4):P * (b % 4 + 1)], dP[:, P * b:P * (b + 1)])
            tr(ps[0:NS, 1, 3 * P:4 * P], dP[:, CK:DK]).then_inc(s("dPt"), 1)

        def s5_in(i):
            k, q = divmod(i, 4)
            if i >= 1:
                pe.wait_ge(s("buread"), i)
            for n in range(2):
                for r_ in range(4):
                    ins = mm(ps[:, 5 + n, CH * r_:CH * (r_ + 1)], bt[n][:, 4 * q + r_, :],
                             uT[:, q, CH * k:CH * (k + 1)], start=True, stop=True)
            ins.then_inc(s("bu"), 1)

        def s5_out(i):
            k, q = divmod(i, 4)
            pe.wait_ge(s("hout"), i + 2)
            if q == 0:
                pe.wait_ge(s("yread"), k + 1)
            for n, (c, a) in enumerate(((ct[0], hr), (ctn, hi), (ct[1], gr), (ct[1], gi))):
                for r_ in range(4):
                    ins = mm(ps[32 * r_:32 * r_ + 32, 7, CH * q:CH * (q + 1)], c[:, 4 * q + r_, :],
                             a[i % 2][:, r_, :], start=n == 0, stop=n == 3, tile_position=(0, 32 * r_))
            ins.then_inc(s("yp"), 1)

        def s5_glu(n):
            w = CH if n else NS
            pe.wait_ge(s("gel"), n + 1)
            for a in range(2):
                for q in range(4):
                    ins = mm(ps[:, 2 + a, w * q:w * (q + 1)], glu[:, a, q, :], y2[:, q, 0:w], start=True, stop=True)
            ins.then_inc(s("glut"), 1)

        def s5_sum(n):
            w = CH if n else NS
            pe.wait_ge(s("gsq"), n + 1)
            for q in range(4):
                for c in range(1 if n else 4):
                    ins = mm(ps[32 * c:32 * c + w, 2, 0:1], yd[:, q, 0:w], cst("ones")[:, 0:1], start=q == 0,
                             stop=q == 3, **({} if n else {"tile_position": (0, 32 * c)}))
            ins.then_inc(s("ssp"), 1)

        pe.wait_ge(s("hout"), 1)
        hs = [a[0][:, :, :].rearrange("p a b -> p (a b)") for a in (hr, hi)]
        for q in range(4):
            for n, r_ in ((n, r_) for n in range(2) for r_ in range(4)):
                t = 4 * q + r_
                ins = mm(ps[32 * r_:32 * r_ + 32, 7, NS * q:NS * (q + 1)], ct[n][:, t, :], hs[n][:, NS * t:NS * (t + 1)],
                         start=n == 0, stop=n == 1, tile_position=(0, 32 * r_))
        ins.then_inc(s("yp"), 1)
        KEY_STEPS = {0: (0, 0), 1: (0, 1), 10: (1, 0), 11: (1, 1)}
        VALUE_STEPS = {5: (0, 0), 6: (0, 1), 14: (1, 0), 15: (1, 1)}
        for i in range(16):
            s5_in(i)
            if i == 2:
                pe.wait_ge(s("ctn"), 1)
            if i >= 2:
                s5_out(i - 2)
            if i == 3:
                pe.wait_ge(s("attTe"), QT)
                pe.wait_ge(s("glul"), 32)
            if i % 4 == 3:
                s5_glu(i // 4)
            if i in (3, 14):
                dec_probs_t(i // 8)
            if i in KEY_STEPS:
                dec_keys(*KEY_STEPS[i])
            if i in VALUE_STEPS:
                dec_values(*VALUE_STEPS[i])
            if i == 0:
                for j in range(QT):
                    att_t(j)
            elif i % 4 == 0:
                s5_sum(i // 4 - 1)

        def wo(p, half):
            j = ORDER3[p]
            if j == QT:
                pe.wait_ge(s("attTe"), NT)
            if p:
                pe.wait_ge((s("woa"), s("wog"))[half], p)
            if j == QT:
                for k in range(4 * half, 4 * half + 4):
                    for c in range(4):
                        r = ring[(IT_WO + c // 2) % R1]
                        c0 = 512 * k + 256 * (c % 2)
                        ins = mm(ps[32 * c:32 * c + 32, 2 * half, 0:256], mixT[:, k, tok(j)], r[:, c0:c0 + 256],
                                 start=k % 4 == 0, stop=k % 4 == 3, tile_position=(0, 32 * c))
                ins.then_inc((s("woA"), s("woS"))[half], 1)
                return
            for n in range(2):
                wait_item(pe, IT_WO + n)
                r = ring[(IT_WO + n) % R1]
                for k in range(4 * half, 4 * half + 4):
                    ins = mm(ps[:, 2 * half + n, :], mixT[:, k, tok(j)], r[:, 512 * k:512 * (k + 1)],
                             start=k % 4 == 0, stop=k % 4 == 3)
            ins.then_inc((s("woA"), s("woS"))[half], 1)

        pe.wait_ge(s("dSm"), 2)
        s5_out(14)
        s5_sum(3)
        s5_out(15)
        pe.wait_ge(s("dOe"), 2)
        for g in range(2):
            ins = mm(ps[0:NS, 4, :], cst("toksel")[:, NS * g:NS * (g + 1)], dO[:, g, :], start=g == 0, stop=g == 1)
        ins.then_inc(s("attSp"), 1)
        wo(0, 0)
        att_t(QT)
        s5_glu(4)
        s5_sum(4)

        pe.wait_ge(s("gluo"), NT)

        def h2_t(p):
            w = TW[ORDER3[p]]
            pe.wait_ge(s("h"), NT + p + 1)
            if p:
                pe.wait_ge(s("hTa"), NT + p)
                pe.wait_ge(s("hTd"), NT + p)
            for half in range(2):
                for c in range(4):
                    k = 4 * half + c
                    ins = tr(ps[:, 6 + half, w * c:w * (c + 1)], h2[0:w, p % 2, P * k:P * (k + 1)])
                ins.then_inc(s("hTp"), 1)

        def logits(p):
            j = ORDER3[p]
            w = TW[j]
            pe.wait_ge(s("hTa"), NT + p + 1)
            pe.wait_ge(s("hTd"), NT + p + 1)
            if p == 0:
                pe.wait_ge(s("mod3"), 112)
            out = ps[0:w, 4 + p % 2, 0:20]
            mm(out, cst("ones", 1)[:, 0:w], rb[:, :], start=True, stop=False)
            for k in range(KD):
                ins = mm(out, h2T[:, k, tok(j)], rw[:, k, :], start=False, stop=k == KD - 1)
            ins.then_inc(s("lg"), 1)

        for p in range(NT):
            for half in range(2):
                if p or half:
                    wo(p, half)
            if p:
                h2_t(p - 1)
            if p >= 2:
                logits(p - 2)
        logits(NT - 2)
        h2_t(NT - 1)
        logits(NT - 1)

        pe.wait_ge(s("rM"), 1)
        Mf = M[:, :, :].rearrange("p j e -> p (j e)")
        mm(ps[:, 0, 0:NT * NE], cst("tri"), Mf, start=True, stop=False)
        for d in range(1, NT):
            mm(ps[:, 0, NE * d:NT * NE], cst("ones"), Mf[:, 0:NE * (NT - d)], start=False, stop=d == NT - 1)
        for j in range(NT):
            ins = mm(ps[:, 1, 0:NE], cst("ones"), M[:, j, :], start=j == 0, stop=j == NT - 1)
        ins.then_inc(s("posp"), 1)
        pe.wait_ge(s("oneh"), 1)
        for k in range(2):
            for j in range(NT):
                ins = mm(ps[:, 2, 0:NTILE], slot1h[:, k, j, :], tt[:, k, j, :], start=k + j == 0,
                         stop=(k, j) == (1, NT - 1))
        ins.then_inc(s("idxp"), 1)

        def rows_t(t, u, wait_gather):
            pe.wait_ge(s_xg[u], wait_gather)
            for c in range(KD):
                ins = tr(ps[:, 4 + c // 4, P * (c % 4):P * (c % 4 + 1)], xg[:, u, P * c:P * (c + 1)])
            ins.then_inc(s("xgp"), 1)

        def weights(w, u, turn):
            pe.wait_ge(efull[3 * u + w], 16 * turn)
            return ering[3 * u + w]

        def half_in(t, u, w, turn, old=True):
            if w == 0:
                pe.wait_ge(s("xga"), t + 1)
                pe.wait_ge(s("xgd"), t + 1)
                if old:
                    pe.wait_ge(s("aTe"), t - 1)
            r = weights(w, u, turn)
            for k in range(KD):
                ins = mm(ps[:, 2 * w + u, :], xgT[:, u, k, :], r[:, 512 * k:512 * (k + 1)],
                         start=k == 0, stop=k == KD - 1)
            ins.then_inc(s("egate") if w == 0 else s("eup"), 1)

        def hidden_t(t, u):
            pe.wait_ge(s("ahid"), t + 1)
            for c in range(4):
                ins = tr(ps[:, u, P * c:P * (c + 1)], a_t[:, u, P * c:P * (c + 1)])
            ins.then_inc(s("aTp"), 1)

        def down(t, u, turn, old=True):
            pe.wait_ge(s("aTe"), t + 1)
            if old:
                pe.wait_ge(s("eya"), t)
                pe.wait_ge(s("eyd"), t)
            r = weights(2, u, turn)
            for n in range(2):
                for c in range(4):
                    ins = mm(ps[:, 6 + n, :], aT[:, u, c, :], r[:, D * c + 512 * n:D * c + 512 * (n + 1)],
                             start=c == 0, stop=c == 3)
            ins.then_inc(s("ey"), 1)

        pe.wait_ge(s("gidx"), 1)
        rows_t(0, 0, 16)
        half_in(0, 0, 0, 1, old=False)
        half_in(0, 0, 1, 1)
        rows_t(1, 1, 16)
        for t in (1, 2):
            u = t % 2
            half_in(t, u, 0, 1 + t // 2, old=t >= 2)
            hidden_t(t - 1, 1 - u)
            half_in(t, u, 1, 1 + t // 2)
            rows_t(t + 1, 1 - u, 32)
            down(t - 1, 1 - u, 1, old=t >= 2)
        with pe.Fori(1, NE // 2 - 1) as i:
            for u in (1, 0):
                t = 2 * i + (2 - u)
                half_in(t, u, 0, i + (2 - u))
                hidden_t(2 * i + (1 - u), 1 - u)
                half_in(t, u, 1, i + (2 - u))
                rows_t(2 * i + (3 - u), 1 - u, 16 * i + 32)
                down(2 * i + (1 - u), 1 - u, i + 1)
        half_in(NE - 1, 1, 0, NE // 2)
        hidden_t(NE - 2, 0)
        half_in(NE - 1, 1, 1, NE // 2)
        down(NE - 2, 0, NE // 2)
        hidden_t(NE - 1, 1)
        down(NE - 1, 1, NE // 2)
        pe.wait_ge(s("eid"), 1)
        pairs = pe.value_load(npair[0:1, 0:1], min_val=0, max_val=EXTRA // 2)
        with pe.Fori(0, EXTRA // 2) as i:
            with pe.If(pairs > i):
                t, turn = 2 * i + NE, i + (NE // 2 + 1)
                rows_t(t, 0, 16 * i + 16 * (NE // 2 + 1))
                half_in(t, 0, 0, turn)
                half_in(t, 0, 1, turn)
                rows_t(t + 1, 1, 16 * i + 16 * (NE // 2 + 1))
                half_in(t + 1, 1, 0, turn)
                hidden_t(t, 0)
                half_in(t + 1, 1, 1, turn)
                down(t, 0, turn)
                hidden_t(t + 1, 1)
                down(t + 1, 1, turn)


def kernel(**inputs):
    import concourse.bacc as bacc
    from concourse.bass_utils import run_bass_kernel_spmd

    x = {k: np.asarray(v) for k, v in inputs.items()}
    nc = bacc.Bacc("TRN2", target_bir_lowering=False, num_devices=1)

    def state(a):
        return np.ascontiguousarray(a.reshape((STT, P) + a.shape[2:]).swapaxes(0, 1))

    def channel(a):
        return np.ascontiguousarray(a.reshape(4, P).T)

    def blocks(a, n):
        g, r, c = a.shape
        out = np.zeros((g // n, n, r, n, c), a.dtype)
        for i in range(n):
            out[:, i, :, i, :] = a.reshape(g // n, n, r, c)[:, i]
        return out.reshape(g // n, n * r, n * c)

    c_all = np.concatenate([x["c_prompt"], x["c_sample"]])
    par = [state(x["ssm_a_re"][0]), state(x["ssm_a_im"][0]),
           state(np.broadcast_to(x["ssm_log_dt"][0][:, None], (GRP, ST))),
           channel(x["ssm_d"][0].reshape(-1)), channel(x["attn_out_g"][0]), channel(x["ssm_out_g"][0]),
           state(x["ssm_b_re"][0]).reshape(P, -1), state(x["ssm_b_im"][0]).reshape(P, -1)]
    ck = x["cache_k"][0][:, CROWS]
    cv = x["cache_v"][0][:, CROWS]
    A = {
        "zero": np.zeros(D, np.float32),
        "const": CONST,
        "par": np.concatenate(par, axis=1),
        "cT": c_all.reshape(NC, KD, P).transpose(2, 1, 0),
        "tab33": np.concatenate([x["rel_bias"], np.ones((1, HEADS), np.float32)]),
        "oh_prompt": OH_PROMPT, "oh_decode": OH_DECODE,
        "ct_re": blocks(x["ssm_c_re"][0].transpose(0, 2, 1), 2).transpose(1, 0, 2),
        "ct_im": blocks(x["ssm_c_im"][0].transpose(0, 2, 1), 2).transpose(1, 0, 2),
        "glu_a": blocks(x["glu_a"][0], 8).transpose(1, 0, 2),
        "glu_b": blocks(x["glu_b"][0], 8).transpose(1, 0, 2),
        "ada_w": x["ada_w"][0],
        "modrow": np.concatenate([x[n][0].reshape(-1, 4, P) for n in ("ada_b", "norm1_g", "norm2_g")])
        .transpose(1, 0, 2).reshape(4, -1), "final_g": x["final_norm_g"],
        "w_in": x["w_in"][0], "w_out": x["w_out"][0],
        "x": np.concatenate([x["x_prompt"][0], x["x_sample"].reshape(NS, D)]),
        "cache_k": ck.reshape(NSEQ, CK, 4, P).transpose(0, 3, 2, 1).reshape(NSEQ, P, 4 * CK),
        "cache_v": cv.reshape(NSEQ, CB, P, AW).transpose(0, 2, 1, 3).reshape(NSEQ, P, CB * AW),
        "h0_re": state(x["state_ssm_re"][0].transpose(1, 2, 0)), "h0_im": state(x["state_ssm_im"][0].transpose(1, 2, 0)),
        "router_w": np.concatenate([x["router_g_w"][0], x["router_e_w"][0].transpose(1, 0, 2).reshape(D, NE)], axis=1)
        .reshape(KD, P, NG + NE).transpose(1, 0, 2),
        "router_b": np.concatenate([x["router_g_b"][0], x["router_e_b"][0].reshape(-1)])[None, :],
        "w_gate": x["w_gate"][0].reshape(NE, D, FE), "w_up": x["w_up"][0].reshape(NE, D, FE),
        "w_down": x["w_down"][0].reshape(NE, FE, D),
    }
    A = {k: np.ascontiguousarray(a) for k, a in A.items()}
    I = {k: nc.dram_tensor("in_" + k, a.shape, mybir.dt.from_np(a.dtype), kind="ExternalInput").ap()
         for k, a in A.items()}
    shapes = {"y": (NTOK, D), "kT": (AW, NTOK), "v": (NTOK, AW), "ssm_p": (P, 2, STT), "ssm_s": (P, 2 * STT * NSEQ)}
    O = {k: nc.dram_tensor("out_" + k, shp, F32, kind="ExternalOutput").ap() for k, shp in shapes.items()}
    build(nc, I, O)
    r = run_bass_kernel_spmd(nc, [{"in_" + k: a for k, a in A.items()}], core_ids=[0]).results[0]
    y, kT, v, sp, ss = (np.asarray(r["out_" + k]) for k in ("y", "kT", "v", "ssm_p", "ssm_s"))
    k = kT.T
    heads = lambda a, lead: np.ascontiguousarray(a.reshape(lead + (HEADS, DH)))
    sp = sp.transpose(1, 2, 0).reshape(2, 1, 1, GRP, ST)
    ss = ss.reshape(P, 2, STT, NSEQ).transpose(1, 3, 2, 0).reshape(2, 1, NSEQ, GRP, ST)
    c = np.ascontiguousarray
    return (c(y[:SEQ].reshape(1, SEQ, D)), c(y[SEQ:].reshape(NSEQ, TDEC, D)),
            heads(k[:SEQ], (1, 1, SEQ)), heads(v[:SEQ], (1, 1, SEQ)),
            heads(k[SEQ:], (1, NSEQ, TDEC)), heads(v[SEQ:], (1, NSEQ, TDEC)),
            c(sp[0]), c(sp[1]), c(ss[0]), c(ss[1]))
```
